# Optimizing a Trainium2 kernel written in Bass

```python
import math
import jax, jax.numpy as jnp
from jax import lax
import numpy as np

D_MODEL = 1024
BATCH = 1
SEQ = 512
DEPTH = 2

N_EVEN = (DEPTH + 1) // 2
N_ODD = DEPTH // 2

GDN_HEAD_DIM = 128
GDN_WIDTH = D_MODEL // 2
GDN_HEADS = GDN_WIDTH // GDN_HEAD_DIM
CONV_K = 4
CHUNK = 64

S5_WIDTH = D_MODEL - GDN_WIDTH
S5_GROUP = 16
S5_GROUPS = S5_WIDTH // S5_GROUP
S5_STATE = 64

SB_HEAD_DIM = 128
SB_HEADS = D_MODEL // SB_HEAD_DIM
QBLOCK = 128

FFN_HIDDEN = -(-8 * D_MODEL // (3 * 256)) * 256

EVEN_IN = 4 * GDN_WIDTH + 2 * GDN_HEADS + S5_WIDTH
NORM_EPS = 1e-6

kernel_name = "hybrid_gdn_s5_stickbreak_adaln"

def rms_norm(x, w):
    xf = x.astype(jnp.float32)
    y = xf * lax.rsqrt(jnp.mean(xf * xf, axis=-1, keepdims=True) + NORM_EPS)
    return y.astype(x.dtype) * w

def l2_normalize(x):
    return x * lax.rsqrt(jnp.sum(x * x, axis=-1, keepdims=True) + NORM_EPS)

def causal_depthwise_conv(x, w):
    k_len, ch = w.shape
    return lax.conv_general_dilated(x, w[:, None, :].astype(x.dtype), window_strides=(1,),
                                    padding=[(k_len - 1, 0)],
                                    dimension_numbers=('NWC', 'WIO', 'NWC'),
                                    feature_group_count=ch)

def gated_delta_rule_chunked(q, k, v, g, beta):
    bsz, seq, nh, dk = q.shape
    dv = v.shape[-1]
    n = seq // CHUNK

    def to_chunks(t):
        return t.reshape(bsz, n, CHUNK, nh, -1).transpose(0, 3, 1, 2, 4)

    q, k, v = to_chunks(q), to_chunks(k), to_chunks(v)
    g = to_chunks(g[..., None])[..., 0]
    beta = to_chunks(beta[..., None])[..., 0]
    gc = jnp.cumsum(g, axis=-1)
    idx = jnp.arange(CHUNK)
    incl = idx[:, None] >= idx[None, :]
    strict = idx[:, None] > idx[None, :]
    decay = jnp.exp(jnp.where(incl, gc[..., :, None] - gc[..., None, :], -jnp.inf))

    k_beta = k * beta[..., None]
    lower = jnp.where(strict, jnp.einsum('bhnid,bhnjd->bhnij', k_beta, k) * decay, 0.0)
    lhs = lower + jnp.eye(CHUNK, dtype=lower.dtype)
    rhs = jnp.concatenate([v * beta[..., None], k_beta * jnp.exp(gc)[..., None]], axis=-1)
    sol = lax.linalg.triangular_solve(lhs, rhs, left_side=True, lower=True, unit_diagonal=True)
    u, w = sol[..., :dv], sol[..., dv:]

    attn = jnp.einsum('bhnid,bhnjd->bhnij', q, k) * decay
    q_dec = q * jnp.exp(gc)[..., None]
    g_last = gc[..., -1:]
    k_dec = k * jnp.exp(g_last - gc)[..., None]
    state_decay = jnp.exp(g_last[..., 0])

    xs = tuple(jnp.moveaxis(t, 2, 0) for t in (q_dec, k_dec, u, w, attn, state_decay))

    def step(state, inp):
        qd, kd, ui, wi, ai, sd = inp
        v_new = ui - jnp.einsum('bhck,bhkv->bhcv', wi, state)
        o = jnp.einsum('bhck,bhkv->bhcv', qd, state) + jnp.einsum('bhcs,bhsv->bhcv', ai, v_new)
        state = state * sd[..., None, None] + jnp.einsum('bhck,bhcv->bhkv', kd, v_new)
        return state, o

    s0 = jnp.zeros((bsz, nh, dk, dv), jnp.float32)
    _, o = lax.scan(step, s0, xs)
    return o.transpose(1, 0, 3, 2, 4).reshape(bsz, seq, nh, dv)

def s5_layer(u, lam_re, lam_im, log_dt, b_re, b_im, c_re, c_im, d_skip, glu_w, glu_b):
    f32 = jnp.float32
    bsz, seq, _ = u.shape
    uf = u.astype(f32).reshape(bsz, seq, S5_GROUPS, S5_GROUP)
    lr, li = lam_re.astype(f32), lam_im.astype(f32)
    dt = jnp.exp(log_dt.astype(f32))[:, None]
    mag = jnp.exp(lr * dt)
    lb_re, lb_im = mag * jnp.cos(li * dt), mag * jnp.sin(li * dt)
    den = lr * lr + li * li
    num_re, num_im = lb_re - 1.0, lb_im
    f_re = (num_re * lr + num_im * li) / den
    f_im = (num_im * lr - num_re * li) / den
    br, bi = b_re.astype(f32), b_im.astype(f32)
    bb_re = f_re[..., None] * br - f_im[..., None] * bi
    bb_im = f_re[..., None] * bi + f_im[..., None] * br
    bu_re = jnp.einsum('blgh,gph->lbgp', uf, bb_re)
    bu_im = jnp.einsum('blgh,gph->lbgp', uf, bb_im)
    a_re = jnp.broadcast_to(lb_re, (seq, 1, S5_GROUPS, S5_STATE))
    a_im = jnp.broadcast_to(lb_im, (seq, 1, S5_GROUPS, S5_STATE))

    def combine(e1, e2):
        a1r, a1i, b1r, b1i = e1
        a2r, a2i, b2r, b2i = e2
        return (a1r * a2r - a1i * a2i, a1r * a2i + a1i * a2r,
                a2r * b1r - a2i * b1i + b2r, a2r * b1i + a2i * b1r + b2i)

    _, _, xr, xi = lax.associative_scan(combine, (a_re, a_im, bu_re, bu_im), axis=0)
    y = (jnp.einsum('lbgp,ghp->blgh', xr, c_re.astype(f32))
         - jnp.einsum('lbgp,ghp->blgh', xi, c_im.astype(f32))
         + d_skip.astype(f32).reshape(S5_GROUPS, S5_GROUP) * uf)
    y = jax.nn.gelu(y.reshape(bsz, seq, S5_WIDTH))
    y = y * jax.nn.sigmoid(y @ glu_w.astype(f32) + glu_b.astype(f32))
    return y.astype(u.dtype)

def even_mixer(h, w_in, conv_w, a_log, dt_bias, head_norm_w, lam_re, lam_im, log_dt,
               b_re, b_im, c_re, c_im, d_skip, glu_w, glu_b, w_out):
    bsz, seq, _ = h.shape
    W, H = GDN_WIDTH, GDN_HEADS
    proj = h @ w_in
    qkv = jax.nn.silu(causal_depthwise_conv(proj[..., :3 * W], conv_w))
    z = proj[..., 3 * W:4 * W]
    b_lin = proj[..., 4 * W:4 * W + H]
    a_lin = proj[..., 4 * W + H:4 * W + 2 * H]
    u = proj[..., 4 * W + 2 * H:]

    f32 = jnp.float32
    q, k, v = (t.astype(f32).reshape(bsz, seq, H, GDN_HEAD_DIM) for t in jnp.split(qkv, 3, axis=-1))
    q = l2_normalize(q) * (GDN_HEAD_DIM ** -0.5)
    k = l2_normalize(k)
    beta = jax.nn.sigmoid(b_lin.astype(f32))
    g = -jnp.exp(a_log.astype(f32)) * jax.nn.softplus(a_lin.astype(f32) + dt_bias.astype(f32))
    o = gated_delta_rule_chunked(q, k, v, g, beta)
    o = rms_norm(o, head_norm_w.astype(f32)) * jax.nn.silu(z.astype(f32).reshape(bsz, seq, H, GDN_HEAD_DIM))
    o = o.reshape(bsz, seq, W).astype(h.dtype)

    y_s5 = s5_layer(u, lam_re, lam_im, log_dt, b_re, b_im, c_re, c_im, d_skip, glu_w, glu_b)
    return jnp.concatenate([o, y_s5], axis=-1) @ w_out

def stick_breaking_attention(q, k, v):
    bsz, seq, nh, d = q.shape
    nb = seq // QBLOCK
    f32 = jnp.float32
    scale = d ** -0.5
    qb = q.astype(f32).reshape(bsz, nb, QBLOCK, nh, d).transpose(1, 0, 3, 2, 4)
    kh = k.astype(f32).transpose(0, 2, 1, 3)
    vh = v.astype(f32).transpose(0, 2, 1, 3)
    key_pos = jnp.arange(seq)

    def block(args):
        qi, bi = args
        q_pos = bi * QBLOCK + jnp.arange(QBLOCK)
        z = jnp.einsum('bhqd,bhkd->bhqk', qi, kh) * scale
        valid = key_pos[None, :] < q_pos[:, None]
        log_1m = jnp.where(valid, jax.nn.log_sigmoid(-z), 0.0)
        between = lax.cumsum(log_1m, axis=3, reverse=True) - log_1m
        wts = jnp.where(valid, jnp.exp(jax.nn.log_sigmoid(z) + between), 0.0)
        return jnp.einsum('bhqk,bhkd->bhqd', wts, vh)

    o = lax.map(block, (qb, jnp.arange(nb)))
    return o.transpose(1, 0, 3, 2, 4).reshape(bsz, seq, nh, d).astype(q.dtype)

def odd_mixer(h, w_in, w_out):
    bsz, seq, _ = h.shape
    q, k, v = (t.reshape(bsz, seq, SB_HEADS, SB_HEAD_DIM) for t in jnp.split(h @ w_in, 3, axis=-1))
    o = stick_breaking_attention(q, k, v)
    return o.reshape(bsz, seq, D_MODEL) @ w_out

def swiglu(h, w_in, w_out):
    gate, up = jnp.split(h @ w_in, 2, axis=-1)
    return (jax.nn.silu(gate) * up) @ w_out

def setup_inputs(seed: int = 0) -> dict:
    key = jax.random.key(seed)
    ks = iter(jax.random.split(key, 32))
    f32 = jnp.float32
    D, F = D_MODEL, FFN_HIDDEN
    G, P, Hs = S5_GROUPS, S5_STATE, S5_GROUP

    def nrm(shape, scale):
        return scale * jax.random.normal(next(ks), shape, f32)

    def unif(shape, lo, hi):
        return jax.random.uniform(next(ks), shape, f32, lo, hi)

    x = nrm((BATCH, SEQ, D), 1.0)
    c = nrm((BATCH, D), 1.0)
    ada_w = nrm((DEPTH, D, 6 * D), D ** -0.5)
    ada_b = nrm((DEPTH, 6 * D), 0.02)
    norm_mix_w = 1.0 + nrm((DEPTH, D), 0.02)
    norm_ffn_w = 1.0 + nrm((DEPTH, D), 0.02)
    ffn_w_in = nrm((DEPTH, D, 2 * F), D ** -0.5)
    ffn_w_out = nrm((DEPTH, F, D), F ** -0.5)

    hy_w_in = nrm((N_EVEN, D, EVEN_IN), D ** -0.5)
    hy_conv_w = nrm((N_EVEN, CONV_K, 3 * GDN_WIDTH), CONV_K ** -0.5)
    hy_a_log = jnp.log(unif((N_EVEN, GDN_HEADS), 1.0, 16.0))
    dt = jnp.exp(unif((N_EVEN, GDN_HEADS), math.log(1e-3), math.log(1e-1)))
    hy_dt_bias = dt + jnp.log(-jnp.expm1(-dt))
    hy_head_norm_w = 1.0 + nrm((N_EVEN, GDN_HEAD_DIM), 0.02)
    s5_lam_re = -0.5 + nrm((N_EVEN, G, P), 0.01)
    s5_lam_im = jnp.pi * jnp.arange(P, dtype=f32) + nrm((N_EVEN, G, P), 0.01)
    s5_log_dt = unif((N_EVEN, G), math.log(1e-3), math.log(1e-1))
    s5_b_re = nrm((N_EVEN, G, P, Hs), (2 * Hs) ** -0.5)
    s5_b_im = nrm((N_EVEN, G, P, Hs), (2 * Hs) ** -0.5)
    s5_c_re = nrm((N_EVEN, G, Hs, P), 0.5)
    s5_c_im = nrm((N_EVEN, G, Hs, P), 0.5)
    s5_d = nrm((N_EVEN, S5_WIDTH), 1.0)
    s5_glu_w = nrm((N_EVEN, S5_WIDTH, S5_WIDTH), S5_WIDTH ** -0.5)
    s5_glu_b = nrm((N_EVEN, S5_WIDTH), 0.02)
    hy_w_out = nrm((N_EVEN, D, D), D ** -0.5)

    sb_w_in = nrm((N_ODD, D, 3 * D), D ** -0.5)
    sb_w_out = nrm((N_ODD, D, D), D ** -0.5)
    final_norm_w = 1.0 + nrm((D,), 0.02)
    return {"x": x, "c": c, "ada_w": ada_w, "ada_b": ada_b,
            "norm_mix_w": norm_mix_w, "norm_ffn_w": norm_ffn_w,
            "ffn_w_in": ffn_w_in, "ffn_w_out": ffn_w_out,
            "hy_w_in": hy_w_in, "hy_conv_w": hy_conv_w, "hy_a_log": hy_a_log,
            "hy_dt_bias": hy_dt_bias, "hy_head_norm_w": hy_head_norm_w,
            "s5_lam_re": s5_lam_re, "s5_lam_im": s5_lam_im, "s5_log_dt": s5_log_dt,
            "s5_b_re": s5_b_re, "s5_b_im": s5_b_im, "s5_c_re": s5_c_re, "s5_c_im": s5_c_im,
            "s5_d": s5_d, "s5_glu_w": s5_glu_w, "s5_glu_b": s5_glu_b, "hy_w_out": hy_w_out,
            "sb_w_in": sb_w_in, "sb_w_out": sb_w_out, "final_norm_w": final_norm_w}

def reference(x, c, ada_w, ada_b, norm_mix_w, norm_ffn_w, ffn_w_in, ffn_w_out,
              hy_w_in, hy_conv_w, hy_a_log, hy_dt_bias, hy_head_norm_w,
              s5_lam_re, s5_lam_im, s5_log_dt, s5_b_re, s5_b_im, s5_c_re, s5_c_im,
              s5_d, s5_glu_w, s5_glu_b, hy_w_out, sb_w_in, sb_w_out, final_norm_w):
    h = x
    c_act = jax.nn.silu(c)
    for i in range(DEPTH):
        mod = (c_act @ ada_w[i] + ada_b[i])[:, None, :]
        sh_m, sc_m, gt_m, sh_f, sc_f, gt_f = jnp.split(mod, 6, axis=-1)
        hn = rms_norm(h, norm_mix_w[i]) * (1.0 + sc_m) + sh_m
        j = i // 2
        if i % 2 == 0:
            y = even_mixer(hn, hy_w_in[j], hy_conv_w[j], hy_a_log[j], hy_dt_bias[j], hy_head_norm_w[j],
                           s5_lam_re[j], s5_lam_im[j], s5_log_dt[j], s5_b_re[j], s5_b_im[j],
                           s5_c_re[j], s5_c_im[j], s5_d[j], s5_glu_w[j], s5_glu_b[j], hy_w_out[j])
        else:
            y = odd_mixer(hn, sb_w_in[j], sb_w_out[j])
        h = h + gt_m * y
        hn = rms_norm(h, norm_ffn_w[i]) * (1.0 + sc_f) + sh_f
        h = h + gt_f * swiglu(hn, ffn_w_in[i], ffn_w_out[i])
    return rms_norm(h, final_norm_w)


_drawn_inputs = setup_inputs


def setup_inputs(seed=0):
    import zlib

    import numpy as np

    out = dict(_drawn_inputs(seed))
    spreads = {}
    factors = {'norm_mix_w': 3.751,
     'norm_ffn_w': 3.116,
     'hy_head_norm_w': 8.0,
     's5_lam_re': 200.0,
     's5_glu_b': 64.0,
     'final_norm_w': 21.541,
     's5_lam_im': 24.28,
     's5_log_dt': 25.72,
     's5_b_re': 32.944,
     's5_b_im': 32.752,
     's5_c_re': 32.592,
     's5_c_im': 32.576}
    for name, (base, spread) in spreads.items():
        noise = np.random.default_rng([zlib.crc32(name.encode()), seed]).standard_normal(out[name].shape)
        drawn = base * np.exp(spread * noise) if base else spread * noise
        out[name] = __import__('jax').numpy.asarray(drawn.astype(out[name].dtype))
    for name, factor in factors.items():
        out[name] = (out[name] * factor).astype(out[name].dtype)
    return out
```

```python
from contextlib import ExitStack

import numpy as np

import concourse.bass as bass
from concourse import mybir

F32 = mybir.dt.float32
F32R = mybir.dt.float32r
I32 = mybir.dt.int32
ALU = mybir.AluOpType
ACT = mybir.ActivationFunctionType
AX = mybir.AxisListType

P = 128
T = 512
D = 1024
KT = D // P
TT = T // P
F = 2816
W = 512
NH = 4
EPS = 1e-6
KB = 1024

G, GH, GP = 32, 16, 64
PAIRS = G // 2
SC = 8
NC = T // SC

HALVES = (12, 10)
FT = sum(HALVES)

B_U, B_QKV, B_Z, B_GLU, B_OUT0, B_FF0 = 0, 4, 16, 20, 24, 32
FF_UNITS = 2 * (HALVES[0] + HALVES[1]) + 2 * 16
B_SB = B_FF0 + FF_UNITS
B_OUT1 = B_SB + 24
B_FF1 = B_OUT1 + 8
B_END = B_FF1 + FF_UNITS

GDN_STAGES = [("q", "k", "v"), ("kT", "qT", "bT"), ("gr",), ("at",), ("lt",), ("dT",), ("l",),
              ("d2", "d2t"), ("x1",), ("d4", "d4t"), ("x2",), ("d8t",), ("x3",), ("xt",),
              ("z0",), ("xc0",), ("xtc0",), ("z1",), ("xc1",), ("xtc1",), ("z2",), ("xtc2",),
              ("u", "w"), ("s0",), ("ws1",), ("s1",), ("ws2",), ("s2",), ("ws3",), ("oT",)]
GDN_AT = {}
for _stage in GDN_STAGES:
    for _h in range(NH):
        for _name in _stage:
            GDN_AT[(_name, _h)] = len(GDN_AT)

TWO_PI = 2 * np.pi
PI_1 = 6.28125
PI_2 = float(np.float32(0.0019350051879882812))
PI_3 = TWO_PI - PI_1 - PI_2
PI_BELOW = float(np.nextafter(np.float32(np.pi), np.float32(0)))
LN2_1, LN2_2 = 0.693359375, -2.12194440e-4
ROUND = 12582912.0



def trunk(nc, x, c, ada_w, ada_b, norm_mix_w, norm_ffn_w, ffn_w_in, ffn_w_out, hy_w_in, hy_conv_w,
          hy_a_log, hy_dt_bias, hy_head_norm_w, s5_lam_re, s5_lam_im, s5_log_dt, s5_b_re, s5_b_im,
          s5_c_re, s5_c_im, s5_d, s5_glu_w, s5_glu_b, hy_w_out, sb_w_in, sb_w_out, final_norm_w,
          out):
    ctx = ExitStack()
    with ctx:
        base = -(-nc.sbuf_base // 64) * 64

        def at(name, offset, shape, dt=F32):
            return nc.alloc_sbuf_tensor_at(name, shape, dt, offset=base + round(offset * KB))

        h = at("h", 0, [P, KT, T])
        raw = [at(f"raw{s}", 16 + 8 * s, [P, 2048]) for s in range(2)]
        whi = [at(f"whi{s}", 32 + 8 * s, [P, 2048], F32R) for s in range(2)]
        wlo = [at(f"wlo{s}", 48 + 8 * s, [P, 2048], F32R) for s in range(2)]
        hn_hi = at("hn_hi", 64, [P, KT, T], F32R)
        hn_lo = at("hn_lo", 80, [P, KT, T], F32R)
        ff_hi = at("ff_hi", 96, [P, 12, T], F32R)
        ff_lo = at("ff_lo", 120, [P, 12, T], F32R)
        ada1_in = [at(f"ada1_in{s}", 144 + 12 * s, [P, 3072]) for s in range(2)]
        ada1_acc = at("ada1_acc", 168, [P, 3072])
        x_tok = at("x_tok", 64, [P, TT, D])
        lam = at("lam", 80, [16, 32, P])
        w_in = at("w_in", 96, [P, 2, PAIRS, P])
        b_re, b_im = (at(n, 112 + i, [P, PAIRS, GH]) for i, n in enumerate(("b_re", "b_im")))
        c_re, nc_re, nc_im = (at(n, 114 + i, [P, PAIRS, GH])
                              for i, n in enumerate(("c_re", "nc_re", "nc_im")))
        bb_re, bb_im = (at(n, 117 + i, [P, PAIRS, GH]) for i, n in enumerate(("bb_re", "bb_im")))
        w_ba = at("w_ba", 119, [P, KT, 8])
        w_ba_hi, w_ba_lo = at("w_ba_hi", 119.25, [P, KT, 8], F32R), at("w_ba_lo", 119.5, [P, KT, 8], F32R)
        u_perm = at("u_perm", 104, [P, 4, SC, NC])
        v_re = at("v_re", 120, [P, PAIRS, SC + 1, GH])
        v_im = at("v_im", 129, [P, PAIRS, SC + 1, GH])
        m_in = at("m_in", 138, [P, G, P])
        u_rows = at("u_rows", 154, [P, G, NC])
        m_pair, u_pair = (t[:, :, :].rearrange("p (i two) m -> p i two m", two=2) for t in (m_in, u_rows))
        wt_re = at("wt_re", 154, [P, PAIRS, SC, GH])
        wt_im = at("wt_im", 162, [P, PAIRS, SC, GH])
        s_re, s_im = at("s_re", 162, [P, PAIRS, NC]), at("s_im", 166, [P, PAIRS, NC])
        c_raw = at("c_raw", 170, [P, 2, 4, P])
        v_t = at("v_t", 138, [P, PAIRS, SC + 1, GH])
        wt_t = at("wt_t", 172, [P, 1024])
        scan_a, scan_b = at("scan_a", 170, [P, 784]), at("scan_b", 173.125, [P, 784])
        pw_re, pw_im = (at(n, 176.25 + 0.5625 * i, [P, SC + 1, PAIRS])
                        for i, n in enumerate(("pw_re", "pw_im")))
        f_co = at("f_co", 177.375, [P, 2, PAIRS])
        y_s5 = at("y_s5", 162, [P, 4, SC, NC])
        u_again = at("u_again", 170, [P, 4, SC, NC])
        ys_hi, ys_lo = at("ys_hi", 154, [P, 4, T], F32R), at("ys_lo", 170, [P, 4, T], F32R)
        ada0_in = [at(f"ada0_in{s}", 178 + 4 * s, [P, 1024]) for s in range(2)]
        ada0_acc = [at("ada0_acc0", 186, [P, 1024]), at("ada0_acc1", 194.5, [P, 1024])]
        conv = at("conv", 96, [P, 3, NH, T])
        z_act = at("z_act", 138, [P, NH, T])

        def gdn(name, offset):
            return at(name, offset, [P, NH, TT, P])

        kT, qT, bT = gdn("kT", 96), gdn("qT", 104), gdn("bT", 112)
        attnT, LT = gdn("attnT", 104), gdn("LT", 112)
        q_tok, k_tok, v_tok = gdn("q_tok", 120), gdn("k_tok", 128), gdn("v_tok", 64)
        kb_tok, qd_tok = gdn("kb_tok", 72), gdn("qd_tok", 80)
        kd_tok, rk_tok = gdn("kd_tok", 88), gdn("rk_tok", 146)
        qdT, dec = gdn("qdT", 120), gdn("dec", 128)
        Da, DaT, Db, DbT, X = (gdn(n, o) for n, o in (("Da", 72), ("DaT", 80), ("Db", 96),
                                                      ("DbT", 128), ("X", 162)))
        XT, Z, vn, wT = gdn("XT", 72), gdn("Z", 96), gdn("vn", 64), gdn("wT", 146)
        o_n, o_z = gdn("o_n", 72), at("o_z", 80, [P, NH, T])
        mo_hi, mo_lo = at("mo_hi", 96, [P, NH, T], F32R), at("mo_lo", 112, [P, NH, T], F32R)
        sb_qk = at("sb_qk", 144, [P, 2, 4, T])
        sb_v = at("sb_v", 160, [P, TT, 4, P])
        zb = [at("zb0", 168, [P, 1280]), at("zb1", 136, [P, 1280])]
        e_b = at("e_b", 173, [P, 1280])
        sp_hi, sp_lo = at("sp_hi", 178, [P, 1280], F32R), at("sp_lo", 183, [P, 1280], F32R)
        w_b = at("w_b", 112, [P, 1280])
        ones_r, tril_r = at("ones_r", 117, [P, P], F32R), at("tril_r", 117.5, [P, P], F32R)
        below = at("below", 118, [P, P])
        out_tok = at("out_tok", 96, [P, TT, D])

        cursor = [190.0]

        def small(name, shape, dt=F32):
            t = at(name, cursor[0], shape, dt)
            cursor[0] += -(-int(np.prod(shape[1:])) // 8) * 8 * 4 / KB
            return t

        ident, ones, triu, strict, tril = (small(n, [P, P])
                                           for n in ("ident", "ones", "triu", "strict", "tril"))
        bd16 = small("bd16", [P, P])
        level = [small(f"level{i}", [P, P]) for i in range(3)]
        tmp = [small(f"tmp{i}", [P, T]) for i in range(2)]
        S = at("S", 194.5, [P, NH, P])
        sq = small("sq", [P, T])
        sq_sum = small("sq_sum", [P, T])
        diag = small("diag", [P, TT, P])
        vec_a, vec_b = at("vec_a", 202.5, [96, P]), at("vec_b", 203.0, [97, P])
        vb = small("vb", [P, 97])
        ada_bias = small("ada_bias", [P, 96])
        mod = small("mod", [P, 96])
        c_col, c_act = small("c_col", [P, 8]), small("c_act", [P, 8])
        n_scale = small("n_scale", [P, KT])
        cst = small("cst", [P, 2])
        ss, rstd = small("ss", [P, TT]), small("rstd", [P, TT])
        ba = small("ba", [P, TT, 8])
        beta, g_log, gc, gc_exp, k_fac, s_fac = (small(n, [P, TT, NH]) for n in (
            "beta", "g_log", "gc", "gc_exp", "k_fac", "s_fac"))
        g_t = [at(f"g_t{i}", 177.5 + 0.0625 * i, [P, TT, NH]) for i in range(2)]
        neg_a, dt_b = small("neg_a", [P, NH]), small("dt_b", [P, NH])
        qk_ss, qk_rn = small("qk_ss", [P, 2, NH, TT]), small("qk_rn", [P, 2, NH, TT])
        o_ss, o_rn = small("o_ss", [P, NH, TT]), small("o_rn", [P, NH, TT])
        q_pw = small("q_pw", [P, 2, SC, PAIRS])
        g_tq = at("g_tq", 176.0, [P, 4, PAIRS])
        bb_t = at("bb_t", 175.0, [P, PAIRS, GH])
        tmp_o = [sq, diag[:, :, :].rearrange("p c i -> p (c i)")]
        assert base + cursor[0] * KB <= nc.sbuf_usable_end, cursor
        EPS_C, ONE_C = cst[:, 0:1], cst[:, 1:2]
        CONV, NMIX, NFFN, NFIN, S5D, GLUB, HNW = 0, 48, 64, 80, 88, 92, 96

        banks = ctx.enter_context(nc.psum_tensor("banks", [P, 8, T], F32))
        bank = [banks[:, i, :] for i in range(8)]
        flat = banks[:, :, :].rearrange("p b t -> p (b t)")

        u_dram = nc.dram_tensor("u_rows_dram", [SC, W, NC], F32, kind="Internal").ap()
        y_dram = nc.dram_tensor("y_rows_dram", [SC, W, NC], F32, kind="Internal").ap()

        def sem(name):
            return ctx.enter_context(nc.semaphore(name))

        raw_in = [sem(f"raw{s}_loaded") for s in range(2)]
        hi_done, lo_done = sem("weights_hi_done"), sem("weights_lo_done")
        block_done, block_free = sem("block_done"), sem("block_free")
        x_in, vec_in, c_in, lam_in, bc_in, gdn_in = (sem(n) for n in (
            "x_loaded", "vectors_loaded", "c_loaded", "lambda_loaded", "b_and_c_loaded",
            "gdn_vectors_loaded"))
        consts, consts_t = sem("constants_ready"), sem("constant_steps")
        vec_t, vec_ready, c_ready = sem("vectors_turned"), sem("vectors_ready"), sem("c_ready")
        x_t, x_done = sem("x_turned"), sem("x_copied")
        ada0_ld = [sem(f"ada0_loaded{s}") for s in range(2)]
        ada1_ld = [sem(f"ada1_loaded{s}") for s in range(2)]
        ada_used, mod_sum, mod_done = sem("ada_tiles_used"), sem("mod_summed"), sem("mod_ready")
        sq_done, sq_added, ss_done = sem("squares_ready"), sem("squares_added"), sem("mean_square_ready")
        sd_done, diag_done, rb_done = sem("norm_root_ready"), sem("norm_diag_ready"), sem("norm_rows_ready")
        h_scaled, hi_norm, hn_done = sem("h_scaled"), sem("hn_hi_done"), sem("hn_done")
        dve_step, act_step, pool_step = sem("dve_steps"), sem("act_steps"), sem("pool_steps")
        dt_done, lam_exp, lam_trig, lam_done = (sem(n) for n in (
            "dt_ready", "lambda_angles", "lambda_trig", "lambda_ready"))
        lam_t, pw_done, c_t, c_done, bb_done, v_done, wt_done, wt_t_done, w_done = (sem(n) for n in (
            "powers_turned", "powers_ready", "c_turned", "c_ready_s5", "b_bar_ready", "v_ready",
            "w_rows_ready", "w_turned", "w_ready"))
        m_zero, k_sum, k_done, m_done, q_done = (sem(n) for n in (
            "m_zeroed", "taps_summed", "taps_ready", "m_ready", "block_powers_ready"))
        u_copied, u_out, u_in, p_sum, p_done, scan_done = (sem(n) for n in (
            "u_permuted", "u_stored", "u_rows_loaded", "chunk_inputs_summed", "chunk_inputs_ready",
            "states_ready"))
        y_sum, y_done, y_out, y_in, u2_in = (sem(n) for n in (
            "y_summed", "y_rows_ready", "y_stored", "y_loaded", "u_loaded_again"))
        y_du, y_act, ys_hi_done, ys_done, glu_sig, glu_mul, mix_s5 = (sem(n) for n in (
            "y_with_skip", "y_gelu", "ys_hi_ready", "ys_ready", "glu_gate_ready", "glu_hi_ready",
            "s5_half_ready"))
        ba_in, ba_split, ba_sum, ba_done = (sem(n) for n in (
            "w_ba_loaded", "w_ba_split", "ba_summed", "ba_ready"))
        g_done, gc_sum, gc_diff, gates = (sem(n) for n in (
            "g_ready", "g_summed", "g_differences", "gate_factors_ready"))
        conv_tap, conv_done = sem("conv_first_tap"), sem("conv_done")
        silu_done = sem("conv_silu_done")
        gdn_done = sem("gdn_product_done")
        drained = [sem(f"gdn_bank{i}_drained") for i in range(4)]
        qk_sq, qk_root, qn_done, kn_done, kb_done, rv_done = (sem(n) for n in (
            "qk_squares", "qk_root", "q_normed", "k_normed", "k_beta", "v_beta"))
        qd_done, rk_done, kd_done = sem("q_decayed"), sem("rk_ready"), sem("k_decayed")
        dec_exp, dec_done, lt_done, dat_done, x0_done = (sem(n) for n in (
            "decay_exp", "decay_masked", "lt_masked", "dat_ready", "x0_ready"))
        o_done, o_sq_done, o_root, on_done, mo_hi_done, mo_done = (sem(n) for n in (
            "o_done", "o_squares", "o_root", "o_normed", "gdn_half_hi", "gdn_half_ready"))
        gate_act, up_mul, ff_hi_done = (sem(n) for n in (
            "gate_silu", "gate_times_up", "hidden_hi"))
        qkv_done, sbz, sbz_done, sbe, sb_sp, sb_mask = (sem(n) for n in (
            "sb_qkv_ready", "sb_scores_done", "sb_scores_copied", "sb_exp", "sb_softplus",
            "sb_softplus_masked"))
        sb_spe, sb_hi, sb_lo, sb_c, sb_w, sb_wm, sb_p, sb_o, sbo_hi, sbo_done = (sem(n) for n in (
            "sb_log", "sb_softplus_hi", "sb_softplus_split", "sb_sums_done", "sb_exponents",
            "sb_exponents_masked", "sb_weights", "sb_values_done", "sb_out_hi", "sb_out_ready"))
        pw0_done = sem("power_zero_set")
        sb_abs, cons_r, below_done = sem("sb_abs"), sem("rounded_constants"), sem("mask_ready")
        g_abs, g_ln, beta_done, qk_red, gr_done_, o_red, oz_done, glu_hi = (sem(n) for n in (
            "decay_input_abs", "softplus_log", "beta_ready", "qk_squares_summed", "unused",
            "o_squares_summed", "o_gated", "glu_product_hi"))
        fin_t, fin_copied, out_sem = sem("output_turned"), sem("output_copied"), sem("output_stored")

        def gp(name, hd):
            q = GDN_AT[(name, hd)]
            return q, 4 + q % 4, q // 4 + 1

        def wait_drained(eng, name, hd):
            q = GDN_AT[(name, hd)]
            eng.wait_ge(drained[q % 4], q // 4 + 1)

        def bc(ap, n):
            return ap.unsqueeze(2).to_broadcast([P, ap.shape[1], n])

        def perm(ap):
            return ap.rearrange("p (c j) -> p j c", j=SC)

        block = ctx.enter_context(nc.Block())

        @block.sync
        def _(sp):
            def load_slot(n, s, views, first=False):
                if not first:
                    sp.wait_ge(lo_done, n - 1)
                for dst, src in views:
                    sp.dma_start(dst, src).then_inc(raw_in[s], 16)

            def cols(wt, col, k=KT, width=256):
                def views(s):
                    half = k // 2
                    dst = raw[s][:, 0:k * width].rearrange("p (k m) -> p k m", k=k)
                    src = wt[:, bass.ds(col, width)].rearrange("(k p) m -> p k m", p=P)
                    return [(dst[:, 0:half, :], src[:, 0:half, :]), (dst[:, half:k, :], src[:, half:k, :])]
                return views

            def ada0_tile(part, t):
                n = 8 * part + t
                if n >= 2:
                    sp.wait_ge(ada_used, n - 1)
                src = ada_w[0].rearrange("(p t) n -> p t n", t=8)[:, t, part * D:(part + 1) * D]
                sp.dma_start(ada0_in[n % 2][:, :], src).then_inc(ada0_ld[n % 2], 16)

            x_rows = x[0].rearrange("(t p) d -> p t d", p=P)
            for t in range(TT):
                sp.dma_start(x_tok[:, t, :], x_rows[:, t, :]).then_inc(x_in, 16)
            for part in range(2):
                for t in range(8):
                    ada0_tile(part, t)
            w = hy_w_in[0]
            U0 = 4 * W + 2 * NH
            load_slot(0, 0, cols(w, U0)(0), first=True)
            load_slot(1, 1, cols(w, U0 + 256)(1), first=True)
            for s in range(2):
                load_slot(2 + s, s, cols(w, 256 * s)(s))
            for t in range(4):
                sp.wait_ge(block_free, B_U + t + 1)
                sp.dma_start(u_dram[:, t * P:(t + 1) * P, :].rearrange("j p c -> p j c"),
                             u_perm[:, t, :, :]).then_inc(u_out, 16)
            sp.wait_ge(u_out, 64)
            sp.wait_ge(w_done, 8)
            for j in range(SC):
                sp.dma_start(u_rows[j * GH:(j + 1) * GH, :, :],
                             u_dram[j].rearrange("(g h) c -> h g c", h=GH)).then_inc(u_in, 16)
            for part in range(2, 4):
                for t in range(8):
                    ada0_tile(part, t)
            sp.wait_ge(k_done, 8)
            for j in range(1, SC):
                sp.dma_start(m_in[j * GH:(j + 1) * GH, :, j * GH:P],
                             m_in[0:GH, :, 0:P - j * GH]).then_inc(m_done, 16)
            for n in range(4, 8):
                load_slot(n, n % 2, cols(w, 256 * (n - 2))(n % 2))
                for t in range(4):
                    i = 4 * (n - 4) + t
                    ada0_tile(4 + i // 8, i % 8)
            load_slot(8, 0, cols(w, 256 * 6)(0))
            load_slot(9, 1, cols(w, 256 * 7)(1))
            for i in range(SC):
                if i == 0:
                    sp.wait_ge(y_done, 4)
                sp.dma_start(y_dram[i].rearrange("(g h) c -> h g c", h=GH),
                             u_rows[i * GH:(i + 1) * GH, :, :]).then_inc(y_out, 16)
            sp.wait_ge(y_out, 128)
            for t in range(4):
                sp.dma_start(y_s5[:, t, :, :],
                             y_dram[:, t * P:(t + 1) * P, :].rearrange("i p c -> p i c")).then_inc(y_in, 16)
                sp.dma_start(u_again[:, t, :, :],
                             u_dram[:, t * P:(t + 1) * P, :].rearrange("i p c -> p i c")).then_inc(u2_in, 16)
            for s in range(2):
                load_slot(10 + s, s, cols(s5_glu_w[0], 256 * s, k=4)(s))
            with sp.Fori(0, 2) as i:
                for s in range(2):
                    load_slot(12 + 2 * i + s, s, cols(hy_w_out[0], 512 * i + 256 * s)(s))

            def ffn(layer, slot):
                first = 0
                for half, n_f in enumerate(HALVES):
                    with sp.Fori(0, n_f // 2) as i:
                        for s in range(2):
                            sp.wait_ge(lo_done, slot + 2 * i + s - 1)
                            dst = raw[s][:, :].rearrange("p (k two m) -> p k two m", k=KT, two=2)
                            for two in range(2):
                                src = ffn_w_in[layer][:, bass.ds(two * F + (first + s) * P + i * 256, P)]
                                sp.dma_start(dst[:, :, two, :], src.rearrange("(k p) m -> p k m", p=P))\
                                  .then_inc(raw_in[s], 16)
                    slot += n_f
                    rows = ffn_w_out[layer][first * P:(first + n_f) * P, :]
                    with sp.Fori(0, 2) as i:
                        for s in range(4):
                            load_slot(slot + 4 * i + s, s % 2,
                                      cols(rows, 512 * i + 128 * s, k=n_f, width=P)(s % 2))
                            if layer == 0:
                                sp.wait_ge(ada_used, 47 + 8 * half + s + 4 * i)
                                src = ada_w[1].rearrange("(p t) n -> p (t n)", t=8)[
                                    :, bass.ds(s * 6 * D + half * 3 * D + i * (4 * 6 * D), 3 * D)]
                                sp.dma_start(ada1_in[s % 2][:, :], src).then_inc(ada1_ld[s % 2], 16)
                    slot += 8
                    first += n_f

            ffn(0, 16)
            with sp.Fori(0, 2) as i:
                for pair in range(2):
                    for kind in range(3):
                        s = (3 * pair + kind) % 2
                        load_slot(54 + 6 * i + 3 * pair + kind, s,
                                  cols(sb_w_in[0], kind * D + 256 * pair + 512 * i)(s))
            with sp.Fori(0, 2) as i:
                for s in range(2):
                    load_slot(66 + 2 * i + s, s, cols(sb_w_out[0], 512 * i + 256 * s)(s))
            ffn(1, 70)
            for t in range(TT):
                sp.wait_ge(fin_copied, KT)
                sp.dma_start(out[0].rearrange("(t p) d -> p t d", p=P)[:, t, :],
                             out_tok[:, t, :]).then_inc(out_sem, 16)
            sp.wait_ge(out_sem, 16 * TT)

        @block.tensor
        def _(pe):
            def pass3(o, lh, ll, rh, rl, first, last):
                pe.matmul(o, lh, rh, start=first, stop=False)
                pe.matmul(o, lh, rl, start=False, stop=False)
                return pe.matmul(o, ll, rh, start=False, stop=last)

            def gemm(unit, b, s, j, rhs_hi, rhs_lo, k_tiles=KT, width=256, pitch=None, units=1):
                mh = whi[s][:, 0:k_tiles * width].rearrange("p (k m) -> p k m", k=k_tiles)
                ml = wlo[s][:, 0:k_tiles * width].rearrange("p (k m) -> p k m", k=k_tiles)
                c0, c1 = j * P, (j + 1) * P
                for k in range(k_tiles):
                    last = pass3(bank[b][:, :], mh[:, k, c0:c1], ml[:, k, c0:c1],
                                 rhs_hi[:, k, :], rhs_lo[:, k, :], k == 0, k == k_tiles - 1)
                last.then_inc(block_done, units)

            def slot_ready(n):
                pe.wait_ge(lo_done, n + 1)

            def four_blocks(slot, unit, rhs_hi, rhs_lo, k_tiles=KT, drained_units=3, first=False):
                for s in range(2):
                    slot_ready(slot + s)
                    for j in range(2):
                        r = 2 * s + j
                        if not first:
                            pe.wait_ge(block_free, unit + r - 3)
                        gemm(unit + r, r, s, j, rhs_hi, rhs_lo, k_tiles)

            def norm(n):
                pe.wait_ge(sq_added, 8 * (n + 1))
                for c_ in range(TT):
                    last = pe.matmul(bank[6][:, c_:c_ + 1], sq_sum[:, c_ * P:(c_ + 1) * P],
                                     ones[:, 0:1], start=True, stop=True)
                last.then_inc(ss_done, 1)
                pe.wait_ge(diag_done, n + 1)
                pe.matmul(bank[6][:, :], ones[:, :], diag[:, :, :].rearrange("p c i -> p (c i)"),
                          start=True, stop=True).then_inc(rb_done, 1)

            def mod_parts(part, accs, n_used):
                pe.wait_ge(ada_used, n_used)
                for n, acc in enumerate(accs):
                    for k in range(KT):
                        m = 8 * (part + n) + k
                        last = pe.matmul(bank[7][:, m:m + 1], acc[:, k * P:(k + 1) * P], ones[:, 0:1],
                                         start=True, stop=True)
                last.then_inc(mod_sum, 1)

            pe.wait_ge(consts, 1)
            pe.wait_ge(vec_in, 16 * 8)
            pe.transpose(bank[7][:, 96:192], vec_a[:, :], ident[0:96, 0:96])
            pe.transpose(bank[7][:, 192:289], vec_b[:, :], ident[0:97, 0:97]).then_inc(vec_t, 1)
            pe.wait_ge(x_in, 16 * TT)
            for k in range(KT):
                b = k % 4
                if k >= 4:
                    pe.wait_ge(x_done, k - 3)
                for t in range(TT):
                    last = pe.transpose(bank[b][:, t * P:(t + 1) * P], x_tok[:, t, k * P:(k + 1) * P],
                                        ident[:, :])
                last.then_inc(x_t, 1)
            pe.wait_ge(bc_in, 16 * 8)
            for part in range(2):
                for q in range(4):
                    last = pe.transpose(bank[4 + part][:, q * P:(q + 1) * P], c_raw[:, part, q, :],
                                        ident[:, :])
            last.then_inc(c_t, 1)
            pe.wait_ge(lam_done, 1)
            pe.wait_ge(x_done, KT)
            for n in range(18):
                row = (16 + n) if n < 16 else 12 + (n - 16)
                last = pe.transpose(bank[3][:, 16 * n:16 * n + 16], lam[:, row, :], ident[0:16, 0:16])
            last.then_inc(lam_t, 1)
            mod_parts(0, ada0_acc, 16)
            norm(0)
            pe.wait_ge(hn_done, 8)
            pe.wait_ge(ba_split, 2)
            for t in range(TT):
                for k in range(KT):
                    last = pass3(bank[7][:, 300 + 8 * t:308 + 8 * t], hn_hi[:, k, t * P:(t + 1) * P],
                                 hn_lo[:, k, t * P:(t + 1) * P], w_ba_hi[:, k, :], w_ba_lo[:, k, :],
                                 k == 0, k == KT - 1)
            last.then_inc(ba_sum, 1)
            pe.wait_ge(bb_done, 1)
            four_blocks(0, B_U, hn_hi, hn_lo, first=True)
            pe.wait_ge(wt_done, 2)
            for q in range(8):
                src = (wt_re, wt_im)[q // 4]
                b = 4 + q % 2
                if q >= 2:
                    pe.wait_ge(w_done, q - 1)
                for r in range(4):
                    i = 4 * (q % 4) + r
                    last = pe.transpose(bank[b][:, r * P:(r + 1) * P],
                                        src[:, i, :, :].rearrange("p j h -> p (j h)"), ident[:, :])
                last.then_inc(wt_t_done, 1)
            pe.wait_ge(bb_done, 1)
            pe.wait_ge(v_done, 1)
            for q in range(8):
                b = 4 + q % 2
                if q >= 2:
                    pe.wait_ge(k_done, q - 1)
                else:
                    pe.wait_ge(w_done, 7 + q)
                i0, par = 4 * (q // 2), q % 2
                rows = slice(64 * par, 64 * par + 64)
                for r in range(4):
                    i = i0 + r
                    o = bank[b][0:GH, r * P:(r + 1) * P]
                    pe.matmul(o, bb_re[rows, i, :], v_re[rows, i, 0:SC, :], start=True, stop=False)
                    last = pe.matmul(o, bb_im[rows, i, :], v_im[rows, i, 0:SC, :], start=False, stop=True)
                last.then_inc(k_sum, 1)
            pe.wait_ge(g_done, 1)
            gl = g_log[:, :, :].rearrange("p c h -> p (c h)")
            pe.matmul(bank[7][:, 340:356], triu[:, :], gl, start=True, stop=True)
            pe.matmul(bank[7][:, 356:372], ones[:, :], gl, start=True, stop=True).then_inc(gc_sum, 1)
            mod_parts(2, ada0_acc, 32)

            pe.wait_ge(w_done, 8)
            pe.wait_ge(k_done, 8)
            pe.wait_ge(gc_diff, 1)
            pe.wait_ge(mod_done, 2)
            pe.wait_ge(u_in, 16 * SC)
            for part in range(2):
                for hb in range(2):
                    b = 4 + 2 * part + hb
                    for r in range(8):
                        for par in range(2):
                            i = 8 * hb + r
                            last = pe.matmul(bank[b][64 * par:64 * par + 64, r * NC:(r + 1) * NC],
                                             w_in[:, part, i, 64 * par:64 * par + 64],
                                             u_rows[:, 2 * i + par, :], start=True, stop=True)
                    last.then_inc(p_sum, 1)
            with pe.Fori(0, 3) as i:
                four_blocks(2 + 2 * i, B_QKV + 4 * i, hn_hi, hn_lo)
            pe.wait_ge(p_done, 4)
            pe.wait_ge(scan_done, 1)
            pe.wait_ge(m_done, 16 * (SC - 1))
            for q in range(4):
                par, i0 = q // 2, 8 * (q % 2)
                rows = slice(64 * par, 64 * par + 64)
                for r in range(8):
                    i, g = i0 + r, 2 * (i0 + r) + par
                    o = bank[4 + q][:, r * NC:(r + 1) * NC]
                    pe.matmul(o, m_in[:, g, :], u_rows[:, g, :], start=True, stop=False)
                    o = bank[4 + q][:, r * NC + 1:(r + 1) * NC]
                    pe.matmul(o, v_re[rows, i, 1:SC + 1, :], s_re[rows, i, 0:NC - 1],
                              start=False, stop=False)
                    last = pe.matmul(o, v_im[rows, i, 1:SC + 1, :], s_im[rows, i, 0:NC - 1],
                                     start=False, stop=True)
                last.then_inc(y_sum, 1)
            four_blocks(8, B_Z, hn_hi, hn_lo)
            pe.wait_ge(y_done, 4)
            mod_parts(4, ada0_acc, 48)
            def product(name, hd, f, n=TT):
                q, b, _ = gp(name, hd)
                if q >= 4:
                    pe.wait_ge(drained[q % 4], q // 4)
                for c_ in range(n):
                    last = f(bank[b][:, c_ * P:(c_ + 1) * P], c_)
                last.then_inc(gdn_done, 1)

            def turn(name, hd, src):
                product(name, hd, lambda o, c_: pe.transpose(o, src[:, hd, c_, :], ident[:, :]))

            def mul(name, hd, l, r):
                product(name, hd, lambda o, c_: pe.matmul(o, l[:, hd, c_, :], r[:, hd, c_, :],
                                                          start=True, stop=True))

            pe.wait_ge(silu_done, 12)
            pe.wait_ge(mod_done, 3)
            cv = conv[:, :, :, :].rearrange("p w h (c i) -> p w h c i", c=TT)
            for hd in range(NH):
                for w_, name in enumerate(("q", "k", "v")):
                    turn(name, hd, cv[:, w_])
            for hd in range(NH):
                pe.wait_ge(kn_done, hd + 1)
                turn("kT", hd, k_tok)
                pe.wait_ge(qn_done, hd + 1)
                turn("qT", hd, q_tok)
                pe.wait_ge(kb_done, hd + 1)
                turn("bT", hd, kb_tok)
            for hd in range(NH):
                product("gr", hd, lambda o, c_: pe.matmul(
                    o, g_log[:, c_, hd:hd + 1].to_broadcast([P, P]), triu[:, :], start=True, stop=True))
            for hd in range(NH):
                wait_drained(pe, "qT", hd)
                wait_drained(pe, "kT", hd)
                mul("at", hd, kT, qT)
            for hd in range(NH):
                wait_drained(pe, "bT", hd)
                mul("lt", hd, kT, bT)
            for hd in range(NH):
                pe.wait_ge(qd_done, hd + 1)
                turn("dT", hd, qd_tok)
            pe.wait_ge(ys_done, 1)
            four_blocks(10, B_GLU, ys_hi, ys_lo, k_tiles=4)
            for hd in range(NH):
                pe.wait_ge(lt_done, hd + 1)
                turn("l", hd, LT)
            for hd in range(NH):
                pe.wait_ge(dat_done, hd + 1)
                wait_drained(pe, "l", hd)
                mul("d2", hd, DaT, Da)
                mul("d2t", hd, Da, DaT)
            for hd in range(NH):
                wait_drained(pe, "d2t", hd)
                pe.wait_ge(x0_done, hd + 1)
                mul("x1", hd, DbT, X)
            for hd in range(NH):
                wait_drained(pe, "d2", hd)
                mul("d4", hd, DbT, Db)
                mul("d4t", hd, Db, DbT)
            for hd in range(NH):
                wait_drained(pe, "d4t", hd)
                wait_drained(pe, "x1", hd)
                mul("x2", hd, DaT, X)
            for hd in range(NH):
                wait_drained(pe, "d4", hd)
                mul("d8t", hd, Da, DaT)
            for hd in range(NH):
                wait_drained(pe, "d8t", hd)
                wait_drained(pe, "x2", hd)
                mul("x3", hd, DbT, X)
            for hd in range(NH):
                wait_drained(pe, "x3", hd)
                turn("xt", hd, X)
            for lv in range(3):
                for hd in range(NH):
                    wait_drained(pe, "xt" if lv == 0 else f"xc{lv - 1}", hd)
                    mul(f"z{lv}", hd, LT, X)
                if lv < 2:
                    for hd in range(NH):
                        wait_drained(pe, f"z{lv}", hd)
                        if lv > 0:
                            wait_drained(pe, f"xtc{lv - 1}", hd)
                        mul(f"xc{lv}", hd, XT, Z)
                for hd in range(NH):
                    wait_drained(pe, f"z{lv}", hd)
                    if lv > 0:
                        wait_drained(pe, f"xtc{lv - 1}", hd)
                    mul(f"xtc{lv}", hd, Z, XT)
            for hd in range(NH):
                wait_drained(pe, "xtc2", hd)
                pe.wait_ge(rv_done, hd + 1)
                mul("u", hd, XT, v_tok)
                pe.wait_ge(rk_done, hd + 1)
                mul("w", hd, rk_tok, XT)
            for c_ in range(TT):
                for hd in range(NH):
                    if c_ == 0:
                        wait_drained(pe, "dT", hd)
                        wait_drained(pe, "u", hd)
                        wait_drained(pe, "w", hd)
                        pe.wait_ge(kd_done, hd + 1)
                        pe.wait_ge(block_free, B_OUT0)
                    else:
                        wait_drained(pe, f"s{c_ - 1}", hd)
                        product(f"ws{c_}", hd, lambda o, _: pe.matmul(
                            o, wT[:, hd, c_, :], S[:, hd, :], start=True, stop=True), n=1)
                        pe.matmul(bank[hd][:, c_ * P:(c_ + 1) * P], qdT[:, hd, c_, :], S[:, hd, :],
                                  start=True, stop=False)
                for hd in range(NH):
                    if c_ > 0:
                        wait_drained(pe, f"ws{c_}", hd)
                    last = pe.matmul(bank[hd][:, c_ * P:(c_ + 1) * P], attnT[:, hd, c_, :],
                                     vn[:, hd, c_, :], start=(c_ == 0), stop=True)
                    if c_ == TT - 1:
                        last.then_inc(o_done, 1)
                    else:
                        product(f"s{c_}", hd, lambda o, _: pe.matmul(
                            o, kd_tok[:, hd, c_, :], vn[:, hd, c_, :], start=True, stop=True), n=1)
            for hd in range(NH):
                pe.wait_ge(on_done, hd + 1)
                turn("oT", hd, o_n)
            pe.wait_ge(mo_done, NH)
            pe.wait_ge(mix_s5, 4)
            mix_hi = [mo_hi[:, k, :] for k in range(4)] + [ys_hi[:, k, :] for k in range(4)]
            mix_lo = [mo_lo[:, k, :] for k in range(4)] + [ys_lo[:, k, :] for k in range(4)]
            with pe.Fori(0, 2) as i:
                for s in range(2):
                    slot_ready(12 + 2 * i + s)
                    mh = whi[s][:, :].rearrange("p (k m) -> p k m", k=KT)
                    ml = wlo[s][:, :].rearrange("p (k m) -> p k m", k=KT)
                    for j in range(2):
                        r = 2 * s + j
                        pe.wait_ge(block_free, B_OUT0 + 4 * i + r - 3)
                        for k in range(KT):
                            last = pass3(bank[r][:, :], mh[:, k, j * P:(j + 1) * P],
                                         ml[:, k, j * P:(j + 1) * P], mix_hi[k], mix_lo[k],
                                         k == 0, k == KT - 1)
                        last.then_inc(block_done, 1)
            norm(1)

            def ffn(layer, slot, unit, n):
                hidden = FT * layer
                for half, n_f in enumerate(HALVES):
                    pe.wait_ge(hn_done, 8 * (n + 1))
                    with pe.Fori(0, n_f // 2) as i:
                        for s in range(2):
                            slot_ready(slot + 2 * i + s)
                            for two in range(2):
                                r = 2 * s + two
                                pe.wait_ge(block_free, unit + 4 * i + r - 3)
                                mh = whi[s][:, :].rearrange("p (k two m) -> p k two m", k=KT, two=2)
                                ml = wlo[s][:, :].rearrange("p (k two m) -> p k two m", k=KT, two=2)
                                for k in range(KT):
                                    last = pass3(bank[r][:, :], mh[:, k, two, :], ml[:, k, two, :],
                                                 hn_hi[:, k, :], hn_lo[:, k, :], k == 0, k == KT - 1)
                                last.then_inc(block_done, 1)
                    slot, unit, hidden = slot + n_f, unit + 2 * n_f, hidden + n_f
                    pe.wait_ge(block_free, unit)
                    with pe.Fori(0, 2) as i:
                        for s in range(4):
                            slot_ready(slot + 4 * i + s)
                            pe.wait_ge(block_free, unit + 8 * i + 2 * s - 3)
                            gemm(0, s, s % 2, 0, ff_hi, ff_lo, n_f, P, units=2)
                    slot, unit = slot + 8, unit + 16
                    if layer == 0:
                        mod_parts(6 + 3 * half, [ada1_acc[:, r * D:(r + 1) * D] for r in range(3)],
                                  56 + 8 * half)

            ffn(0, 16, B_FF0, 1)
            norm(2)
            off = (0, 512, 1024, 896)
            z_bank = (0, 1, 2, 1)
            z_col = (0, 0, 0, 384)
            pe.wait_ge(hn_done, 24)
            pe.wait_ge(cons_r, 1)

            def z_of(b0, i):
                return bank[b0 + z_bank[i]][:, z_col[i]:z_col[i] + T - P * i]

            with pe.Fori(0, 2) as it:
                for pair in range(2):
                    for kind in range(3):
                        idx = 3 * pair + kind
                        s = idx % 2
                        unit = B_SB + 12 * it + 2 * idx
                        slot_ready(54 + 6 * it + idx)
                        for j in range(2):
                            b = (2 * idx + j) % 4
                            pe.wait_ge(block_free, unit + j - 3)
                            if kind < 2:
                                gemm(0, b, s, j, hn_hi, hn_lo)
                                continue
                            mh = whi[s][:, :].rearrange("p (k m) -> p k m", k=KT)
                            ml = wlo[s][:, :].rearrange("p (k m) -> p k m", k=KT)
                            for tt in range(2):
                                t0 = (2 * j + tt) * P
                                for k in range(KT):
                                    last = pass3(bank[b][:, tt * 256:(tt + 1) * 256],
                                                 hn_hi[:, k, t0:t0 + P], hn_lo[:, k, t0:t0 + P],
                                                 mh[:, k, :], ml[:, k, :], k == 0, k == KT - 1)
                            last.then_inc(block_done, 1)
                pe.wait_ge(block_free, B_SB + 12 * it + 12)

                def scores(hd):
                    if hd > 0:
                        pe.wait_ge(sbz_done, 4 * it + hd)
                    for i in range(TT):
                        last = pe.matmul(z_of(0, i), sb_qk[:, 1, hd, i * P:(i + 1) * P],
                                         sb_qk[:, 0, hd, i * P:T], start=True, stop=True)
                    last.then_inc(sbz, 1)

                def sums(hd):
                    pe.wait_ge(sb_lo, 4 * it + hd + 1)
                    if hd > 0:
                        pe.wait_ge(sb_w, 4 * it + hd)
                    for i in range(TT):
                        o = z_of(3, i)
                        for j in range(i, TT):
                            lhs = tril_r if j == i else ones_r
                            oj = o[:, P * (j - i):]
                            n = T - P * j
                            pe.matmul(oj, lhs[:, :], sp_hi[:, off[j]:off[j] + n], start=(j == i), stop=False)
                            last = pe.matmul(oj, lhs[:, :], sp_lo[:, off[j]:off[j] + n],
                                             start=False, stop=(j == TT - 1))
                    last.then_inc(sb_c, 1)

                def values(hd):
                    pe.wait_ge(sb_p, 4 * it + hd + 1)
                    if hd >= 2:
                        pe.wait_ge(sbo_done, 4 * it + hd - 1)
                    for i in range(TT):
                        last = pe.matmul(bank[6 + hd % 2][:, P * i:T], sb_v[:, i, hd, :],
                                         w_b[:, off[i]:off[i] + T - P * i], start=(i == 0),
                                         stop=(i == TT - 1))
                    last.then_inc(sb_o, 1)

                scores(0)
                for hd in range(4):
                    if hd < 3:
                        scores(hd + 1)
                    sums(hd)
                    values(hd)
                pe.wait_ge(sbz_done, 4 * it + 4)
                pe.wait_ge(sb_w, 4 * it + 4)
                pe.wait_ge(sbo_done, 4 * it + 4)
            with pe.Fori(0, 2) as i:
                four_blocks(66 + 2 * i, B_OUT1 + 4 * i, ff_hi, ff_lo)
            norm(3)
            ffn(1, 70, B_FF1, 3)
            norm(4)
            for k in range(KT):
                pe.wait_ge(h_scaled, 8 * 4 + k + 1)
                if k >= 4:
                    pe.wait_ge(fin_copied, k - 3)
                for t in range(TT):
                    last = pe.transpose(bank[k % 4][:, t * P:(t + 1) * P],
                                        tmp[k % 2][:, t * P:(t + 1) * P], ident[:, :])
                last.then_inc(fin_t, 1)

        @block.scalar
        def _(act):
            count = [0]

            def step(ins):
                count[0] += 1
                ins.then_inc(act_step, 1)
                act.wait_ge(act_step, count[0])

            act.dma_start(vec_b[CONV:CONV + 48, :], hy_conv_w[0].rearrange("j (b p) -> (j b) p", p=P))\
               .then_inc(vec_in, 16)
            act.dma_start(vec_b[NMIX:NMIX + 16, :], norm_mix_w.rearrange("l (k p) -> (l k) p", p=P))\
               .then_inc(vec_in, 16)
            act.dma_start(vec_b[NFFN:NFFN + 16, :], norm_ffn_w.rearrange("l (k p) -> (l k) p", p=P))\
               .then_inc(vec_in, 16)
            act.dma_start(vec_b[NFIN:NFIN + 8, :], final_norm_w.rearrange("(k p) -> k p", p=P))\
               .then_inc(vec_in, 16)
            act.dma_start(vec_b[S5D:S5D + 4, :], s5_d[0].rearrange("(k p) -> k p", p=P)).then_inc(vec_in, 16)
            act.dma_start(vec_b[GLUB:GLUB + 4, :], s5_glu_b[0].rearrange("(k p) -> k p", p=P))\
               .then_inc(vec_in, 16)
            act.dma_start(vec_b[HNW:HNW + 1, :], hy_head_norm_w).then_inc(vec_in, 16)
            act.dma_start(vec_a[:, :], ada_b.rearrange("l (k p) -> (l k) p", p=P)).then_inc(vec_in, 16)
            act.dma_start(c_col[:, :], c[0].rearrange("(p t) -> p t", t=8)).then_inc(c_in, 16)
            act.dma_start(lam[:, 0, :], s5_lam_re[0].rearrange("(i two) p -> i (two p)", two=2))\
               .then_inc(lam_in, 16)
            act.dma_start(lam[:, 1, :], s5_lam_im[0].rearrange("(i two) p -> i (two p)", two=2))\
               .then_inc(lam_in, 16)
            act.dma_start(lam[:, 14, 0:2], s5_log_dt[0].rearrange("(i two) -> i two", two=2))\
               .then_inc(lam_in, 16)
            for par in range(2):
                rows = slice(64 * par, 64 * par + 64)
                for dst, src in ((b_re, s5_b_re), (b_im, s5_b_im)):
                    act.dma_start(dst[rows, :, :], src[0].rearrange("(i two) p h -> two p i h", two=2)[par])\
                       .then_inc(bc_in, 16)
            for part, src in enumerate((s5_c_re, s5_c_im)):
                rows = src[0].rearrange("(q g) h p -> (g h) q p", q=4)
                for two in range(2):
                    act.dma_start(c_raw[:, part, :, 64 * two:64 * two + 64], rows).then_inc(bc_in, 16)
            act.dma_start(w_ba[:, :, :], hy_w_in[0][:, 4 * W:4 * W + 8].rearrange("(k p) n -> p k n", p=P))\
               .then_inc(ba_in, 16)
            act.dma_start(neg_a[:, :], hy_a_log.to_broadcast([P, NH]))\
               .then_inc(gdn_in, 16)
            act.dma_start(dt_b[:, :], hy_dt_bias.to_broadcast([P, NH])).then_inc(gdn_in, 16)

            act.wait_ge(lam_in, 48)
            act.activation(lam[:, 14, 0:2], lam[:, 14, 0:2], ACT.Exp).then_inc(dt_done, 1)
            act.wait_ge(gdn_in, 32)
            act.activation(neg_a[:, :], neg_a[:, :], ACT.Exp)
            act.wait_ge(c_in, 16)
            act.activation(c_act[:, :], c_col[:, :], ACT.Silu).then_inc(c_ready, 1)
            act.wait_ge(lam_exp, 1)
            act.activation(lam[:, 10, :], lam[:, 8, :], ACT.Sin)
            act.activation(lam[:, 11, :], lam[:, 7, :], ACT.Sin).then_inc(lam_trig, 1)
            for k in range(KT):
                act.wait_ge(x_t, k + 1)
                act.activation(h[:, k, :], bank[k % 4], ACT.Copy)
                if k > 0:
                    act.wait_ge(sq_added, k)
                act.activation(sq[:, :], bank[k % 4], ACT.Square).then_inc(x_done, 1)
            act.wait_ge(c_t, 1)
            for par in range(2):
                rows = slice(64 * par, 64 * par + 64)
                for dst, b, scale in ((c_re, 4, 1.0), (nc_re, 4, -1.0), (nc_im, 5, -1.0)):
                    src = bank[b].rearrange("p (i two h) -> p i two h", two=2, h=GH)[rows, :, par, :]
                    last = act.activation(dst[rows, :, :], src, ACT.Copy, scale=scale)
            last.then_inc(c_done, 1)
            act.wait_ge(lam_t, 1)
            for dst, n0 in ((pw_re, 0), (pw_im, 8)):
                act.activation(dst[:, 1:SC + 1, :],
                               bank[3][:, 16 * n0:16 * n0 + 128].rearrange("p (k i) -> p k i", k=SC), ACT.Copy)
            act.activation(f_co[:, :, :], bank[3][:, 256:288].rearrange("p (k i) -> p k i", k=2),
                           ACT.Copy).then_inc(pw_done, 1)
            act.wait_ge(ba_in, 16)
            act.activation(w_ba_hi[:, :, :], w_ba[:, :, :], ACT.Copy).then_inc(ba_split, 1)

            def hi(n, s, width=2048, first=False):
                act.wait_ge(raw_in[s], raw_value(n))
                if not first:
                    act.wait_ge(block_done, 2 * (n - 1))
                act.activation(whi[s][:, 0:width], raw[s][:, 0:width], ACT.Copy).then_inc(hi_done, 1)

            def hi_at(n0, i, per, s, width=2048):
                act.wait_ge(raw_in[s], 32 * (n0 // 2 + 1) + 16 * per * i)
                act.wait_ge(block_done, 2 * (n0 - 1) + 2 * per * i)
                act.activation(whi[s][:, 0:width], raw[s][:, 0:width], ACT.Copy).then_inc(hi_done, 1)

            def raw_value(n):
                return 32 * (n // 2 + 1)

            def norm(n, shift):
                act.wait_ge(ss_done, n + 1)
                act.activation(rstd[:, :], bank[6][:, 0:TT], ACT.Sqrt, bias=EPS_C, scale=1.0 / D)\
                   .then_inc(sd_done, 1)
                if shift is None:
                    return
                for k in range(KT):
                    act.wait_ge(h_scaled, 8 * n + k + 1)
                    act.activation(hn_hi[:, k, :], tmp[k % 2][:, :], ACT.Identity,
                                   bias=mod[:, shift + k:shift + k + 1]).then_inc(hi_norm, 1)

            def square(value, n, m, i=None):
                at_ = m if i is None else m + 4 * i
                act.wait_ge(block_free, value)
                act.wait_ge(sq_added, 8 * n + at_)
                act.activation(sq[:, :], h[:, at_, :], ACT.Square).then_inc(sq_done, 1)

            norm(0, 0)
            hi(0, 0, first=True)
            hi(1, 1, first=True)
            for r in range(4):
                act.wait_ge(block_done, B_U + r + 1)
                act.activation(u_perm[:, r, :, :], perm(bank[r]), ACT.Copy).then_inc(block_free, 1)
                if r % 2:
                    hi(2 + r // 2, r // 2)
            for q in range(8):
                act.wait_ge(wt_t_done, q + 1)
                if q == 4:
                    act.wait_ge(u_out, 64)
                act.activation(w_in[:, q // 4, 4 * (q % 4):4 * (q % 4) + 4, :],
                               bank[4 + q % 2].rearrange("p (i m) -> p i m", i=4), ACT.Copy)\
                   .then_inc(w_done, 1)
            act.wait_ge(g_abs, 1)
            step(act.activation(g_t[0][:, :, :], g_t[0][:, :, :], ACT.Exp, scale=-1.0))
            act.activation(g_t[0][:, :, :], g_t[0][:, :, :], ACT.Ln, bias=ONE_C).then_inc(g_ln, 1)
            act.activation(beta[:, :, :], ba[:, :, 0:NH], ACT.Sigmoid).then_inc(beta_done, 1)
            act.wait_ge(m_zero, 1)
            for q in range(8):
                act.wait_ge(k_sum, q + 1)
                act.activation(m_pair[0:GH, 4 * (q // 2):4 * (q // 2) + 4, q % 2, :],
                               bank[4 + q % 2][0:GH, :].rearrange("p (g m) -> p g m", g=4), ACT.Copy)\
                   .then_inc(k_done, 1)
            act.wait_ge(gc_diff, 1)
            act.activation(gc_exp[:, :, :], gc[:, :, :], ACT.Exp)
            act.activation(k_fac[:, :, :], k_fac[:, :, :], ACT.Exp)
            act.activation(s_fac[:, :, :], s_fac[:, :, :], ACT.Exp).then_inc(gates, 1)
            for q in range(4):
                act.wait_ge(p_sum, q + 1)
                dst = (s_re, s_im)[q // 2]
                act.activation(dst[:, 8 * (q % 2):8 * (q % 2) + 8, :],
                               bank[4 + q].rearrange("p (i c) -> p i c", c=NC), ACT.Copy).then_inc(p_done, 1)
            act.preload_act_table(ACT.Silu)
            for i in range(3):
                def tap(r):
                    act.wait_ge(block_done, B_QKV + 4 * i + r + 1)
                    w3 = vb[:, CONV + 36 + r + 4 * i:CONV + 37 + r + 4 * i]
                    act.activation(conv[:, i, r, :], bank[r], ACT.Identity, scale=w3).then_inc(conv_tap, 1)

                def silu(r):
                    act.wait_ge(block_free, B_QKV + 4 * i + r + 1)
                    act.activation(conv[:, i, r, :], conv[:, i, r, :], ACT.Silu).then_inc(silu_done, 1)

                tap(0)
                tap(1)
                silu(0)
                hi_at(4, i, 2, 0)
                tap(2)
                silu(1)
                tap(3)
                silu(2)
                hi_at(5, i, 2, 1)
                silu(3)
            for q in range(4):
                act.wait_ge(y_sum, q + 1)
                act.activation(u_pair[:, 8 * (q % 2):8 * (q % 2) + 8, q // 2, :], bank[4 + q].rearrange("p (g c) -> p g c", c=NC),
                               ACT.Copy).then_inc(y_done, 1)
            for r in range(4):
                act.wait_ge(block_done, B_Z + r + 1)
                act.activation(z_act[:, r, :], bank[r], ACT.Silu).then_inc(block_free, 1)
                if r % 2:
                    hi(10 + r // 2, r // 2, 1024)

            def drain(name, hd, dst, func=ACT.Copy):
                q, b, _ = gp(name, hd)
                act.wait_ge(gdn_done, q + 1)
                act.activation(dst[:, hd, :, :], bank[b].rearrange("p (c i) -> p c i", c=TT), func)\
                   .then_inc(drained[q % 4], 1)

            for hd in range(NH):
                for w_, name in enumerate(("q", "k")):
                    q, b, _ = gp(name, hd)
                    act.wait_ge(gdn_done, q + 1)
                    if hd > 0:
                        act.wait_ge(qk_red, 2 * hd - 1 + w_)
                    act.activation(tmp[w_][:, :], bank[b], ACT.Square).then_inc(qk_sq, 1)
                    drain(name, hd, (q_tok, k_tok)[w_])
                drain("v", hd, v_tok)
            act.wait_ge(qk_red, 2 * NH)
            act.activation(qk_rn[:, :, :, :], qk_ss[:, :, :, :], ACT.Sqrt, bias=EPS_C).then_inc(qk_root, 1)
            for hd in range(NH):
                drain("kT", hd, kT)
                drain("qT", hd, qT)
                drain("bT", hd, bT)
            for hd in range(NH):
                wait_drained(act, "gr", hd)
                act.activation(dec[:, hd, :, :], dec[:, hd, :, :], ACT.Exp).then_inc(dec_exp, 1)
            for hd in range(NH):
                drain("dT", hd, qdT)
            act.wait_ge(y_du, 1)
            step(act.activation(y_s5[:, :, :, :], y_s5[:, :, :, :], ACT.Gelu_apprx_tanh))
            act.activation(ys_hi[:, :, :], y_s5[:, :, :, :].rearrange("p k j c -> p k (j c)"), ACT.Copy)\
               .then_inc(ys_hi_done, 1)
            act.wait_ge(block_done, B_GLU + 4)
            for r in range(4):
                if r >= 2:
                    act.wait_ge(glu_mul, r - 1)
                act.activation(tmp[r % 2][:, :], bank[r], ACT.Sigmoid,
                               bias=vb[:, GLUB + r:GLUB + r + 1]).then_inc(block_free, 1)
            for r in range(4):
                act.wait_ge(glu_mul, r + 1)
                act.activation(perm(ys_hi[:, r, :]), y_s5[:, r, :, :], ACT.Copy).then_inc(glu_hi, 1)
            hi(12, 0)
            hi(13, 1)
            for hd in range(NH):
                drain("d2", hd, Db)
                drain("d2t", hd, DbT)
            for hd in range(NH):
                drain("d4", hd, Da)
            for hd in range(NH):
                drain("d8t", hd, DbT)
            for hd in range(NH):
                drain("xt", hd, XT)
            for hd in range(NH):
                drain("u", hd, vn)
                drain("w", hd, wT)
            for hd in range(NH):
                act.wait_ge(o_done, hd + 1)
                if hd >= 2:
                    act.wait_ge(o_red, hd - 1)
                act.activation(tmp_o[hd % 2][:, :], bank[hd], ACT.Square).then_inc(o_sq_done, 1)
            act.wait_ge(o_red, NH)
            act.activation(o_rn[:, :, :], o_ss[:, :, :], ACT.Sqrt, bias=EPS_C, scale=1.0 / P)\
               .then_inc(o_root, 1)
            for hd in range(NH):
                act.wait_ge(oz_done, hd + 1)
                act.activation(mo_hi[:, hd, :], o_z[:, hd, :], ACT.Copy).then_inc(mo_hi_done, 1)

            def residual_blocks(unit, slot, n):
                with act.Fori(0, 2) as i:
                    for r in range(4):
                        if r % 2:
                            hi_at(slot + 2 + r // 2, i, 2, r // 2)
                        square(unit + 4 * i + r + 1, n, r, i)

            residual_blocks(B_OUT0, 12, 1)
            norm(1, 24)

            def ffn(layer, slot, unit, n):
                act.preload_act_table(ACT.Silu)
                hidden = FT * layer
                for half, n_f in enumerate(HALVES):
                    with act.Fori(0, n_f // 2) as i:
                        for s in range(2):
                            m = hidden + 2 * i + s
                            act.wait_ge(block_done, unit + 4 * i + 2 * s + 1)
                            act.activation(tmp[0][:, :], bank[2 * s], ACT.Silu).then_inc(gate_act, 1)
                            hi_at(slot + 2 + s, i, 2, s)
                            act.wait_ge(up_mul, m + 1)
                            act.activation(ff_hi[:, 2 * i + s, :], tmp[1][:, :], ACT.Copy)\
                               .then_inc(ff_hi_done, 1)
                    slot, unit, hidden = slot + n_f, unit + 2 * n_f, hidden + n_f
                    final = layer == 1 and half == 1

                    def body(i, last=False):
                        for s in range(4):
                            if not (last and s >= 2):
                                hi_at(slot + 2 + s, i, 4, s % 2, n_f * P if s < 2 else 2048)
                            if half == 1:
                                square(unit + 8 * i + 2 * s + 2, n + 1, s, i)
                    if final:
                        body(0)
                        body(1, True)
                    else:
                        with act.Fori(0, 2) as i:
                            body(i)
                    slot, unit = slot + 8, unit + 16

            ffn(0, 16, B_FF0, 1)
            act.activation(ones_r[:, :], ones[:, :], ACT.Copy)
            act.activation(tril_r[:, :], tril[:, :], ACT.Copy).then_inc(cons_r, 1)
            norm(2, 48)
            act.preload_act_table(ACT.Ln)
            with act.Fori(0, 2) as it:
                for idx in range(6):
                    pair, kind = idx // 3, idx % 3
                    unit = B_SB + 2 * idx
                    for j in range(2):
                        b = (2 * idx + j) % 4
                        act.wait_ge(block_done, unit + 12 * it + j + 1)
                        if kind < 2:
                            act.activation(sb_qk[:, kind, 2 * pair + j, :], bank[b], ACT.Copy,
                                           scale=float(P) ** -0.5 if kind == 0 else 1.0)\
                               .then_inc(block_free, 1)
                        else:
                            act.activation(sb_v[:, 2 * j:2 * j + 2, 2 * pair:2 * pair + 2, :],
                                           bank[b].rearrange("p (t h d) -> p t h d", t=2, h=2), ACT.Copy)\
                               .then_inc(block_free, 1)
                    hi_at(56 + idx, it, 6, idx % 2)

                def weights_of(hd):
                    act.wait_ge(sb_wm, 4 * it + hd + 1)
                    act.activation(w_b[:, :], w_b[:, :], ACT.Exp).then_inc(sb_p, 1)

                def out_hi(hd):
                    act.wait_ge(sb_o, 4 * it + hd + 1)
                    act.activation(ff_hi[:, 4 * it + hd, :], bank[6 + hd % 2], ACT.Copy).then_inc(sbo_hi, 1)

                for hd in range(4):
                    n = 4 * it + hd
                    act.wait_ge(sbz, n + 1)
                    act.activation(zb[hd % 2][:, :], flat[:, 0:1280], ACT.Copy).then_inc(sbz_done, 1)
                    if hd > 0:
                        weights_of(hd - 1)
                    act.wait_ge(sb_abs, n + 1)
                    act.activation(e_b[:, :], e_b[:, :], ACT.Exp).then_inc(sbe, 1)
                    act.wait_ge(sbe, n + 1)
                    act.activation(e_b[:, :], e_b[:, :], ACT.Ln, bias=ONE_C).then_inc(sb_spe, 1)
                    act.wait_ge(sb_mask, n + 1)
                    if hd > 0:
                        act.wait_ge(sb_c, n)
                    act.activation(sp_hi[:, :], e_b[:, :], ACT.Copy).then_inc(sb_hi, 1)
                    if hd > 0:
                        out_hi(hd - 1)
                weights_of(3)
                out_hi(3)
            residual_blocks(B_OUT1, 66, 3)
            norm(3, 72)
            ffn(1, 70, B_FF1, 3)
            norm(4, None)
            for k in range(KT):
                act.wait_ge(fin_t, k + 1)
                act.activation(out_tok[:, :, k * P:(k + 1) * P],
                               bank[k % 4].rearrange("p (t f) -> p t f", t=TT), ACT.Copy)\
                   .then_inc(fin_copied, 1)

        @block.vector
        def _(dve):
            count = [0]
            ahead = [None]

            def step(ins):
                count[0] += 1
                ins.then_inc(dve_step, 1)
                dve.wait_ge(dve_step, count[0] if ahead[0] is None else count[0] + ahead[0])

            TTO, TS, STT = dve.tensor_tensor, dve.tensor_scalar, dve.scalar_tensor_tensor
            MUL, ADD, SUB, MAX, MIN = ALU.mult, ALU.add, ALU.subtract, ALU.max, ALU.min

            dve.wait_ge(vec_t, 1)
            dve.tensor_copy(ada_bias[:, :], bank[7][:, 96:192])
            dve.tensor_copy(vb[:, :], bank[7][:, 192:289]).then_inc(vec_ready, 1)
            dve.memset(sq_sum[:, :], 0.0).then_inc(dve_step, 1)
            count[0] += 1

            def L(i, n=1):
                return lam[:, i, :] if n == 1 else lam[:, i:i + n, :]

            dve.wait_ge(dt_done, 1)
            dt_bc = lam[:, 14, 0:2].unsqueeze(2).to_broadcast([16, 2, GP])
            for src, dst in ((0, 2), (1, 3)):
                step(TTO(L(dst).rearrange("i (two p) -> i two p", two=2),
                         L(src).rearrange("i (two p) -> i two p", two=2), dt_bc, MUL))
            step(TS(L(2), L(2), -87.0, 87.0, MAX, MIN))
            step(TS(L(4), L(2), 1.0 / float(np.log(2)), ROUND, MUL, ADD))
            step(TS(L(4), L(4), ROUND, None, SUB))
            step(STT(L(5), L(4), -LN2_1, L(2), MUL, ADD))
            step(STT(L(5), L(4), -LN2_2, L(5), MUL, ADD))
            step(TS(L(6), L(5), 1.0 / 7, 1.0, MUL, ADD))
            for n in range(6, 0, -1):
                step(STT(L(6), L(6), 1.0 / n, L(5), MUL, MUL))
                step(TS(L(6), L(6), 1.0, None, ADD))
            step(TS(L(7).bitcast(I32), L(4), 127.0, 8388608.0, ADD, MUL))
            step(TTO(L(6), L(6), L(7), MUL))
            step(TS(L(4), L(3), 1.0 / TWO_PI, ROUND, MUL, ADD))
            step(TS(L(4), L(4), ROUND, None, SUB))
            step(STT(L(5), L(4), -PI_1, L(3), MUL, ADD))
            step(STT(L(5), L(4), -PI_2, L(5), MUL, ADD))
            step(STT(L(5), L(4), -PI_3, L(5), MUL, ADD))
            step(TS(L(8), L(5), -PI_BELOW, PI_BELOW, MAX, MIN))
            step(TS(L(7), L(5), float(np.pi / 2), None, ADD))
            step(TS(L(9), L(7), PI_BELOW, TWO_PI, ALU.is_gt, MUL))
            step(TTO(L(7), L(7), L(9), SUB))
            TS(L(7), L(7), -PI_BELOW, PI_BELOW, MAX, MIN).then_inc(lam_exp, 1)
            step(TTO(L(9), L(0), L(0), MUL))
            step(TTO(L(4), L(1), L(1), MUL))
            step(TTO(L(9), L(9), L(4), ADD))
            step(dve.reciprocal(L(9), L(9)))
            dve.wait_ge(lam_trig, 1)
            step(TTO(L(16), L(6), L(11), MUL))
            step(TTO(L(24), L(6), L(10), MUL))
            step(TS(L(5), L(16), 1.0, None, SUB))
            step(TTO(L(7), L(5), L(0), MUL))
            step(TTO(L(8), L(24), L(1), MUL))
            step(TTO(L(7), L(7), L(8), ADD))
            step(TTO(L(12), L(7), L(9), MUL))
            step(TTO(L(7), L(24), L(0), MUL))
            step(TTO(L(8), L(5), L(1), MUL))
            step(TTO(L(7), L(7), L(8), SUB))
            step(TTO(L(13), L(7), L(9), MUL))

            for src, by, dst, n in ((0, 0, 1, 1), (0, 1, 2, 2), (0, 3, 4, 4)):
                ar, ai = lam[:, 16 + src:16 + src + n, :], lam[:, 24 + src:24 + src + n, :]
                br = lam[:, 16 + by:17 + by, :].to_broadcast([16, n, P])
                bi = lam[:, 24 + by:25 + by, :].to_broadcast([16, n, P])
                dr, di = lam[:, 16 + dst:16 + dst + n, :], lam[:, 24 + dst:24 + dst + n, :]
                t0 = lam[:, 0:n, :]
                step(TTO(t0, ai, bi, MUL))
                step(TTO(dr, ar, br, MUL))
                step(TTO(dr, dr, t0, SUB))
                step(TTO(t0, ai, br, MUL))
                step(TTO(di, ar, bi, MUL))
                last = TTO(di, di, t0, ADD)
                if n < 4:
                    step(last)
            last.then_inc(lam_done, 1)

            def ada0_tile(part, t):
                n = 8 * part + t
                acc = ada0_acc[part % 2]
                if n == 0:
                    dve.wait_ge(c_ready, 1)
                if t == 0 and part % 2 == 0 and part > 0:
                    dve.wait_ge(mod_sum, part // 2)
                dve.wait_ge(ada0_ld[n % 2], 16 * (n // 2 + 1))
                if t == 0:
                    TS(acc[:, :], ada0_in[n % 2][:, :], c_act[:, t:t + 1], None, MUL).then_inc(ada_used, 1)
                else:
                    dve.wait_ge(ada_used, n)
                    STT(acc[:, :], ada0_in[n % 2][:, :], c_act[:, t:t + 1], acc[:, :], MUL, ADD)\
                        .then_inc(ada_used, 1)

            def mod_parts(n, part, parts=2):
                dve.wait_ge(mod_sum, n + 1)
                c_ = slice(8 * part, 8 * (part + parts))
                TTO(mod[:, c_], bank[7][:, c_], ada_bias[:, c_], ADD).then_inc(mod_done, 1)

            def add_square(n, k):
                dve.wait_ge(sq_done if n else x_done, (8 * (n - 1) + k + 1) if n else k + 1)
                TTO(sq_sum[:, :], sq_sum[:, :], sq[:, :], ADD).then_inc(sq_added, 1)

            for k in range(KT):
                add_square(0, k)
            for part in range(2):
                for t in range(8):
                    ada0_tile(part, t)
            dve.wait_ge(pw_done, 1)
            dve.wait_ge(bc_in, 16 * 8)
            f_re = f_co[:, 0, :].unsqueeze(2).to_broadcast([P, PAIRS, GH])
            f_im = f_co[:, 1, :].unsqueeze(2).to_broadcast([P, PAIRS, GH])
            t0 = bb_t[:, :, :]
            step(TTO(t0, b_im[:, :, :], f_im, MUL))
            step(TTO(bb_re[:, :, :], b_re[:, :, :], f_re, MUL))
            step(TTO(bb_re[:, :, :], bb_re[:, :, :], t0, SUB))
            step(TTO(t0, b_re[:, :, :], f_im, MUL))
            step(TTO(bb_im[:, :, :], b_im[:, :, :], f_re, MUL))
            TTO(bb_im[:, :, :], bb_im[:, :, :], t0, ADD).then_inc(bb_done, 1)
            mod_parts(0, 0)
            dve.wait_ge(ba_split, 1)
            TTO(w_ba_lo[:, :, :], w_ba[:, :, :], w_ba_hi[:, :, :].bitcast(F32), SUB).then_inc(ba_split, 1)

            def lo(n, s, width=2048):
                dve.wait_ge(hi_done, n + 1)
                TTO(wlo[s][:, 0:width], raw[s][:, 0:width], whi[s][:, 0:width].bitcast(F32), SUB)\
                    .then_inc(lo_done, 1)

            def norm(n, scale_w, shift):
                if shift is not None:
                    dve.wait_ge(mod_done, (1, 3, 4, 5)[n])
                    step(STT(n_scale[:, :], mod[:, shift + 8:shift + 16], 1.0, vb[:, scale_w:scale_w + 8],
                             ADD, MUL))
                dve.wait_ge(sd_done, n + 1)
                step(dve.reciprocal(rstd[:, :], rstd[:, :]))
                for c_ in range(TT):
                    last = TS(diag[:, c_, :], ident[:, :], rstd[:, c_:c_ + 1], None, MUL)
                last.then_inc(diag_done, 1)
                if n < 4:
                    dve.memset(sq_sum[:, :], 0.0)
                dve.wait_ge(rb_done, n + 1)

                def scaled(k):
                    if n == 4:
                        if k >= 2:
                            dve.wait_ge(fin_t, k - 1)
                        w_ = vb[:, scale_w + k:scale_w + k + 1]
                    else:
                        if k >= 2:
                            dve.wait_ge(hn_done, 8 * n + k - 1)
                        w_ = n_scale[:, k:k + 1]
                    STT(tmp[k % 2][:, :], h[:, k, :], w_, bank[6], MUL, MUL).then_inc(h_scaled, 1)

                def rest(k):
                    dve.wait_ge(hi_norm, 8 * n + k + 1)
                    STT(hn_lo[:, k, :], tmp[k % 2][:, :], mod[:, shift + k:shift + k + 1],
                        hn_hi[:, k, :].bitcast(F32), ADD, SUB).then_inc(hn_done, 1)

                for k in range(KT):
                    scaled(k)
                    if n < 4 and k >= 1:
                        rest(k - 1)
                if n < 4:
                    rest(KT - 1)

            norm(0, NMIX, 0)
            lo(0, 0)
            lo(1, 1)
            pr = pw_re[:, 0:SC, :][:, ::-1, :].rearrange("p k i -> p i k")
            pi = pw_im[:, 0:SC, :][:, ::-1, :].rearrange("p k i -> p i k")
            dve.wait_ge(c_t, 1)
            dve.wait_ge(pw0_done, 1)
            dve.wait_ge(bb_done, 1)
            for part, (a_, b_, dst, op) in enumerate(((pr, pi, wt_re, SUB), (pi, pr, wt_im, ADD))):
                if part:
                    dve.wait_ge(wt_done, 1)
                for half in range(2):
                    ii = slice(8 * half, 8 * half + 8)

                    def b4(x_):
                        return x_[:, ii, :].unsqueeze(2).to_broadcast([P, 8, SC, GH])

                    def p4(x_):
                        return x_[:, ii, :].unsqueeze(3).to_broadcast([P, 8, SC, GH])

                    d_ = dst[:, ii, :, :]
                    t_ = wt_t[:, :].rearrange("p (i j h) -> p i j h", i=8, j=SC)
                    step(TTO(t_, b4(bb_im), p4(b_), MUL))
                    step(TTO(d_, b4(bb_re), p4(a_), MUL))
                    last = TTO(d_, d_, t_, op)
                    if half == 0:
                        step(last)
                last.then_inc(wt_done, 1)
            lo(2, 0)
            dve.wait_ge(ba_sum, 1)
            step(dve.tensor_copy(ba[:, :, :], bank[7][:, 300:332].rearrange("p (c n) -> p c n", c=TT)))
            dve.wait_ge(gdn_in, 32)
            a4 = ba[:, :, NH:2 * NH]
            step(TTO(a4, a4, dt_b[:, :].unsqueeze(1).to_broadcast([P, TT, NH]), ADD))
            step(TS(g_t[0][:, :, :], a4, -1.0, None, MUL))
            TTO(g_t[0][:, :, :], g_t[0][:, :, :], a4, MAX).then_inc(g_abs, 1)
            lo(3, 1)
            dve.wait_ge(g_ln, 1)
            step(STT(g_t[1][:, :, :], a4, 0.0, g_t[0][:, :, :], MAX, ADD))
            STT(g_log[:, :, :], g_t[1][:, :, :], -1.0,
                neg_a[:, :].unsqueeze(1).to_broadcast([P, TT, NH]), MUL, MUL).then_inc(g_done, 1)
            for t in range(8):
                ada0_tile(2, t)
            dve.wait_ge(gc_sum, 1)
            step(dve.tensor_copy(gc[:, :, :], bank[7][:, 340:356].rearrange("p (c n) -> p c n", c=TT)))
            dve.tensor_copy(s_fac[:, :, :], bank[7][:, 356:372].rearrange("p (c n) -> p c n", c=TT))
            TTO(k_fac[:, :, :], bank[7][:, 356:372].rearrange("p (c n) -> p c n", c=TT), gc[:, :, :], SUB)\
                .then_inc(gc_diff, 1)
            for t in range(8):
                ada0_tile(3, t)
            mod_parts(1, 2)
            for i in range(3):
                for r in range(4):
                    dve.wait_ge(conv_tap, 4 * i + r + 1)
                    for s in range(1, 4):
                        w_ = CONV + 12 * (3 - s) + 4 * i + r
                        d_ = conv[:, i, r, s:T]
                        last = STT(d_, bank[r][:, 0:T - s], vb[:, w_:w_ + 1], d_, MUL, ADD)
                        if s < 3:
                            step(last)
                    last.then_inc(block_free, 1)
                    if r == 1:
                        lo(4 + 2 * i, 0)
                    if r == 3:
                        lo(5 + 2 * i, 1)
                    if i < 2:
                        ada0_tile(4 + i, 2 * r)
                        ada0_tile(4 + i, 2 * r + 1)
            lo(10, 0, 1024)
            lo(11, 1, 1024)
            mod_parts(2, 4)

            def product(name, hd):
                q, b, _ = gp(name, hd)
                dve.wait_ge(gdn_done, q + 1)
                return bank[b].rearrange("p (c i) -> p c i", c=TT), drained[q % 4]

            for hd in range(NH):
                for w_ in range(2):
                    dve.wait_ge(qk_sq, 2 * hd + w_ + 1)
                    dve.tensor_reduce(qk_ss[:, w_, hd, :], tmp[w_][:, :].rearrange("p (c i) -> p c i", c=TT),
                                      AX.X, ADD).then_inc(qk_red, 1)
            dve.wait_ge(qk_root, 1)
            step(dve.reciprocal(qk_rn[:, :, :, :], qk_rn[:, :, :, :]))
            step(TS(qk_rn[:, 0, :, :], qk_rn[:, 0, :, :], float(P) ** -0.5, None, MUL))

            def col(t_, hd):
                return bc(t_[:, :, hd], P)

            dve.wait_ge(gates, 1)
            dve.wait_ge(beta_done, 1)
            for hd in range(NH):
                wait_drained(dve, "v", hd)
                TTO(k_tok[:, hd, :, :], k_tok[:, hd, :, :], bc(qk_rn[:, 1, hd, :], P), MUL).then_inc(kn_done, 1)
                TTO(q_tok[:, hd, :, :], q_tok[:, hd, :, :], bc(qk_rn[:, 0, hd, :], P), MUL).then_inc(qn_done, 1)
                dve.wait_ge(kn_done, hd + 1)
                TTO(kb_tok[:, hd, :, :], k_tok[:, hd, :, :], col(beta, hd), MUL).then_inc(kb_done, 1)
                TTO(v_tok[:, hd, :, :], v_tok[:, hd, :, :], col(beta, hd), MUL).then_inc(rv_done, 1)
            for hd in range(NH):
                src, free = product("gr", hd)
                dve.wait_ge(kd_done, hd + 1)
                wait_drained(dve, "kT", hd)
                for c_ in range(TT):
                    last = TS(dec[:, hd, c_, :], src[:, c_, :], gc[:, c_, hd:hd + 1], 0.0, SUB, MIN)
                last.then_inc(free, 1)
            for name, done, dst in (("at", dec_done, attnT), ("lt", dec_done, LT)):
                for hd in range(NH):
                    src, free = product(name, hd)
                    dve.wait_ge(done, hd + 1)
                    TTO(dst[:, hd, :, :], src, dec[:, hd, :, :], MUL).then_inc(free, 1)
            dve.wait_ge(y_in, 64)
            dve.wait_ge(u2_in, 64)
            for r in range(4):
                last = STT(y_s5[:, r, :, :], u_again[:, r, :, :], vb[:, S5D + r:S5D + r + 1],
                           y_s5[:, r, :, :], MUL, ADD)
            last.then_inc(y_du, 1)
            dve.wait_ge(ys_hi_done, 1)
            TTO(ys_lo[:, :, :], y_s5[:, :, :, :].rearrange("p k j c -> p k (j c)"),
                ys_hi[:, :, :].bitcast(F32), SUB).then_inc(ys_done, 1)
            for r in range(4):
                dve.wait_ge(block_free, B_GLU + r + 1)
                TTO(y_s5[:, r, :, :], y_s5[:, r, :, :], tmp[r % 2][:, :].rearrange("p (j c) -> p j c", j=SC),
                    MUL).then_inc(glu_mul, 1)
            for r in range(4):
                dve.wait_ge(glu_hi, r + 1)
                TTO(perm(ys_lo[:, r, :]), y_s5[:, r, :, :], perm(ys_hi[:, r, :].bitcast(F32)), SUB)\
                    .then_inc(mix_s5, 1)
            lo(12, 0)
            lo(13, 1)
            for hd in range(NH):
                src, free = product("l", hd)
                TTO(Da[:, hd, :, :], src, bd16[:, :].unsqueeze(1).to_broadcast([P, TT, P]), MUL)\
                    .then_inc(free, 1)
                wait_drained(dve, "l", hd)
                TTO(X[:, hd, :, :], ident[:, :].unsqueeze(1).to_broadcast([P, TT, P]), Da[:, hd, :, :], SUB)\
                    .then_inc(x0_done, 1)

            def onto(name, dst, op):
                for hd in range(NH):
                    src, free = product(name, hd)
                    TTO(dst[:, hd, :, :], dst[:, hd, :, :], src, op).then_inc(free, 1)

            onto("x1", X, ADD)
            for hd in range(NH):
                src, free = product("d4t", hd)
                dve.tensor_copy(DaT[:, hd, :, :], src).then_inc(free, 1)
            onto("x2", X, ADD)
            onto("x3", X, ADD)
            for lv in range(3):
                for hd in range(NH):
                    src, free = product(f"z{lv}", hd)
                    TTO(Z[:, hd, :, :], src, level[lv][:, :].unsqueeze(1).to_broadcast([P, TT, P]), MUL)\
                        .then_inc(free, 1)
                if lv < 2:
                    onto(f"xc{lv}", X, SUB)
                onto(f"xtc{lv}", XT, SUB)
            for c_ in range(TT):
                if c_ > 0:
                    for hd in range(NH):
                        q, b, _ = gp(f"ws{c_}", hd)
                        dve.wait_ge(gdn_done, q + 1)
                        TTO(vn[:, hd, c_, :], vn[:, hd, c_, :], bank[b][:, 0:P], SUB).then_inc(drained[q % 4], 1)
                if c_ < TT - 1:
                    for hd in range(NH):
                        q, b, _ = gp(f"s{c_}", hd)
                        dve.wait_ge(gdn_done, q + 1)
                        if c_ == 0:
                            dve.tensor_copy(S[:, hd, :], bank[b][:, 0:P]).then_inc(drained[q % 4], 1)
                        else:
                            STT(S[:, hd, :], S[:, hd, :], s_fac[:, c_, hd:hd + 1], bank[b][:, 0:P], MUL, ADD)\
                                .then_inc(drained[q % 4], 1)
            for hd in range(NH):
                dve.wait_ge(o_sq_done, hd + 1)
                dve.tensor_reduce(o_ss[:, hd, :], tmp_o[hd % 2][:, :].rearrange("p (c i) -> p c i", c=TT),
                                  AX.X, ADD).then_inc(o_red, 1)
            dve.wait_ge(o_root, 1)
            step(dve.reciprocal(o_rn[:, :, :], o_rn[:, :, :]))
            for hd in range(NH):
                TTO(o_n[:, hd, :, :], bank[hd].rearrange("p (c i) -> p c i", c=TT), bc(o_rn[:, hd, :], P), MUL)\
                    .then_inc(on_done, 1)
            for hd in range(NH):
                q, b, _ = gp("oT", hd)
                dve.wait_ge(gdn_done, q + 1)
                STT(o_z[:, hd, :], bank[b], vb[:, HNW:HNW + 1], z_act[:, hd, :], MUL, MUL).then_inc(oz_done, 1)
            for hd in range(NH):
                dve.wait_ge(mo_hi_done, hd + 1)
                TTO(mo_lo[:, hd, :], o_z[:, hd, :], mo_hi[:, hd, :].bitcast(F32), SUB).then_inc(mo_done, 1)

            def residual(value, b, gate, m, units=1):
                dve.wait_ge(block_done, value)
                STT(h[:, m, :], bank[b], mod[:, bass.ds(gate + m, 1)], h[:, m, :], MUL, ADD)\
                    .then_inc(block_free, units)

            def residual_blocks(unit, slot, n, gate):
                with dve.Fori(0, 2) as i:
                    for r in range(4):
                        m = 4 * i + r
                        residual(unit + 4 * i + r + 1, r, gate, m)
                        if r % 2:
                            lo(slot + 2 + r // 2 + 2 * i, r // 2)
                        add_square(n, m)

            residual_blocks(B_OUT0, 12, 1, 16)
            norm(1, NFFN, 24)

            def ffn(layer, slot, unit, n, gate):
                hidden = FT * layer
                for half, n_f in enumerate(HALVES):
                    with dve.Fori(0, n_f // 2) as i:
                        for s in range(2):
                            m = hidden + 2 * i + s
                            dve.wait_ge(block_done, unit + 4 * i + 2 * s + 2)
                            dve.wait_ge(gate_act, m + 1)
                            dve.wait_ge(block_free, unit + 4 * i + 2 * s)
                            TTO(tmp[1][:, :], tmp[0][:, :], bank[2 * s + 1], MUL).then_inc(up_mul, 1)
                            lo(slot + 2 + 2 * i + s, s)
                            dve.wait_ge(ff_hi_done, m + 1)
                            TTO(ff_lo[:, 2 * i + s, :], tmp[1][:, :], ff_hi[:, 2 * i + s, :].bitcast(F32), SUB)\
                                .then_inc(block_free, 2)
                    slot, unit, hidden = slot + n_f, unit + 2 * n_f, hidden + n_f
                    if layer == 0:
                        if half == 1:
                            dve.wait_ge(mod_sum, 4)
                        step(dve.memset(ada1_acc[:, :], 0.0))

                    def body(i, last=False):
                        for s in range(4):
                            m = 4 * i + s
                            residual(unit + 8 * i + 2 * s + 2, s, gate, m, units=2)
                            if not (last and s >= 2):
                                lo(slot + 2 + s + 4 * i, s % 2, n_f * P if s < 2 else 2048)
                            if layer == 0:
                                dve.wait_ge(ada1_ld[s % 2], 16 * (4 * half + s // 2 + 1) + 32 * i)
                                dve.wait_ge(ada_used, 48 + 8 * half + s + 4 * i)
                                STT(ada1_acc[:, :], ada1_in[s % 2][:, :], c_act[:, bass.ds(s + 4 * i, 1)],
                                    ada1_acc[:, :], MUL, ADD).then_inc(ada_used, 1)
                            if half == 1:
                                add_square(n + 1, m)
                    if layer == 1 and half == 1:
                        body(0)
                        body(1, True)
                    else:
                        with dve.Fori(0, 2) as i:
                            body(i)
                    slot, unit = slot + 8, unit + 16
                    if layer == 0:
                        mod_parts(3 + half, 6 + 3 * half, 3)

            ffn(0, 16, B_FF0, 1, 40)
            norm(2, NMIX + 8, 48)
            with dve.Fori(0, 2) as it:
                for idx in range(6):
                    lo(56 + idx + 6 * it, idx % 2)

                def exponents(hd):
                    dve.wait_ge(sb_c, 4 * it + hd + 1)
                    if hd > 0:
                        dve.wait_ge(sb_o, 4 * it + hd)
                    TTO(w_b[:, :], zb[hd % 2][:, :], flat[:, 3 * T:3 * T + 1280], SUB).then_inc(sb_w, 1)

                def out_lo(hd):
                    dve.wait_ge(sbo_hi, 4 * it + hd + 1)
                    TTO(ff_lo[:, 4 * it + hd, :], bank[6 + hd % 2], ff_hi[:, 4 * it + hd, :].bitcast(F32), SUB)\
                        .then_inc(sbo_done, 1)

                for hd in range(4):
                    n = 4 * it + hd
                    dve.wait_ge(sbz_done, n + 1)
                    STT(e_b[:, :], zb[hd % 2][:, :], -1.0, zb[hd % 2][:, :], MUL, MIN).then_inc(sb_abs, 1)
                    if hd > 0:
                        exponents(hd - 1)
                    dve.wait_ge(sb_spe, n + 1)
                    STT(e_b[:, :], zb[hd % 2][:, :], 0.0, e_b[:, :], MAX, ADD).then_inc(sb_sp, 1)
                    dve.wait_ge(sb_hi, n + 1)
                    TTO(sp_lo[:, :], e_b[:, :], sp_hi[:, :].bitcast(F32), SUB).then_inc(sb_lo, 1)
                    if hd > 0:
                        out_lo(hd - 1)
                    dve.wait_ge(sb_lo, n + 1)
                exponents(3)
                out_lo(3)
            residual_blocks(B_OUT1, 66, 3, 64)
            norm(3, NFFN + 8, 72)
            ffn(1, 70, B_FF1, 3, 88)
            norm(4, NFIN, None)

        @block.gpsimd
        def _(pool):
            count = [0]

            def step(ins, extra=None):
                count[0] += 1
                ins.then_inc(pool_step, 1)
                pool.wait_ge(pool_step, count[0] if extra is None else count[0] + extra)

            MUL, ADD, SUB = ALU.mult, ALU.add, ALU.subtract

            def select(ap, pattern, start, mult, op=ALU.is_ge, fill=0.0):
                return pool.affine_select(out=ap, in_=ap, compare_op=op, fill=fill, base=start,
                                          pattern=pattern, channel_multiplier=mult)

            pool.memset(EPS_C, EPS)
            pool.memset(ONE_C, 1.0)
            pool.memset(ones[:, :], 1.0)
            step(pool.memset(ident[:, :], 0.0))
            select(ident[:, :], [[-1, P]], 0, 1, ALU.not_equal, 1.0).then_inc(consts, 1)
            for m_ in (triu, strict, tril, bd16, level[0], level[1]):
                last = pool.memset(m_[:, :], 1.0)
            step(last)
            select(triu[:, :], [[1, P]], 0, -1)
            select(strict[:, :], [[1, P]], -1, -1)
            select(tril[:, :], [[-1, P]], 0, 1)
            for m_, w_ in ((bd16, 16), (level[0], 32), (level[1], 64)):
                v = m_[:, :].rearrange("p (b x) -> p b x", x=w_)
                step(select(v, [[-w_, P // w_], [0, w_]], 0, 1))
                step(select(v, [[w_, P // w_], [0, w_]], w_ - 1, -1))
            step(pool.tensor_tensor(level[2][:, :], ones[:, :], level[1][:, :], SUB))
            step(pool.tensor_tensor(level[1][:, :], level[1][:, :], level[0][:, :], SUB))
            step(pool.tensor_tensor(level[0][:, :], level[0][:, :], bd16[:, :], SUB))
            pool.memset(pw_re[:, 0, :], 1.0)
            pool.memset(pw_im[:, 0, :], 0.0).then_inc(pw0_done, 1)
            pool.wait_ge(pw0_done, 1)
            pool.wait_ge(c_done, 1)
            pool.wait_ge(pw_done, 1)

            def c4(x_):
                return x_[:, :, :].unsqueeze(2).to_broadcast([P, PAIRS, SC + 1, GH])

            def p4(x_):
                return x_[:, :, :].rearrange("p k i -> p i k").unsqueeze(3).to_broadcast([P, PAIRS, SC + 1, GH])

            t_ = v_t[:, :, :, :]
            for dst, a_, b_ in ((v_re, c_re, nc_im), (v_im, nc_im, nc_re)):
                d_ = dst[:, :, :, :]
                pool.tensor_tensor(t_, c4(b_), p4(pw_im), MUL)
                step(pool.tensor_tensor(d_, c4(a_), p4(pw_re), MUL))
                last = pool.tensor_tensor(d_, d_, t_, ADD)
                if dst is v_re:
                    step(last)
            last.then_inc(v_done, 1)
            pool.wait_ge(v_done, 1)
            pool.memset(m_in[:, :, :], 0.0).then_inc(m_zero, 1)
            pool.tensor_copy(q_pw[:, 0, 0, :], pw_re[:, SC, :])
            step(pool.tensor_copy(q_pw[:, 1, 0, :], pw_im[:, SC, :]))
            q_t = g_tq[:, :, :]
            for src, by, dst, n in ((0, 0, 1, 1), (0, 1, 2, 2), (0, 3, 4, 4)):
                ar, ai = q_pw[:, 0, src:src + n, :], q_pw[:, 1, src:src + n, :]
                br = q_pw[:, 0, by:by + 1, :].to_broadcast([P, n, PAIRS])
                bi = q_pw[:, 1, by:by + 1, :].to_broadcast([P, n, PAIRS])
                dr, di = q_pw[:, 0, dst:dst + n, :], q_pw[:, 1, dst:dst + n, :]
                step(pool.tensor_tensor(q_t[:, 0:n, :], ai, bi, MUL))
                step(pool.tensor_tensor(dr, ar, br, MUL))
                step(pool.tensor_tensor(dr, dr, q_t[:, 0:n, :], SUB))
                step(pool.tensor_tensor(q_t[:, 0:n, :], ai, br, MUL))
                step(pool.tensor_tensor(di, ar, bi, MUL))
                step(pool.tensor_tensor(di, di, q_t[:, 0:n, :], ADD))

            pool.wait_ge(p_done, 4)
            pool.wait_ge(c_t, 1)
            xr = s_re[:, :, :].rearrange("p i (b s) -> p i b s", s=8)
            xi = s_im[:, :, :].rearrange("p i (b s) -> p i b s", s=8)

            def advance(dr, di, sr, si, cr, ci, shape, extra=None):
                n = int(np.prod(shape))
                ta, tb = ((t0_[:, 0:n] if len(shape) == 1 else t0_[:, 0:n].rearrange(
                    *(("p (i b) -> p i b",) if len(shape) == 2 else ("p (i b s) -> p i b s",)),
                    **(dict(i=shape[0]) if len(shape) == 2 else dict(i=shape[0], b=shape[1]))))
                    for t0_ in (scan_a, scan_b))
                tt = pool.tensor_tensor
                tt(ta, sr, cr, MUL)
                step(tt(tb, si, ci, MUL), extra)
                step(tt(ta, ta, tb, SUB), extra)
                tt(dr, dr, ta, ADD)
                step(tt(tb, si, cr, MUL), extra)
                step(tt(ta, sr, ci, MUL), extra)
                step(tt(ta, ta, tb, ADD), extra)
                last = tt(di, di, ta, ADD)
                if n == 784:
                    last.then_inc(scan_done, 1)
                else:
                    step(last, extra)

            c1r = q_pw[:, 0, 0, :].unsqueeze(2).to_broadcast([P, PAIRS, 8])
            c1i = q_pw[:, 1, 0, :].unsqueeze(2).to_broadcast([P, PAIRS, 8])
            for s in range(1, 8):
                advance(xr[:, :, :, s], xi[:, :, :, s], xr[:, :, :, s - 1], xi[:, :, :, s - 1],
                        c1r, c1i, (PAIRS, 8))
            for b in range(1, 8):
                advance(xr[:, :, b, 7], xi[:, :, b, 7], xr[:, :, b - 1, 7], xi[:, :, b - 1, 7],
                        q_pw[:, 0, 7, :], q_pw[:, 1, 7, :], (PAIRS,))
            shape4 = [P, PAIRS, 7, 7]
            advance(xr[:, :, 1:8, 0:7], xi[:, :, 1:8, 0:7],
                    xr[:, :, 0:7, 7].unsqueeze(3).to_broadcast(shape4),
                    xi[:, :, 0:7, 7].unsqueeze(3).to_broadcast(shape4),
                    q_pw[:, 0, 0:7, :].rearrange("p s i -> p i s").unsqueeze(2).to_broadcast(shape4),
                    q_pw[:, 1, 0:7, :].rearrange("p s i -> p i s").unsqueeze(2).to_broadcast(shape4),
                    (PAIRS, 7, 7))

            pool.wait_ge(gates, 1)
            for hd in range(NH):
                pool.wait_ge(qn_done, hd + 1)
                pool.tensor_tensor(kd_tok[:, hd, :, :], k_tok[:, hd, :, :], bc(k_fac[:, :, hd], P), MUL)\
                    .then_inc(kd_done, 1)
                pool.tensor_tensor(qd_tok[:, hd, :, :], q_tok[:, hd, :, :], bc(gc_exp[:, :, hd], P), MUL)\
                    .then_inc(qd_done, 1)
                pool.wait_ge(kb_done, hd + 1)
                pool.tensor_tensor(rk_tok[:, hd, :, :], kb_tok[:, hd, :, :], bc(gc_exp[:, :, hd], P), MUL)\
                    .then_inc(rk_done, 1)
            for hd in range(NH):
                pool.wait_ge(dec_exp, hd + 1)
                select(dec[:, hd, :, :], [[0, TT], [1, P]], 0, -1).then_inc(dec_done, 1)
            for hd in range(NH):
                wait_drained(pool, "lt", hd)
                select(LT[:, hd, :, :], [[0, TT], [1, P]], -1, -1).then_inc(lt_done, 1)
                wait_drained(pool, "dT", hd)
                pool.wait_ge(lt_done, hd + 1)
                pool.tensor_tensor(DaT[:, hd, :, :], LT[:, hd, :, :],
                                   bd16[:, :].unsqueeze(1).to_broadcast([P, TT, P]), MUL).then_inc(dat_done, 1)
            off = (0, 512, 1024, 896)
            pool.wait_ge(cons_r, 1)
            step(pool.memset(below[:, :], 0.0))
            select(below[:, :], [[1, P]], -1, -1, fill=-1e30).then_inc(below_done, 1)
            pool.wait_ge(below_done, 1)
            with pool.Fori(0, 2) as it:
                for hd in range(5):
                    if hd > 0:
                        pool.wait_ge(sb_w, 4 * it + hd)
                        for i in range(TT):
                            d_ = w_b[:, off[i]:off[i] + P]
                            last = pool.tensor_tensor(d_, d_, below[:, :], ADD)
                        last.then_inc(sb_wm, 1)
                    if hd < 4:
                        pool.wait_ge(sb_sp, 4 * it + hd + 1)
                        for i in range(TT):
                            d_ = e_b[:, off[i]:off[i] + P]
                            last = pool.tensor_tensor(d_, d_, strict[:, :], MUL)
                        last.then_inc(sb_mask, 1)


_INS = ["x", "c", "ada_w", "ada_b", "norm_mix_w", "norm_ffn_w", "ffn_w_in", "ffn_w_out", "hy_w_in",
        "hy_conv_w", "hy_a_log", "hy_dt_bias", "hy_head_norm_w", "s5_lam_re", "s5_lam_im",
        "s5_log_dt", "s5_b_re", "s5_b_im", "s5_c_re", "s5_c_im", "s5_d", "s5_glu_w", "s5_glu_b",
        "hy_w_out", "sb_w_in", "sb_w_out", "final_norm_w"]


def kernel(**inputs):
    import concourse.bacc as bacc
    from concourse.bass_utils import run_bass_kernel_spmd

    nc = bacc.Bacc("TRN2", target_bir_lowering=False, num_devices=1)
    arrays, args = {}, []
    for name in _INS:
        v = np.ascontiguousarray(inputs[name])
        arrays[f"in_{name}_dram"] = v
        args.append(nc.dram_tensor(f"in_{name}_dram", v.shape, mybir.dt.from_np(v.dtype),
                                   kind="ExternalInput").ap())
    args.append(nc.dram_tensor("out_0_dram", (1, T, D), F32, kind="ExternalOutput").ap())
    trunk(nc, *args)
    r = run_bass_kernel_spmd(nc, [arrays], core_ids=[0])
    return r.results[0]["out_0_dram"]
```

```python
from contextlib import ExitStack

import numpy as np

import concourse.bass as bass
from concourse import mybir

F32 = mybir.dt.float32
F32R = mybir.dt.float32r
I32 = mybir.dt.int32
ALU = mybir.AluOpType
ACT = mybir.ActivationFunctionType
AX = mybir.AxisListType

P = 128
T = 512
D = 1024
KT = D // P
TT = T // P
F = 2816
W = 512
NH = 4
EPS = 1e-6
KB = 1024

G, GH, GP = 32, 16, 64
PAIRS = G // 2
SC = 8
NC = T // SC

HALVES = (12, 10)
FT = sum(HALVES)

B_U, B_QKV, B_Z, B_GLU, B_OUT0, B_FF0 = 0, 4, 16, 20, 24, 32
FF_UNITS = 2 * (HALVES[0] + HALVES[1]) + 2 * 16
B_SB = B_FF0 + FF_UNITS
B_OUT1 = B_SB + 24
B_FF1 = B_OUT1 + 8

GDN_STAGES = [("q", "k", "v"), ("kT", "qT", "bT"), ("gr",), ("at",), ("lt",), ("dT",), ("l",),
              ("d2", "d2t"), ("x1",), ("d4", "d4t"), ("x2",), ("d8t",), ("x3",), ("xt",),
              ("z0",), ("xc0",), ("xtc0",), ("z1",), ("xc1",), ("xtc1",), ("z2",), ("xtc2",),
              ("u", "w"), ("s0",), ("ws1",), ("s1",), ("ws2",), ("s2",), ("ws3",), ("oT",)]
GDN_AT = {}
for _stage in GDN_STAGES:
    for _h in range(NH):
        for _name in _stage:
            GDN_AT[(_name, _h)] = len(GDN_AT)

TWO_PI = 2 * np.pi
PI_1 = 6.28125
PI_2 = float(np.float32(0.0019350051879882812))
PI_3 = TWO_PI - PI_1 - PI_2
PI_BELOW = float(np.nextafter(np.float32(np.pi), np.float32(0)))
LN2_1, LN2_2 = 0.693359375, -2.12194440e-4
ROUND = 12582912.0

Z_OFF = (0, T, 2 * T, T + 384)
Z_BANK, Z_COL = tuple(o // T for o in Z_OFF), tuple(o % T for o in Z_OFF)


def trunk(nc, x, c, ada_w, ada_b, norm_mix_w, norm_ffn_w, ffn_w_in, ffn_w_out, hy_w_in, hy_conv_w,
          hy_a_log, hy_dt_bias, hy_head_norm_w, s5_lam_re, s5_lam_im, s5_log_dt, s5_b_re, s5_b_im,
          s5_c_re, s5_c_im, s5_d, s5_glu_w, s5_glu_b, hy_w_out, sb_w_in, sb_w_out, final_norm_w,
          out):
    ctx = ExitStack()
    with ctx:
        base = -(-nc.sbuf_base // 64) * 64

        def at(name, offset, shape, dt=F32):
            return nc.alloc_sbuf_tensor_at(name, shape, dt, offset=base + round(offset * KB))

        h = at("h", 0, [P, KT, T])
        raw = [at(f"raw{s}", 16 + 8 * s, [P, 2048]) for s in range(2)]
        whi = [at(f"whi{s}", 32 + 8 * s, [P, 2048], F32R) for s in range(2)]
        wlo = [at(f"wlo{s}", 48 + 8 * s, [P, 2048], F32R) for s in range(2)]
        hn_hi = at("hn_hi", 64, [P, KT, T], F32R)
        hn_lo = at("hn_lo", 80, [P, KT, T], F32R)
        ff_hi = at("ff_hi", 96, [P, 12, T], F32R)
        ff_lo = at("ff_lo", 120, [P, 12, T], F32R)
        ada1_in = [at(f"ada1_in{s}", 144 + 12 * s, [P, 3072]) for s in range(2)]
        ada1_acc = at("ada1_acc", 168, [P, 3072])
        x_tok = at("x_tok", 64, [P, TT, D])
        lam = at("lam", 154, [16, 32, P])
        ada_first = [at(f"ada_first{g}", o, [P, 4, D]) for g, o in enumerate((96, 120, 138))]
        ada_first.append(ada_first[0])
        w_in = at("w_in", 96, [P, 2, PAIRS, P])
        b_re, b_im = (at(n, 112 + i, [P, PAIRS, GH]) for i, n in enumerate(("b_re", "b_im")))
        c_re, nc_re, nc_im = (at(n, 114 + i, [P, PAIRS, GH])
                              for i, n in enumerate(("c_re", "nc_re", "nc_im")))
        bb_re, bb_im = (at(n, 117 + i, [P, PAIRS, GH]) for i, n in enumerate(("bb_re", "bb_im")))
        w_ba = at("w_ba", 119, [P, KT, 8])
        w_ba_hi, w_ba_lo = at("w_ba_hi", 119.25, [P, KT, 8], F32R), at("w_ba_lo", 119.5, [P, KT, 8], F32R)
        u_perm = at("u_perm", 104, [P, 4, SC, NC])
        v_re = at("v_re", 120, [P, PAIRS, SC + 1, GH])
        v_im = at("v_im", 129, [P, PAIRS, SC + 1, GH])
        m_in = at("m_in", 138, [P, G, P])
        u_rows = at("u_rows", 154, [P, G, NC])
        m_pair, u_pair = (t[:, :, :].rearrange("p (i two) m -> p i two m", two=2) for t in (m_in, u_rows))
        wt_re = at("wt_re", 154, [P, PAIRS, SC, GH])
        wt_im = at("wt_im", 162, [P, PAIRS, SC, GH])
        s_re, s_im = at("s_re", 162, [P, PAIRS, NC]), at("s_im", 166, [P, PAIRS, NC])
        c_raw = at("c_raw", 170, [P, 2, 4, P])
        v_t = at("v_t", 138, [P, PAIRS, SC + 1, GH])
        wt_t = at("wt_t", 172, [P, 1024])
        scan_a, scan_b = at("scan_a", 170, [P, 49 * PAIRS]), at("scan_b", 173.125, [P, 49 * PAIRS])
        pw_re, pw_im = (at(n, 176.25 + 0.5625 * i, [P, SC + 1, PAIRS])
                        for i, n in enumerate(("pw_re", "pw_im")))
        f_co = at("f_co", 177.375, [P, 2, PAIRS])
        y_s5 = at("y_s5", 162, [P, 4, SC, NC])
        u_again = at("u_again", 170, [P, 4, SC, NC])
        ys_hi, ys_lo = at("ys_hi", 154, [P, 4, T], F32R), at("ys_lo", 170, [P, 4, T], F32R)
        ada0_in = [at(f"ada0_in{s}", 178 + 4 * s, [P, 1024]) for s in range(2)]
        ada0_acc = [at("ada0_acc0", 186, [P, 1024]), at("ada0_acc1", 194.5, [P, 1024])]
        conv = at("conv", 96, [P, 3, NH, T])
        z_act = at("z_act", 138, [P, NH, T])

        def gdn(name, offset):
            return at(name, offset, [P, NH, TT, P])

        kT, qT, bT = gdn("kT", 96), gdn("qT", 104), gdn("bT", 112)
        attnT, LT = gdn("attnT", 104), gdn("LT", 112)
        q_tok, k_tok, v_tok = gdn("q_tok", 120), gdn("k_tok", 128), gdn("v_tok", 64)
        kb_tok, qd_tok = gdn("kb_tok", 72), gdn("qd_tok", 80)
        kd_tok, rk_tok = gdn("kd_tok", 88), gdn("rk_tok", 146)
        qdT, dec = gdn("qdT", 120), gdn("dec", 128)
        Da, DaT, Db, DbT, X = (gdn(n, o) for n, o in (("Da", 72), ("DaT", 80), ("Db", 96),
                                                      ("DbT", 128), ("X", 178)))
        XT, Z, vn, wT = gdn("XT", 72), gdn("Z", 96), gdn("vn", 64), gdn("wT", 146)
        o_n, o_z = gdn("o_n", 72), at("o_z", 80, [P, NH, T])
        mo_hi, mo_lo = at("mo_hi", 96, [P, NH, T], F32R), at("mo_lo", 112, [P, NH, T], F32R)
        sb_qk = at("sb_qk", 144, [P, 2, 4, T])
        sb_v = at("sb_v", 160, [P, TT, 4, P])
        zb = [at("zb0", 168, [P, 1280]), at("zb1", 136, [P, 1280])]
        e_b = at("e_b", 173, [P, 1280])
        sp_hi, sp_lo = at("sp_hi", 178, [P, 1280], F32R), at("sp_lo", 183, [P, 1280], F32R)
        w_b = at("w_b", 112, [P, 1280])
        ones_r, tril_r = at("ones_r", 117, [P, P], F32R), at("tril_r", 117.5, [P, P], F32R)
        ident_r, below_r = at("ident_r", 118, [P, P], F32R), at("below_r", 118.5, [P, P], F32R)
        out_tok = at("out_tok", 96, [P, TT, D])

        cursor = [190.0]

        def small(name, shape, dt=F32):
            t = at(name, cursor[0], shape, dt)
            cursor[0] += -(-int(np.prod(shape[1:])) // 8) * 8 * 4 / KB
            return t

        ident, ones, triu, tril, below = (small(n, [P, P])
                                          for n in ("ident", "ones", "triu", "tril", "below"))
        bd16 = small("bd16", [P, P])
        level = [small(f"level{i}", [P, P]) for i in range(3)]
        tmp = [small(f"tmp{i}", [P, T]) for i in range(2)]
        S = at("S", 194.5, [P, NH, P])
        sq = small("sq", [P, T])
        sq_sum = small("sq_sum", [P, T])
        diag = small("diag", [P, TT, P])
        vec_a, vec_b = at("vec_a", 174.0, [96, P]), at("vec_b", 174.5, [97, P])
        ba_row = at("ba_row", 202.5, [8, T])
        vb = small("vb", [P, 97])
        ada_bias = small("ada_bias", [P, 96])
        mod = small("mod", [P, 96])
        c_col, c_act = small("c_col", [P, 8]), small("c_act", [P, 8])
        n_scale = small("n_scale", [P, KT])
        cst = small("cst", [P, 2])
        ss, rstd = small("ss", [P, TT]), small("rstd", [P, TT])
        ba = small("ba", [P, TT, 8])
        beta, g_log, gc, gc_exp, k_fac, s_fac = (small(n, [P, TT, NH]) for n in (
            "beta", "g_log", "gc", "gc_exp", "k_fac", "s_fac"))
        g_t = [at(f"g_t{i}", 177.5 + 0.0625 * i, [P, TT, NH]) for i in range(2)]
        neg_a, dt_b = small("neg_a", [P, NH]), small("dt_b", [P, NH])
        qk_ss, qk_rn = small("qk_ss", [P, 2, NH, TT]), small("qk_rn", [P, 2, NH, TT])
        o_ss, o_rn = small("o_ss", [P, NH, TT]), small("o_rn", [P, NH, TT])
        q_pw = small("q_pw", [P, 2, SC, PAIRS])
        g_tq = at("g_tq", 176.0, [P, 4, PAIRS])
        bb_t = at("bb_t", 175.0, [P, PAIRS, GH])
        tmp_o = [sq, diag[:, :, :].rearrange("p c i -> p (c i)")]
        assert base + cursor[0] * KB <= nc.sbuf_usable_end, cursor
        EPS_C, ONE_C = cst[:, 0:1], cst[:, 1:2]
        CONV, NMIX, NFFN, NFIN, S5D, GLUB, HNW = 0, 48, 64, 80, 88, 92, 96

        banks = ctx.enter_context(nc.psum_tensor("banks", [P, 8, T], F32))
        bank = [banks[:, i, :] for i in range(8)]
        flat = banks[:, :, :].rearrange("p b t -> p (b t)")

        u_dram = nc.dram_tensor("u_rows_dram", [SC, W, NC], F32, kind="Internal").ap()
        y_dram = nc.dram_tensor("y_rows_dram", [SC, W, NC], F32, kind="Internal").ap()

        def sem(name):
            return ctx.enter_context(nc.semaphore(name))

        raw_in = [sem(f"raw{s}_loaded") for s in range(2)]
        hi_done, lo_done = sem("weights_hi_done"), sem("weights_lo_done")
        block_done, block_free = sem("block_done"), sem("block_free")
        x_in, vec_in, c_in, lam_in, bc_in, gdn_in = (sem(n) for n in (
            "x_loaded", "vectors_loaded", "c_loaded", "lambda_loaded", "b_and_c_loaded",
            "gdn_vectors_loaded"))
        consts = sem("constants_ready")
        vec_t, vec_ready, c_ready = sem("vectors_turned"), sem("vectors_ready"), sem("c_ready")
        x_t, x_done = sem("x_turned"), sem("x_copied")
        ada0_ld = [sem(f"ada0_loaded{s}") for s in range(2)]
        first_ld = [sem(f"ada_first{g}_loaded") for g in range(4)]
        ba_rows, ba_copied = sem("ba_rows_summed"), sem("ba_rows_copied")
        ada1_ld = [sem(f"ada1_loaded{s}") for s in range(2)]
        ada_used, mod_sum, mod_done = sem("ada_tiles_used"), sem("mod_summed"), sem("mod_ready")
        sq_done, sq_added, ss_done = sem("squares_ready"), sem("squares_added"), sem("mean_square_ready")
        sd_done, diag_done, rb_done = sem("norm_root_ready"), sem("norm_diag_ready"), sem("norm_rows_ready")
        h_scaled, hi_norm, hn_done = sem("h_scaled"), sem("hn_hi_done"), sem("hn_done")
        dve_step, act_step, pool_step = sem("dve_steps"), sem("act_steps"), sem("pool_steps")
        dt_done, lam_exp, lam_trig, lam_done = (sem(n) for n in (
            "dt_ready", "lambda_angles", "lambda_trig", "lambda_ready"))
        lam_t, pw_done, c_t, c_done, bb_done, v_done, wt_done, wt_t_done, w_done = (sem(n) for n in (
            "powers_turned", "powers_ready", "c_turned", "c_ready_s5", "b_bar_ready", "v_ready",
            "w_rows_ready", "w_turned", "w_ready"))
        m_zero, k_sum, k_done, m_done = (sem(n) for n in (
            "m_zeroed", "taps_summed", "taps_ready", "m_ready"))
        u_out, u_in, p_sum, p_done, scan_done = (sem(n) for n in (
            "u_stored", "u_rows_loaded", "chunk_inputs_summed", "chunk_inputs_ready",
            "states_ready"))
        y_sum, y_done, y_out, y_in, u2_in = (sem(n) for n in (
            "y_summed", "y_rows_ready", "y_stored", "y_loaded", "u_loaded_again"))
        y_du, ys_hi_done, ys_done, glu_mul, mix_s5 = (sem(n) for n in (
            "y_with_skip", "ys_hi_ready", "ys_ready", "glu_product_ready",
            "s5_half_ready"))
        ba_in, ba_split, ba_sum = (sem(n) for n in (
            "w_ba_loaded", "w_ba_split", "ba_summed"))
        g_done, gc_sum, gc_diff, gates = (sem(n) for n in (
            "g_ready", "g_summed", "g_differences", "gate_factors_ready"))
        conv_tap = sem("conv_first_tap")
        silu_done = sem("conv_silu_done")
        gdn_done = sem("gdn_product_done")
        drained = [sem(f"gdn_bank{i}_drained") for i in range(4)]
        qk_sq, qk_root, qn_done, kn_done, kb_done, rv_done = (sem(n) for n in (
            "qk_squares", "qk_root", "q_normed", "k_normed", "k_beta", "v_beta"))
        qd_done, rk_done, kd_done = sem("q_decayed"), sem("rk_ready"), sem("k_decayed")
        dec_exp, dec_done, lt_done, dat_done, x0_done = (sem(n) for n in (
            "decay_exp", "decay_masked", "lt_masked", "dat_ready", "x0_ready"))
        o_done, o_sq_done, o_root, on_done, mo_hi_done, mo_done = (sem(n) for n in (
            "o_done", "o_squares", "o_root", "o_normed", "gdn_half_hi", "gdn_half_ready"))
        gate_act, up_mul, ff_hi_done = (sem(n) for n in (
            "gate_silu", "gate_times_up", "hidden_hi"))
        sbz, sbz_done, sbe, sb_sp = (sem(n) for n in (
            "sb_scores_done", "sb_scores_copied", "sb_exp", "sb_softplus"))
        sb_spe, sb_hi, sb_lo, sb_c, sb_w, sb_p, sb_o, sbo_hi, sbo_done = (sem(n) for n in (
            "sb_log", "sb_softplus_hi", "sb_softplus_split", "sb_sums_done", "sb_exponents",
            "sb_weights", "sb_values_done", "sb_out_hi", "sb_out_ready"))
        lam_recip = sem("lambda_reciprocal")
        pw0_done, neg_a_done = sem("power_zero_set"), sem("decay_rates_ready")
        sb_abs, cons_r = sem("sb_abs"), sem("rounded_constants")
        g_abs, g_ln, beta_done, qk_red, o_red, oz_done, glu_hi = (sem(n) for n in (
            "decay_input_abs", "softplus_log", "beta_ready", "qk_squares_summed",
            "o_squares_summed", "o_gated", "glu_product_hi"))
        fin_t, fin_copied, out_sem = sem("output_turned"), sem("output_copied"), sem("output_stored")

        def gp(name, hd):
            q = GDN_AT[(name, hd)]
            return q, 4 + q % 4, q // 4 + 1

        def wait_drained(eng, name, hd):
            q = GDN_AT[(name, hd)]
            eng.wait_ge(drained[q % 4], q // 4 + 1)

        def bc(ap, n):
            return ap.unsqueeze(2).to_broadcast([P, ap.shape[1], n])

        def perm(ap):
            return ap.rearrange("p (c j) -> p j c", j=SC)

        def ada_steps(eng, layer, n_f, body):
            if layer == 0:
                body(0, False)
                with eng.Fori(1, 5) as i:
                    body(i, True)
                if n_f > 10:
                    body(5, False)
            else:
                with eng.Fori(0, n_f // 2) as i:
                    body(i, False)

        block = ctx.enter_context(nc.Block())

        @block.sync
        def _(sp):
            def load_slot(n, s, views, first=False):
                if not first:
                    sp.wait_ge(lo_done, n - 1)
                for dst, src in views:
                    sp.dma_start(dst, src).then_inc(raw_in[s], 16)

            def cols(wt, col, k=KT, width=256):
                def views(s):
                    half = k // 2
                    dst = raw[s][:, 0:k * width].rearrange("p (k m) -> p k m", k=k)
                    src = wt[:, bass.ds(col, width)].rearrange("(k p) m -> p k m", p=P)
                    return [(dst[:, 0:half, :], src[:, 0:half, :]), (dst[:, half:k, :], src[:, half:k, :])]
                return views

            def ada0_tile(part, t):
                n = 8 * part + t
                if n >= 18:
                    sp.wait_ge(ada_used, n - 1)
                src = ada_w[0].rearrange("(p t) n -> p t n", t=8)[:, t, part * D:(part + 1) * D]
                sp.dma_start(ada0_in[n % 2][:, :], src).then_inc(ada0_ld[n % 2], 16)

            x_rows = x[0].rearrange("(t p) d -> p t d", p=P)
            for t in range(TT):
                sp.dma_start(x_tok[:, t, :], x_rows[:, t, :]).then_inc(x_in, 16)
            w = hy_w_in[0]
            U0 = 4 * W + 2 * NH
            for g in range(4):
                if g == 3:
                    sp.wait_ge(ada_used, 4)
                rows = ada_w[0].rearrange("(p t) n -> p t n", t=8)[:, 4 * (g % 2):4 * (g % 2) + 4, :]
                sp.dma_start(ada_first[g][:, :, :], rows[:, :, (g // 2) * D:(g // 2 + 1) * D])\
                  .then_inc(first_ld[g], 16)
                if g == 1:
                    load_slot(0, 0, cols(w, U0)(0), first=True)
            load_slot(1, 1, cols(w, U0 + 256)(1), first=True)
            for s in range(2):
                load_slot(2 + s, s, cols(w, 256 * s)(s))
            for t in range(4):
                sp.wait_ge(block_free, B_U + t + 1)
                sp.dma_start(u_dram[:, t * P:(t + 1) * P, :].rearrange("j p c -> p j c"),
                             u_perm[:, t, :, :]).then_inc(u_out, 16)
            sp.wait_ge(u_out, 64)
            sp.wait_ge(w_done, 8)
            for j in range(SC):
                sp.dma_start(u_rows[j * GH:(j + 1) * GH, :, :],
                             u_dram[j].rearrange("(g h) c -> h g c", h=GH)).then_inc(u_in, 16)
            for t in range(4):
                ada0_tile(2, t)
            sp.wait_ge(k_done, 8)
            for j in range(1, SC):
                sp.dma_start(m_in[j * GH:(j + 1) * GH, :, j * GH:P],
                             m_in[0:GH, :, 0:P - j * GH]).then_inc(m_done, 16)
            for n in range(4, 8):
                load_slot(n, n % 2, cols(w, 256 * (n - 2))(n % 2))
                for i in range(2 if n < 6 else 4):
                    if n < 6:
                        ada0_tile(2, 4 + 2 * (n - 4) + i)
                    else:
                        ada0_tile(3, 4 * (n - 6) + i)
            load_slot(8, 0, cols(w, 256 * 6)(0))
            load_slot(9, 1, cols(w, 256 * 7)(1))
            for part in range(4, 6):
                for t in range(8):
                    ada0_tile(part, t)
            sp.wait_ge(scan_done, 1)
            for t in range(4):
                sp.dma_start(u_again[:, t, :, :],
                             u_dram[:, t * P:(t + 1) * P, :].rearrange("i p c -> p i c")).then_inc(u2_in, 16)
            for i in range(SC):
                if i == 0:
                    sp.wait_ge(y_done, 4)
                sp.dma_start(y_dram[i].rearrange("(g h) c -> h g c", h=GH),
                             u_rows[i * GH:(i + 1) * GH, :, :]).then_inc(y_out, 16)
            sp.wait_ge(y_out, 128)
            for t in range(4):
                sp.dma_start(y_s5[:, t, :, :],
                             y_dram[:, t * P:(t + 1) * P, :].rearrange("i p c -> p i c")).then_inc(y_in, 16)
            for s in range(2):
                load_slot(10 + s, s, cols(s5_glu_w[0], 256 * s, k=4)(s))
            with sp.Fori(0, 2) as i:
                for s in range(2):
                    load_slot(12 + 2 * i + s, s, cols(hy_w_out[0], 512 * i + 256 * s)(s))

            def ffn(layer, slot):
                first = 0
                for half, n_f in enumerate(HALVES):
                    def in_slots(i):
                        for s in range(2):
                            sp.wait_ge(lo_done, slot + 2 * i + s - 1)
                            dst = raw[s][:, :].rearrange("p (k two m) -> p k two m", k=KT, two=2)
                            for two in range(2):
                                src = ffn_w_in[layer][:, bass.ds(two * F + (first + s) * P + i * 256, P)]
                                sp.dma_start(dst[:, :, two, :], src.rearrange("(k p) m -> p k m", p=P))\
                                  .then_inc(raw_in[s], 16)

                    with sp.Fori(0, n_f // 2) as i:
                        in_slots(i)
                    slot += n_f
                    rows = ffn_w_out[layer][first * P:(first + n_f) * P, :]
                    with sp.Fori(0, 2) as i:
                        for s in range(4):
                            load_slot(slot + 4 * i + s, s % 2,
                                      cols(rows, 512 * i + 128 * s, k=n_f, width=P)(s % 2))
                    slot += 8
                    first += n_f

            ffn(0, 16)
            with sp.Fori(0, 2) as i:
                for pair in range(2):
                    for kind in range(3):
                        s = (3 * pair + kind) % 2
                        load_slot(54 + 6 * i + 3 * pair + kind, s,
                                  cols(sb_w_in[0], kind * D + 256 * pair + 512 * i)(s))
            with sp.Fori(0, 2) as i:
                for s in range(2):
                    load_slot(66 + 2 * i + s, s, cols(sb_w_out[0], 512 * i + 256 * s)(s))
            ffn(1, 70)
            for t in range(TT):
                sp.wait_ge(fin_copied, KT)
                sp.dma_start(out[0].rearrange("(t p) d -> p t d", p=P)[:, t, :],
                             out_tok[:, t, :]).then_inc(out_sem, 16)
            sp.wait_ge(out_sem, 16 * TT)

        @block.tensor
        def _(pe):
            def pass3(o, lh, ll, rh, rl, first, last):
                pe.matmul(o, lh, rh, start=first, stop=False)
                pe.matmul(o, lh, rl, start=False, stop=False)
                return pe.matmul(o, ll, rh, start=False, stop=last)

            def gemm(b, s, j, rhs_hi, rhs_lo, k_tiles=KT, width=256, units=1, last_tile=None):
                mh = whi[s][:, 0:k_tiles * width].rearrange("p (k m) -> p k m", k=k_tiles)
                ml = wlo[s][:, 0:k_tiles * width].rearrange("p (k m) -> p k m", k=k_tiles)
                c0, c1 = j * P, (j + 1) * P
                for k in range(k_tiles):
                    if last_tile is not None and k == k_tiles - 1:
                        pe.wait_ge(block_free, last_tile)
                    last = pass3(bank[b][:, :], mh[:, k, c0:c1], ml[:, k, c0:c1],
                                 rhs_hi[:, k, :], rhs_lo[:, k, :], k == 0, k == k_tiles - 1)
                last.then_inc(block_done, units)

            def slot_ready(n):
                pe.wait_ge(lo_done, n + 1)

            def four_blocks(slot, unit, rhs_hi, rhs_lo, k_tiles=KT, first=False):
                for s in range(2):
                    slot_ready(slot + s)
                    for j in range(2):
                        r = 2 * s + j
                        if not first:
                            pe.wait_ge(block_free, unit + r - 3)
                        gemm(r, s, j, rhs_hi, rhs_lo, k_tiles)

            def norm(n):
                pe.wait_ge(sq_added, 8 * (n + 1))
                for c_ in range(TT):
                    last = pe.matmul(bank[6][:, c_:c_ + 1], sq_sum[:, c_ * P:(c_ + 1) * P],
                                     ones[:, 0:1], start=True, stop=True)
                last.then_inc(ss_done, 1)
                pe.wait_ge(diag_done, n + 1)
                pe.matmul(bank[6][:, :], ones[:, :], diag[:, :, :].rearrange("p c i -> p (c i)"),
                          start=True, stop=True).then_inc(rb_done, 1)

            def mod_parts(part, accs, n_used):
                for n, acc in enumerate(accs):
                    pe.wait_ge(ada_used, n_used[n])
                    for k in range(KT):
                        m = 8 * (part + n) + k
                        last = pe.matmul(bank[7][:, m:m + 1], acc[:, k * P:(k + 1) * P], ones[:, 0:1],
                                         start=True, stop=True)
                last.then_inc(mod_sum, 1)

            pe.wait_ge(consts, 1)
            pe.wait_ge(x_in, 16 * TT)
            for k in range(KT):
                b = k % 4
                if k >= 4:
                    pe.wait_ge(x_done, k - 3)
                for t in range(TT):
                    last = pe.transpose(bank[b][:, t * P:(t + 1) * P], x_tok[:, t, k * P:(k + 1) * P],
                                        ident[:, :])
                last.then_inc(x_t, 1)
            norm(0)
            pe.wait_ge(vec_in, 16 * 8)
            pe.transpose(bank[7][:, 96:192], vec_a[:, :], ident[0:96, 0:96])
            pe.transpose(bank[7][:, 192:289], vec_b[:, :], ident[0:97, 0:97]).then_inc(vec_t, 1)
            pe.wait_ge(bc_in, 16 * 8)
            for part in range(2):
                for q in range(4):
                    last = pe.transpose(bank[4 + part][:, q * P:(q + 1) * P], c_raw[:, part, q, :],
                                        ident[:, :])
            last.then_inc(c_t, 1)
            pe.wait_ge(vec_ready, 1)
            mod_parts(0, ada0_acc, (8, 16))
            pe.wait_ge(lam_done, 1)
            pe.wait_ge(c_done, 1)
            for n in range(18):
                row = (16 + n) if n < 16 else 12 + (n - 16)
                last = pe.transpose(bank[4][:, 16 * n:16 * n + 16], lam[:, row, :], ident[0:16, 0:16])
            last.then_inc(lam_t, 1)
            pe.wait_ge(c_done, 1)
            pe.wait_ge(ba_split, 2)
            for k in range(KT):
                pe.wait_ge(hn_done, k + 1)
                last = pass3(bank[5][0:8, :], w_ba_hi[:, k, :], w_ba_lo[:, k, :], hn_hi[:, k, :],
                             hn_lo[:, k, :], k == 0, k == KT - 1)
            last.then_inc(ba_rows, 1)
            four_blocks(0, B_U, hn_hi, hn_lo, first=True)
            pe.wait_ge(ba_copied, 1)
            pe.wait_ge(mod_done, 1)
            for t in range(TT):
                last = pe.transpose(bank[7][:, 300 + 8 * t:308 + 8 * t], ba_row[:, t * P:(t + 1) * P],
                                    ident[0:8, 0:8])
            last.then_inc(ba_sum, 1)
            pe.wait_ge(wt_done, 2)
            for q in range(8):
                src = (wt_re, wt_im)[q // 4]
                b = 4 + q % 2
                if q >= 2:
                    pe.wait_ge(w_done, q - 1)
                for r in range(4):
                    i = 4 * (q % 4) + r
                    last = pe.transpose(bank[b][:, r * P:(r + 1) * P],
                                        src[:, i, :, :].rearrange("p j h -> p (j h)"), ident[:, :])
                last.then_inc(wt_t_done, 1)
            pe.wait_ge(bb_done, 1)
            pe.wait_ge(v_done, 1)
            for q in range(8):
                b = 4 + q % 2
                if q >= 2:
                    pe.wait_ge(k_done, q - 1)
                else:
                    pe.wait_ge(w_done, 7 + q)
                i0, par = 4 * (q // 2), q % 2
                rows = slice(64 * par, 64 * par + 64)
                for r in range(4):
                    i = i0 + r
                    o = bank[b][0:GH, r * P:(r + 1) * P]
                    pe.matmul(o, bb_re[rows, i, :], v_re[rows, i, 0:SC, :], start=True, stop=False)
                    last = pe.matmul(o, bb_im[rows, i, :], v_im[rows, i, 0:SC, :], start=False, stop=True)
                last.then_inc(k_sum, 1)
            pe.wait_ge(g_done, 1)
            gl = g_log[:, :, :].rearrange("p c h -> p (c h)")
            pe.matmul(bank[7][:, 340:356], triu[:, :], gl, start=True, stop=True)
            pe.matmul(bank[7][:, 356:372], ones[:, :], gl, start=True, stop=True).then_inc(gc_sum, 1)

            pe.wait_ge(w_done, 8)
            pe.wait_ge(k_done, 8)
            pe.wait_ge(gc_diff, 1)
            pe.wait_ge(u_in, 16 * SC)
            for part in range(2):
                for hb in range(2):
                    b = 4 + 2 * part + hb
                    for r in range(8):
                        for par in range(2):
                            i = 8 * hb + r
                            last = pe.matmul(bank[b][64 * par:64 * par + 64, r * NC:(r + 1) * NC],
                                             w_in[:, part, i, 64 * par:64 * par + 64],
                                             u_rows[:, 2 * i + par, :], start=True, stop=True)
                    last.then_inc(p_sum, 1)
            with pe.Fori(0, 3) as i:
                four_blocks(2 + 2 * i, B_QKV + 4 * i, hn_hi, hn_lo)
            mod_parts(2, ada0_acc, (24, 32))
            pe.wait_ge(p_done, 4)
            pe.wait_ge(scan_done, 1)
            pe.wait_ge(m_done, 16 * (SC - 1))
            pe.wait_ge(mod_done, 2)
            for q in range(4):
                par, i0 = q // 2, 8 * (q % 2)
                rows = slice(64 * par, 64 * par + 64)
                for r in range(8):
                    i, g = i0 + r, 2 * (i0 + r) + par
                    o = bank[4 + q][:, r * NC:(r + 1) * NC]
                    pe.matmul(o, m_in[:, g, :], u_rows[:, g, :], start=True, stop=False)
                    o = bank[4 + q][:, r * NC + 1:(r + 1) * NC]
                    pe.matmul(o, v_re[rows, i, 1:SC + 1, :], s_re[rows, i, 0:NC - 1],
                              start=False, stop=False)
                    last = pe.matmul(o, v_im[rows, i, 1:SC + 1, :], s_im[rows, i, 0:NC - 1],
                                     start=False, stop=True)
                last.then_inc(y_sum, 1)
            for s in range(2):
                slot_ready(8 + s)
                for j in range(2):
                    pe.wait_ge(block_free, B_Z + 2 * s + j - 3)
                    gemm(2 * s + j, s, j, hn_hi, hn_lo)
                if s == 0:
                    pe.wait_ge(y_done, 4)
                    mod_parts(4, ada0_acc, (40, 48))
            def product(name, hd, f, n=TT):
                q, b, _ = gp(name, hd)
                if q >= 4:
                    pe.wait_ge(drained[q % 4], q // 4)
                for c_ in range(n):
                    last = f(bank[b][:, c_ * P:(c_ + 1) * P], c_)
                last.then_inc(gdn_done, 1)

            def turn(name, hd, src):
                product(name, hd, lambda o, c_: pe.transpose(o, src[:, hd, c_, :], ident[:, :]))

            def mul(name, hd, l, r):
                product(name, hd, lambda o, c_: pe.matmul(o, l[:, hd, c_, :], r[:, hd, c_, :],
                                                          start=True, stop=True))

            pe.wait_ge(silu_done, 12)
            pe.wait_ge(mod_done, 3)
            cv = conv[:, :, :, :].rearrange("p w h (c i) -> p w h c i", c=TT)
            for hd in range(NH):
                for w_, name in enumerate(("q", "k", "v")):
                    turn(name, hd, cv[:, w_])
            for hd in range(NH):
                pe.wait_ge(kn_done, hd + 1)
                turn("kT", hd, k_tok)
                pe.wait_ge(qn_done, hd + 1)
                turn("qT", hd, q_tok)
                pe.wait_ge(kb_done, hd + 1)
                turn("bT", hd, kb_tok)
            for hd in range(NH):
                product("gr", hd, lambda o, c_: pe.matmul(
                    o, g_log[:, c_, hd:hd + 1].to_broadcast([P, P]), triu[:, :], start=True, stop=True))
            for hd in range(NH):
                wait_drained(pe, "qT", hd)
                wait_drained(pe, "kT", hd)
                mul("at", hd, kT, qT)
            for hd in range(NH):
                wait_drained(pe, "bT", hd)
                mul("lt", hd, kT, bT)
            for hd in range(NH):
                pe.wait_ge(qd_done, hd + 1)
                turn("dT", hd, qd_tok)
            for hd in range(NH):
                pe.wait_ge(lt_done, hd + 1)
                turn("l", hd, LT)
            pe.wait_ge(ys_done, 1)
            four_blocks(10, B_GLU, ys_hi, ys_lo, k_tiles=4)
            for hd in range(NH):
                pe.wait_ge(dat_done, hd + 1)
                wait_drained(pe, "l", hd)
                mul("d2", hd, DaT, Da)
                mul("d2t", hd, Da, DaT)
            for hd in range(NH):
                wait_drained(pe, "d2t", hd)
                pe.wait_ge(x0_done, hd + 1)
                mul("x1", hd, DbT, X)
            for hd in range(NH):
                wait_drained(pe, "d2", hd)
                mul("d4", hd, DbT, Db)
                mul("d4t", hd, Db, DbT)
            for hd in range(NH):
                wait_drained(pe, "d4t", hd)
                wait_drained(pe, "x1", hd)
                mul("x2", hd, DaT, X)
            for hd in range(NH):
                wait_drained(pe, "d4", hd)
                mul("d8t", hd, Da, DaT)
            for hd in range(NH):
                wait_drained(pe, "d8t", hd)
                wait_drained(pe, "x2", hd)
                mul("x3", hd, DbT, X)
            for hd in range(NH):
                wait_drained(pe, "x3", hd)
                turn("xt", hd, X)
            for lv in range(3):
                for hd in range(NH):
                    wait_drained(pe, "xt" if lv == 0 else f"xc{lv - 1}", hd)
                    mul(f"z{lv}", hd, LT, X)
                if lv < 2:
                    for hd in range(NH):
                        wait_drained(pe, f"z{lv}", hd)
                        if lv > 0:
                            wait_drained(pe, f"xtc{lv - 1}", hd)
                        mul(f"xc{lv}", hd, XT, Z)
                for hd in range(NH):
                    wait_drained(pe, f"z{lv}", hd)
                    if lv > 0:
                        wait_drained(pe, f"xtc{lv - 1}", hd)
                    mul(f"xtc{lv}", hd, Z, XT)
            for hd in range(NH):
                wait_drained(pe, "xtc2", hd)
                pe.wait_ge(rv_done, hd + 1)
                mul("u", hd, XT, v_tok)
                pe.wait_ge(rk_done, hd + 1)
                mul("w", hd, rk_tok, XT)
            for c_ in range(TT):
                for hd in range(NH):
                    if c_ == 0:
                        wait_drained(pe, "dT", hd)
                        wait_drained(pe, "u", hd)
                        wait_drained(pe, "w", hd)
                        pe.wait_ge(kd_done, hd + 1)
                        pe.wait_ge(block_free, B_OUT0)
                    else:
                        wait_drained(pe, f"s{c_ - 1}", hd)
                        product(f"ws{c_}", hd, lambda o, _: pe.matmul(
                            o, wT[:, hd, c_, :], S[:, hd, :], start=True, stop=True), n=1)
                        pe.matmul(bank[hd][:, c_ * P:(c_ + 1) * P], qdT[:, hd, c_, :], S[:, hd, :],
                                  start=True, stop=False)
                for hd in range(NH):
                    if c_ > 0:
                        wait_drained(pe, f"ws{c_}", hd)
                    last = pe.matmul(bank[hd][:, c_ * P:(c_ + 1) * P], attnT[:, hd, c_, :],
                                     vn[:, hd, c_, :], start=(c_ == 0), stop=True)
                    if c_ == TT - 1:
                        last.then_inc(o_done, 1)
                    else:
                        product(f"s{c_}", hd, lambda o, _: pe.matmul(
                            o, kd_tok[:, hd, c_, :], vn[:, hd, c_, :], start=True, stop=True), n=1)
            for hd in range(NH):
                pe.wait_ge(on_done, hd + 1)
                turn("oT", hd, o_n)
            pe.wait_ge(mo_done, NH)
            pe.wait_ge(mix_s5, 4)
            mix_hi = [mo_hi[:, k, :] for k in range(4)] + [ys_hi[:, k, :] for k in range(4)]
            mix_lo = [mo_lo[:, k, :] for k in range(4)] + [ys_lo[:, k, :] for k in range(4)]
            with pe.Fori(0, 2) as i:
                for s in range(2):
                    slot_ready(12 + 2 * i + s)
                    mh = whi[s][:, :].rearrange("p (k m) -> p k m", k=KT)
                    ml = wlo[s][:, :].rearrange("p (k m) -> p k m", k=KT)
                    for j in range(2):
                        r = 2 * s + j
                        pe.wait_ge(block_free, B_OUT0 + 4 * i + r - 3)
                        for k in range(KT):
                            last = pass3(bank[r][:, :], mh[:, k, j * P:(j + 1) * P],
                                         ml[:, k, j * P:(j + 1) * P], mix_hi[k], mix_lo[k],
                                         k == 0, k == KT - 1)
                        last.then_inc(block_done, 1)
            norm(1)

            def ffn(layer, slot, unit, n):
                for half, n_f in enumerate(HALVES):
                    with pe.Fori(0, n_f // 2) as i:
                        for s in range(2):
                            slot_ready(slot + 2 * i + s)
                            for two in range(2):
                                r = 2 * s + two
                                pe.wait_ge(block_free, unit + 4 * i + r - 3)
                                mh = whi[s][:, :].rearrange("p (k two m) -> p k two m", k=KT, two=2)
                                ml = wlo[s][:, :].rearrange("p (k two m) -> p k two m", k=KT, two=2)
                                for k in range(KT):
                                    if r == 0:
                                        pe.wait_ge(hn_done, 8 * n + k + 1)
                                    last = pass3(bank[r][:, :], mh[:, k, two, :], ml[:, k, two, :],
                                                 hn_hi[:, k, :], hn_lo[:, k, :], k == 0, k == KT - 1)
                                last.then_inc(block_done, 1)
                    slot, unit = slot + n_f, unit + 2 * n_f
                    if layer == 0 and half == 0:
                        mod_parts(6 + 3 * half, [ada1_acc[:, r * D:(r + 1) * D] for r in range(3)],
                                  [56 + 8 * half] * 3)
                    with pe.Fori(0, 2) as i:
                        for s in range(4):
                            slot_ready(slot + 4 * i + s)
                            pe.wait_ge(block_free, unit + 8 * i + 2 * s - 3)
                            gemm(s, s % 2, 0, ff_hi, ff_lo, n_f, P, units=2,
                                 last_tile=unit if s == 0 else None)
                    slot, unit = slot + 8, unit + 16
                    if layer == 0 and half == 1:
                        mod_parts(6 + 3 * half, [ada1_acc[:, r * D:(r + 1) * D] for r in range(3)],
                                  [56 + 8 * half] * 3)

            ffn(0, 16, B_FF0, 1)
            norm(2)
            pe.wait_ge(cons_r, 1)

            def project(p_, m):
                kind, j = m // 2, m % 2
                s, unit = (p_ + kind) % 2, B_SB + 6 * p_ + m
                if j == 0:
                    slot_ready(54 + 3 * p_ + kind)
                pe.wait_ge(block_free, unit - 1)
                mh = whi[s][:, :].rearrange("p (k m) -> p k m", k=KT)
                ml = wlo[s][:, :].rearrange("p (k m) -> p k m", k=KT)
                if kind < 2:
                    for k in range(KT):
                        if p_ == 0 and m == 0:
                            pe.wait_ge(hn_done, 16 + k + 1)
                        last = pass3(bank[7 - j][:, :], mh[:, k, j * P:(j + 1) * P],
                                     ml[:, k, j * P:(j + 1) * P], hn_hi[:, k, :], hn_lo[:, k, :],
                                     k == 0, k == KT - 1)
                else:
                    for tt in range(2):
                        t0 = (2 * j + tt) * P
                        for k in range(KT):
                            last = pass3(bank[7 - j][:, tt * 256:(tt + 1) * 256],
                                         hn_hi[:, k, t0:t0 + P], hn_lo[:, k, t0:t0 + P],
                                         mh[:, k, :], ml[:, k, :], k == 0, k == KT - 1)
                last.then_inc(block_done, 1)

            def z_of(b0, i):
                return bank[b0 + Z_BANK[i]][:, Z_COL[i]:Z_COL[i] + T - P * i]

            def scores(hd):
                if hd % 2 == 0:
                    pe.wait_ge(block_free, B_SB + 3 * hd + 6)
                    if hd > 0:
                        pe.wait_ge(sbo_done, hd)
                else:
                    pe.wait_ge(sbz_done, hd)
                n = hd % 4
                for i in range(TT):
                    pe.matmul(z_of(0, i), sb_qk[:, 1, n, i * P:(i + 1) * P], sb_qk[:, 0, n, i * P:T],
                              start=True, stop=False)
                    last = pe.matmul(z_of(0, i)[:, 0:P], ident_r[:, :], below_r[:, :],
                                     start=False, stop=True)
                last.then_inc(sbz, 1)

            def sums(hd):
                pe.wait_ge(sb_lo, hd + 1)
                if hd > 0:
                    pe.wait_ge(sb_w, hd)
                for i in range(TT):
                    o = z_of(3, i)
                    for j in range(i, TT):
                        lhs = tril_r if j == i else ones_r
                        oj = o[:, P * (j - i):]
                        n = T - P * j
                        pe.matmul(oj, lhs[:, :], sp_hi[:, Z_OFF[j]:Z_OFF[j] + n], start=(j == i), stop=False)
                        last = pe.matmul(oj, lhs[:, :], sp_lo[:, Z_OFF[j]:Z_OFF[j] + n],
                                         start=False, stop=(j == TT - 1))
                last.then_inc(sb_c, 1)

            def values(hd):
                pe.wait_ge(sb_p, hd + 1)
                pe.wait_ge(sbz_done, hd - hd % 2 + 2)
                for i in range(TT):
                    last = pe.matmul(bank[hd % 2][:, P * i:T], sb_v[:, i, hd % 4, :],
                                     w_b[:, Z_OFF[i]:Z_OFF[i] + T - P * i], start=(i == 0),
                                     stop=(i == TT - 1))
                last.then_inc(sb_o, 1)

            def out_block(m, k0, k1, last_part=True):
                s, j = (m // 2) % 2, m % 2
                if k0 == 0:
                    if j == 0:
                        slot_ready(66 + m // 2)
                    pe.wait_ge(block_free, B_OUT1 + m - 1)
                mh = whi[s][:, :].rearrange("p (k m) -> p k m", k=KT)
                ml = wlo[s][:, :].rearrange("p (k m) -> p k m", k=KT)
                for k in range(k0, k1):
                    last = pass3(bank[7 - j][:, :], mh[:, k, j * P:(j + 1) * P],
                                 ml[:, k, j * P:(j + 1) * P], ff_hi[:, k, :], ff_lo[:, k, :],
                                 k == 0, k == KT - 1)
                if k1 == KT:
                    last.then_inc(block_done, 1)

            for m in range(6):
                project(0, m)
            for p_ in range(4):
                def fill(m):
                    if p_ < 3:
                        project(p_ + 1, m)
                    elif m < 2:
                        pe.wait_ge(sbo_done, 6)
                        out_block(m, 0, 6)
                a, b = 2 * p_, 2 * p_ + 1
                fill(0)
                scores(a)
                fill(1)
                scores(b)
                fill(2)
                sums(a)
                fill(3)
                fill(4)
                sums(b)
                values(a)
                fill(5)
                values(b)
            pe.wait_ge(sbo_done, 8)
            for m in range(KT):
                out_block(m, 6 if m < 2 else 0, KT)
            norm(3)
            ffn(1, 70, B_FF1, 3)
            norm(4)
            for k in range(KT):
                pe.wait_ge(h_scaled, 8 * 4 + k + 1)
                if k >= 4:
                    pe.wait_ge(fin_copied, k - 3)
                for t in range(TT):
                    last = pe.transpose(bank[k % 4][:, t * P:(t + 1) * P],
                                        tmp[k % 2][:, t * P:(t + 1) * P], ident[:, :])
                last.then_inc(fin_t, 1)

        @block.scalar
        def _(act):
            count = [0]

            def step(ins):
                count[0] += 1
                ins.then_inc(act_step, 1)
                act.wait_ge(act_step, count[0])

            def norm_root(n):
                act.wait_ge(ss_done, n + 1)
                act.activation(rstd[:, :], bank[6][:, 0:TT], ACT.Sqrt, bias=EPS_C, scale=1.0 / D)\
                   .then_inc(sd_done, 1)

            act.dma_start(lam[:, 0, :], s5_lam_re[0].rearrange("(i two) p -> i (two p)", two=2))\
               .then_inc(lam_in, 16)
            act.dma_start(lam[:, 1, :], s5_lam_im[0].rearrange("(i two) p -> i (two p)", two=2))\
               .then_inc(lam_in, 16)
            act.dma_start(lam[:, 14, 0:2], s5_log_dt[0].rearrange("(i two) -> i two", two=2))\
               .then_inc(lam_in, 16)
            act.dma_start(c_col[:, :], c[0].rearrange("(p t) -> p t", t=8)).then_inc(c_in, 16)
            act.wait_ge(lam_in, 48)
            act.activation(lam[:, 14, 0:2], lam[:, 14, 0:2], ACT.Exp).then_inc(dt_done, 1)
            act.dma_start(vec_b[CONV:CONV + 48, :], hy_conv_w[0].rearrange("j (b p) -> (j b) p", p=P))\
               .then_inc(vec_in, 16)
            act.dma_start(vec_b[NMIX:NMIX + 16, :], norm_mix_w.rearrange("l (k p) -> (l k) p", p=P))\
               .then_inc(vec_in, 16)
            act.dma_start(vec_b[NFFN:NFFN + 16, :], norm_ffn_w.rearrange("l (k p) -> (l k) p", p=P))\
               .then_inc(vec_in, 16)
            act.dma_start(vec_b[NFIN:NFIN + 8, :], final_norm_w.rearrange("(k p) -> k p", p=P))\
               .then_inc(vec_in, 16)
            act.dma_start(vec_b[S5D:S5D + 4, :], s5_d[0].rearrange("(k p) -> k p", p=P)).then_inc(vec_in, 16)
            act.dma_start(vec_b[GLUB:GLUB + 4, :], s5_glu_b[0].rearrange("(k p) -> k p", p=P))\
               .then_inc(vec_in, 16)
            act.dma_start(vec_b[HNW:HNW + 1, :], hy_head_norm_w).then_inc(vec_in, 16)
            act.dma_start(vec_a[:, :], ada_b.rearrange("l (k p) -> (l k) p", p=P)).then_inc(vec_in, 16)
            act.wait_ge(c_in, 16)
            act.activation(c_act[:, :], c_col[:, :], ACT.Silu).then_inc(c_ready, 1)
            for k in range(KT):
                act.wait_ge(x_t, k + 1)
                act.activation(h[:, k, :], bank[k % 4], ACT.Copy)
                if k > 0:
                    act.wait_ge(sq_added, k)
                act.activation(sq[:, :], bank[k % 4], ACT.Square).then_inc(x_done, 1)
            act.wait_ge(lam_exp, 1)
            act.activation(lam[:, 10, :], lam[:, 8, :], ACT.Sin)
            act.activation(lam[:, 11, :], lam[:, 7, :], ACT.Sin).then_inc(lam_trig, 1)
            norm_root(0)
            act.wait_ge(c_t, 1)
            for par in range(2):
                rows = slice(64 * par, 64 * par + 64)
                for dst, b, scale in ((c_re, 4, 1.0), (nc_re, 4, -1.0), (nc_im, 5, -1.0)):
                    src = bank[b].rearrange("p (i two h) -> p i two h", two=2, h=GH)[rows, :, par, :]
                    last = act.activation(dst[rows, :, :], src, ACT.Copy, scale=scale)
            last.then_inc(c_done, 1)
            act.wait_ge(ba_in, 16)
            act.activation(w_ba_hi[:, :, :], w_ba[:, :, :], ACT.Copy).then_inc(ba_split, 1)

            def hi(n, s, width=2048, first=False):
                act.wait_ge(raw_in[s], raw_value(n))
                if not first:
                    act.wait_ge(block_done, 2 * (n - 1))
                act.activation(whi[s][:, 0:width], raw[s][:, 0:width], ACT.Copy).then_inc(hi_done, 1)

            def hi_at(n0, i, per, s, width=2048):
                act.wait_ge(raw_in[s], 32 * (n0 // 2 + 1) + 16 * per * i)
                act.wait_ge(block_done, 2 * (n0 - 1) + 2 * per * i)
                act.activation(whi[s][:, 0:width], raw[s][:, 0:width], ACT.Copy).then_inc(hi_done, 1)

            def raw_value(n):
                return 32 * (n // 2 + 1)

            def norm_hi(n, shift, tiles=range(KT)):
                for k in tiles:
                    act.wait_ge(h_scaled, 8 * n + k + 1)
                    act.activation(hn_hi[:, k, :], tmp[k % 2][:, :], ACT.Identity,
                                   bias=mod[:, shift + k:shift + k + 1]).then_inc(hi_norm, 1)

            def norm(n, shift):
                norm_root(n)
                norm_hi(n, shift)

            def square(value, n, m, i=None):
                at_ = m if i is None else m + 4 * i
                act.wait_ge(block_free, value)
                act.wait_ge(sq_added, 8 * n + at_)
                act.activation(sq[:, :], h[:, at_, :], ACT.Square).then_inc(sq_done, 1)

            def powers():
                act.wait_ge(lam_t, 1)
                for dst, n0 in ((pw_re, 0), (pw_im, 8)):
                    act.activation(dst[:, 1:SC + 1, :],
                                   bank[4][:, 16 * n0:16 * n0 + 128].rearrange("p (k i) -> p k i", k=SC), ACT.Copy)
                act.activation(f_co[:, :, :], bank[4][:, 256:288].rearrange("p (k i) -> p k i", k=2),
                               ACT.Copy).then_inc(pw_done, 1)

            hi(0, 0, first=True)
            norm_hi(0, 0, range(3))
            powers()
            norm_hi(0, 0, range(3, KT))
            hi(1, 1, first=True)
            act.wait_ge(ba_rows, 1)
            act.activation(ba_row[:, :], bank[5][0:8, :], ACT.Copy).then_inc(ba_copied, 1)
            act.wait_ge(gdn_in, 32)
            act.activation(neg_a[:, :], neg_a[:, :], ACT.Exp).then_inc(neg_a_done, 1)
            for r in range(4):
                act.wait_ge(block_done, B_U + r + 1)
                act.activation(u_perm[:, r, :, :], perm(bank[r]), ACT.Copy).then_inc(block_free, 1)
                if r % 2:
                    hi(2 + r // 2, r // 2)
            for q in range(8):
                act.wait_ge(wt_t_done, q + 1)
                if q == 4:
                    act.wait_ge(u_out, 64)
                act.activation(w_in[:, q // 4, 4 * (q % 4):4 * (q % 4) + 4, :],
                               bank[4 + q % 2].rearrange("p (i m) -> p i m", i=4), ACT.Copy)\
                   .then_inc(w_done, 1)
            act.wait_ge(g_abs, 1)
            step(act.activation(g_t[0][:, :, :], g_t[0][:, :, :], ACT.Exp, scale=-1.0))
            act.activation(g_t[0][:, :, :], g_t[0][:, :, :], ACT.Ln, bias=ONE_C).then_inc(g_ln, 1)
            act.activation(beta[:, :, :], ba[:, :, 0:NH], ACT.Sigmoid).then_inc(beta_done, 1)
            act.wait_ge(m_zero, 1)
            for q in range(8):
                act.wait_ge(k_sum, q + 1)
                act.activation(m_pair[0:GH, 4 * (q // 2):4 * (q // 2) + 4, q % 2, :],
                               bank[4 + q % 2][0:GH, :].rearrange("p (g m) -> p g m", g=4), ACT.Copy)\
                   .then_inc(k_done, 1)
            act.wait_ge(gc_diff, 1)
            act.activation(gc_exp[:, :, :], gc[:, :, :], ACT.Exp)
            act.activation(k_fac[:, :, :], k_fac[:, :, :], ACT.Exp)
            act.activation(s_fac[:, :, :], s_fac[:, :, :], ACT.Exp).then_inc(gates, 1)
            for q in range(4):
                act.wait_ge(p_sum, q + 1)
                dst = (s_re, s_im)[q // 2]
                act.activation(dst[:, 8 * (q % 2):8 * (q % 2) + 8, :],
                               bank[4 + q].rearrange("p (i c) -> p i c", c=NC), ACT.Copy).then_inc(p_done, 1)
            act.preload_act_table(ACT.Silu)
            for i in range(3):
                def tap(r):
                    act.wait_ge(block_done, B_QKV + 4 * i + r + 1)
                    w3 = vb[:, CONV + 36 + r + 4 * i:CONV + 37 + r + 4 * i]
                    act.activation(conv[:, i, r, :], bank[r], ACT.Identity, scale=w3).then_inc(conv_tap, 1)

                def silu(r):
                    act.wait_ge(block_free, B_QKV + 4 * i + r + 1)
                    act.activation(conv[:, i, r, :], conv[:, i, r, :], ACT.Silu).then_inc(silu_done, 1)

                tap(0)
                tap(1)
                silu(0)
                hi_at(4, i, 2, 0)
                tap(2)
                silu(1)
                tap(3)
                silu(2)
                hi_at(5, i, 2, 1)
                silu(3)
            for q in range(4):
                act.wait_ge(y_sum, q + 1)
                act.activation(u_pair[:, 8 * (q % 2):8 * (q % 2) + 8, q // 2, :],
                               bank[4 + q].rearrange("p (g c) -> p g c", c=NC),
                               ACT.Copy).then_inc(y_done, 1)
            for r in range(4):
                act.wait_ge(block_done, B_Z + r + 1)
                act.activation(z_act[:, r, :], bank[r], ACT.Silu).then_inc(block_free, 1)
                if r % 2:
                    hi(10 + r // 2, r // 2, 1024)

            def drain(name, hd, dst, func=ACT.Copy):
                q, b, _ = gp(name, hd)
                act.wait_ge(gdn_done, q + 1)
                act.activation(dst[:, hd, :, :], bank[b].rearrange("p (c i) -> p c i", c=TT), func)\
                   .then_inc(drained[q % 4], 1)

            for hd in range(NH):
                for w_, name in enumerate(("q", "k")):
                    q, b, _ = gp(name, hd)
                    act.wait_ge(gdn_done, q + 1)
                    if hd > 0:
                        act.wait_ge(qk_red, 2 * hd - 1 + w_)
                    act.activation(tmp[w_][:, :], bank[b], ACT.Square).then_inc(qk_sq, 1)
                    drain(name, hd, (q_tok, k_tok)[w_])
                drain("v", hd, v_tok)
            act.wait_ge(qk_red, 2 * NH)
            act.activation(qk_rn[:, :, :, :], qk_ss[:, :, :, :], ACT.Sqrt, bias=EPS_C).then_inc(qk_root, 1)
            for hd in range(NH):
                drain("kT", hd, kT)
                drain("qT", hd, qT)
                drain("bT", hd, bT)
            for hd in range(NH):
                wait_drained(act, "gr", hd)
                act.activation(dec[:, hd, :, :], dec[:, hd, :, :], ACT.Exp).then_inc(dec_exp, 1)
            act.wait_ge(y_du, 1)
            step(act.activation(y_s5[:, :, :, :], y_s5[:, :, :, :], ACT.Gelu_apprx_tanh))
            act.activation(ys_hi[:, :, :], y_s5[:, :, :, :].rearrange("p k j c -> p k (j c)"), ACT.Copy)\
               .then_inc(ys_hi_done, 1)
            for hd in range(NH):
                drain("dT", hd, qdT)
            for r in range(4):
                act.wait_ge(block_done, B_GLU + r + 1)
                if r >= 2:
                    act.wait_ge(glu_mul, r - 1)
                act.activation(tmp[r % 2][:, :], bank[r], ACT.Sigmoid,
                               bias=vb[:, GLUB + r:GLUB + r + 1]).then_inc(block_free, 1)
            for hd in range(NH):
                drain("d2", hd, Db)
                drain("d2t", hd, DbT)
            for hd in range(NH):
                drain("d4", hd, Da)
            for hd in range(NH):
                drain("d8t", hd, DbT)
            for r in range(4):
                act.wait_ge(glu_mul, r + 1)
                act.activation(perm(ys_hi[:, r, :]), y_s5[:, r, :, :], ACT.Copy).then_inc(glu_hi, 1)
            for hd in range(NH):
                drain("xt", hd, XT)
            hi(12, 0)
            hi(13, 1)
            for hd in range(NH):
                drain("u", hd, vn)
                drain("w", hd, wT)
            for hd in range(NH):
                act.wait_ge(o_done, hd + 1)
                if hd >= 2:
                    act.wait_ge(o_red, hd - 1)
                act.activation(tmp_o[hd % 2][:, :], bank[hd], ACT.Square).then_inc(o_sq_done, 1)
            act.wait_ge(o_red, NH)
            act.activation(o_rn[:, :, :], o_ss[:, :, :], ACT.Sqrt, bias=EPS_C, scale=1.0 / P)\
               .then_inc(o_root, 1)
            for hd in range(NH):
                act.wait_ge(oz_done, hd + 1)
                act.activation(mo_hi[:, hd, :], o_z[:, hd, :], ACT.Copy).then_inc(mo_hi_done, 1)

            def residual_blocks(unit, slot, n):
                with act.Fori(0, 2) as i:
                    for r in range(4):
                        if r % 2:
                            hi_at(slot + 2 + r // 2, i, 2, r // 2)
                        square(unit + 4 * i + r + 1, n, r, i)

            residual_blocks(B_OUT0, 12, 1)
            norm(1, 24)

            def ffn(layer, slot, unit, n):
                act.preload_act_table(ACT.Silu)
                hidden = FT * layer
                for half, n_f in enumerate(HALVES):
                    with act.Fori(0, n_f // 2) as i:
                        for s in range(2):
                            m = hidden + 2 * i + s
                            act.wait_ge(block_done, unit + 4 * i + 2 * s + 1)
                            act.activation(tmp[0][:, :], bank[2 * s], ACT.Silu).then_inc(gate_act, 1)
                            hi_at(slot + 2 + s, i, 2, s)
                            act.wait_ge(up_mul, m + 1)
                            act.activation(ff_hi[:, 2 * i + s, :], tmp[1][:, :], ACT.Copy)\
                               .then_inc(ff_hi_done, 1)
                    slot, unit, hidden = slot + n_f, unit + 2 * n_f, hidden + n_f
                    final = layer == 1 and half == 1

                    def body(i, last=False):
                        for s in range(4):
                            if not (last and s >= 2):
                                hi_at(slot + 2 + s, i, 4, s % 2, n_f * P if s < 2 else 2048)
                            if half == 1:
                                square(unit + 8 * i + 2 * s + 2, n + 1, s, i)
                    if final:
                        body(0)
                        body(1, True)
                    else:
                        with act.Fori(0, 2) as i:
                            body(i)
                    slot, unit = slot + 8, unit + 16

            ffn(0, 16, B_FF0, 1)
            act.activation(ones_r[:, :], ones[:, :], ACT.Copy)
            act.activation(ident_r[:, :], ident[:, :], ACT.Copy)
            act.activation(below_r[:, :], below[:, :], ACT.Copy)
            act.activation(tril_r[:, :], tril[:, :], ACT.Copy).then_inc(cons_r, 1)
            norm(2, 48)

            def projected(p_, m):
                kind, j, n = m // 2, m % 2, 2 * (p_ % 2)
                act.wait_ge(block_done, B_SB + 6 * p_ + m + 1)
                if kind < 2:
                    act.activation(sb_qk[:, kind, n + j, :], bank[7 - j], ACT.Copy,
                                   scale=float(P) ** -0.5 if kind == 0 else 1.0).then_inc(block_free, 1)
                else:
                    act.activation(sb_v[:, 2 * j:2 * j + 2, n:n + 2, :],
                                   bank[7 - j].rearrange("p (t h d) -> p t h d", t=2, h=2), ACT.Copy)\
                       .then_inc(block_free, 1)

            def next_hi(p_, kind):
                if p_ < 4:
                    n = 56 + 3 * p_ + kind
                    hi(n, n % 2)

            def scores(hd):
                act.wait_ge(sbz, hd + 1)
                if hd >= 2:
                    act.wait_ge(sb_w, hd - 1)
                act.activation(zb[hd % 2][:, :], flat[:, 0:1280], ACT.Copy).then_inc(sbz_done, 1)
                act.wait_ge(sb_abs, hd + 1)
                act.activation(e_b[:, :], e_b[:, :], ACT.Exp).then_inc(sbe, 1)
                act.wait_ge(sbe, hd + 1)
                act.activation(e_b[:, :], e_b[:, :], ACT.Ln, bias=ONE_C).then_inc(sb_spe, 1)

            def softplus_hi(hd):
                act.wait_ge(sb_sp, hd + 1)
                if hd > 0:
                    act.wait_ge(sb_c, hd)
                act.activation(sp_hi[:, :], e_b[:, :], ACT.Copy).then_inc(sb_hi, 1)

            def weights_of(hd):
                act.wait_ge(sb_w, hd + 1)
                act.activation(w_b[:, :], w_b[:, :], ACT.Exp).then_inc(sb_p, 1)

            def out_hi(hd):
                act.wait_ge(sb_o, hd + 1)
                act.activation(ff_hi[:, hd, :], bank[hd % 2], ACT.Copy).then_inc(sbo_hi, 1)

            for m in range(6):
                projected(0, m)
                if m % 2:
                    next_hi(0, m // 2)
            for p_ in range(4):
                def fill(m):
                    if p_ < 3:
                        projected(p_ + 1, m)
                a, b = 2 * p_, 2 * p_ + 1
                fill(0)
                scores(a)
                fill(1)
                softplus_hi(a)
                scores(b)
                next_hi(p_ + 1, 0)
                fill(2)
                softplus_hi(b)
                weights_of(a)
                fill(3)
                next_hi(p_ + 1, 1)
                fill(4)
                out_hi(a)
                weights_of(b)
                fill(5)
                next_hi(p_ + 1, 2)
                out_hi(b)
            residual_blocks(B_OUT1, 66, 3)
            norm(3, 72)
            ffn(1, 70, B_FF1, 3)
            norm_root(4)
            for k in range(KT):
                act.wait_ge(fin_t, k + 1)
                act.activation(out_tok[:, :, k * P:(k + 1) * P],
                               bank[k % 4].rearrange("p (t f) -> p t f", t=TT), ACT.Copy)\
                   .then_inc(fin_copied, 1)

        @block.vector
        def _(dve):
            count = [0]

            def step(ins):
                count[0] += 1
                ins.then_inc(dve_step, 1)
                dve.wait_ge(dve_step, count[0])

            TTO, TS, STT = dve.tensor_tensor, dve.tensor_scalar, dve.scalar_tensor_tensor
            MUL, ADD, SUB, MAX, MIN = ALU.mult, ALU.add, ALU.subtract, ALU.max, ALU.min

            dve.memset(sq_sum[:, :], 0.0).then_inc(dve_step, 1)
            count[0] += 1

            def L(i):
                return lam[:, i, :]

            dve.wait_ge(dt_done, 1)
            dt_bc = lam[:, 14, 0:2].unsqueeze(2).to_broadcast([16, 2, GP])
            for src, dst in ((0, 2), (1, 3)):
                step(TTO(L(dst).rearrange("i (two p) -> i two p", two=2),
                         L(src).rearrange("i (two p) -> i two p", two=2), dt_bc, MUL))
            step(TS(L(2), L(2), -87.0, 87.0, MAX, MIN))
            step(TS(L(4), L(2), 1.0 / float(np.log(2)), ROUND, MUL, ADD))
            step(TS(L(4), L(4), ROUND, None, SUB))
            step(STT(L(5), L(4), -LN2_1, L(2), MUL, ADD))
            step(STT(L(5), L(4), -LN2_2, L(5), MUL, ADD))
            step(TS(L(6), L(5), 1.0 / 7, 1.0, MUL, ADD))
            for n in range(6, 0, -1):
                step(STT(L(6), L(6), 1.0 / n, L(5), MUL, MUL))
                step(TS(L(6), L(6), 1.0, None, ADD))
            step(TS(L(7).bitcast(I32), L(4), 127.0, 8388608.0, ADD, MUL))
            step(TTO(L(6), L(6), L(7), MUL))
            step(TS(L(4), L(3), 1.0 / TWO_PI, ROUND, MUL, ADD))
            step(TS(L(4), L(4), ROUND, None, SUB))
            step(STT(L(5), L(4), -PI_1, L(3), MUL, ADD))
            step(STT(L(5), L(4), -PI_2, L(5), MUL, ADD))
            step(STT(L(5), L(4), -PI_3, L(5), MUL, ADD))
            step(TS(L(8), L(5), -PI_BELOW, PI_BELOW, MAX, MIN))
            step(TS(L(7), L(5), float(np.pi / 2), None, ADD))
            step(TS(L(9), L(7), PI_BELOW, TWO_PI, ALU.is_gt, MUL))
            step(TTO(L(7), L(7), L(9), SUB))
            TS(L(7), L(7), -PI_BELOW, PI_BELOW, MAX, MIN).then_inc(lam_exp, 1)
            step(TTO(L(9), L(0), L(0), MUL))
            step(TTO(L(4), L(1), L(1), MUL))
            step(TTO(L(9), L(9), L(4), ADD))
            dve.reciprocal(L(9), L(9)).then_inc(lam_recip, 1)
            def ada0_tile(part, t):
                n = 8 * part + t
                acc = ada0_acc[part % 2]
                if n == 0:
                    dve.wait_ge(c_ready, 1)
                if t == 0 and part % 2 == 0 and part > 0:
                    dve.wait_ge(mod_sum, part // 2)
                if n < 16:
                    dve.wait_ge(first_ld[n // 4], 16)
                    src = ada_first[n // 4][:, n % 4, :]
                else:
                    dve.wait_ge(ada0_ld[n % 2], 16 * (n // 2 - 7))
                    src = ada0_in[n % 2][:, :]
                if t == 0:
                    TS(acc[:, :], src, c_act[:, t:t + 1], None, MUL).then_inc(ada_used, 1)
                else:
                    dve.wait_ge(ada_used, n)
                    STT(acc[:, :], src, c_act[:, t:t + 1], acc[:, :], MUL, ADD)\
                        .then_inc(ada_used, 1)

            def mod_parts(n, part, parts=2):
                dve.wait_ge(mod_sum, n + 1)
                c_ = slice(8 * part, 8 * (part + parts))
                TTO(mod[:, c_], bank[7][:, c_], ada_bias[:, c_], ADD).then_inc(mod_done, 1)

            def add_square(n, k):
                dve.wait_ge(sq_done if n else x_done, (8 * (n - 1) + k + 1) if n else k + 1)
                TTO(sq_sum[:, :], sq_sum[:, :], sq[:, :], ADD).then_inc(sq_added, 1)

            def lo(n, s, width=2048):
                dve.wait_ge(hi_done, n + 1)
                TTO(wlo[s][:, 0:width], raw[s][:, 0:width], whi[s][:, 0:width].bitcast(F32), SUB)\
                    .then_inc(lo_done, 1)

            def norm_diag(n):
                dve.wait_ge(sd_done, n + 1)
                step(dve.reciprocal(rstd[:, :], rstd[:, :]))
                for c_ in range(TT):
                    last = TS(diag[:, c_, :], ident[:, :], rstd[:, c_:c_ + 1], None, MUL)
                last.then_inc(diag_done, 1)

            def norm_apply(n, scale_w, shift):
                if n < 4:
                    dve.memset(sq_sum[:, :], 0.0)
                    dve.wait_ge(mod_done, (1, 3, 4, 5)[n])
                    step(STT(n_scale[:, :], mod[:, shift + 8:shift + 16], 1.0, vb[:, scale_w:scale_w + 8],
                             ADD, MUL))
                dve.wait_ge(rb_done, n + 1)

                def scaled(k):
                    if n == 4:
                        if k >= 2:
                            dve.wait_ge(fin_t, k - 1)
                        w_ = vb[:, scale_w + k:scale_w + k + 1]
                    else:
                        if k >= 2:
                            dve.wait_ge(hn_done, 8 * n + k - 1)
                        w_ = n_scale[:, k:k + 1]
                    STT(tmp[k % 2][:, :], h[:, k, :], w_, bank[6], MUL, MUL).then_inc(h_scaled, 1)

                def rest(k):
                    dve.wait_ge(hi_norm, 8 * n + k + 1)
                    STT(hn_lo[:, k, :], tmp[k % 2][:, :], mod[:, shift + k:shift + k + 1],
                        hn_hi[:, k, :].bitcast(F32), ADD, SUB).then_inc(hn_done, 1)

                for k in range(KT):
                    scaled(k)
                    if n < 4 and k >= 1:
                        rest(k - 1)
                if n < 4:
                    rest(KT - 1)

            def norm(n, scale_w, shift):
                norm_diag(n)
                norm_apply(n, scale_w, shift)

            for k in range(KT):
                add_square(0, k)
                ada0_tile(0, k)
            for t in range(4):
                ada0_tile(1, t)
            norm_diag(0)
            dve.wait_ge(vec_t, 1)
            dve.tensor_copy(ada_bias[:, :], bank[7][:, 96:192])
            dve.tensor_copy(vb[:, :], bank[7][:, 192:289]).then_inc(vec_ready, 1)
            for t in range(4, 8):
                ada0_tile(1, t)
            dve.wait_ge(ba_split, 1)
            TTO(w_ba_lo[:, :, :], w_ba[:, :, :], w_ba_hi[:, :, :].bitcast(F32), SUB).then_inc(ba_split, 1)
            lo(0, 0)
            mod_parts(0, 0)
            norm_apply(0, NMIX, 0)
            lo(1, 1)
            dve.wait_ge(pw_done, 1)
            dve.wait_ge(bc_in, 16 * 8)
            f_re = f_co[:, 0, :].unsqueeze(2).to_broadcast([P, PAIRS, GH])
            f_im = f_co[:, 1, :].unsqueeze(2).to_broadcast([P, PAIRS, GH])
            t0 = bb_t[:, :, :]
            step(TTO(t0, b_im[:, :, :], f_im, MUL))
            step(TTO(bb_re[:, :, :], b_re[:, :, :], f_re, MUL))
            step(TTO(bb_re[:, :, :], bb_re[:, :, :], t0, SUB))
            step(TTO(t0, b_re[:, :, :], f_im, MUL))
            step(TTO(bb_im[:, :, :], b_im[:, :, :], f_re, MUL))
            TTO(bb_im[:, :, :], bb_im[:, :, :], t0, ADD).then_inc(bb_done, 1)
            pr = pw_re[:, 0:SC, :][:, ::-1, :].rearrange("p k i -> p i k")
            pi = pw_im[:, 0:SC, :][:, ::-1, :].rearrange("p k i -> p i k")
            dve.wait_ge(c_t, 1)
            dve.wait_ge(pw0_done, 1)
            dve.wait_ge(bb_done, 1)
            for part, (a_, b_, dst, op) in enumerate(((pr, pi, wt_re, SUB), (pi, pr, wt_im, ADD))):
                if part:
                    dve.wait_ge(wt_done, 1)
                for half in range(2):
                    ii = slice(8 * half, 8 * half + 8)

                    def b4(x_):
                        return x_[:, ii, :].unsqueeze(2).to_broadcast([P, 8, SC, GH])

                    def p4(x_):
                        return x_[:, ii, :].unsqueeze(3).to_broadcast([P, 8, SC, GH])

                    d_ = dst[:, ii, :, :]
                    t_ = wt_t[:, :].rearrange("p (i j h) -> p i j h", i=8, j=SC)
                    step(TTO(t_, b4(bb_im), p4(b_), MUL))
                    step(TTO(d_, b4(bb_re), p4(a_), MUL))
                    last = TTO(d_, d_, t_, op)
                    if half == 0:
                        step(last)
                last.then_inc(wt_done, 1)
            dve.wait_ge(ba_sum, 1)
            step(dve.tensor_copy(ba[:, :, :], bank[7][:, 300:332].rearrange("p (c n) -> p c n", c=TT)))
            dve.wait_ge(gdn_in, 32)
            dve.wait_ge(neg_a_done, 1)
            a4 = ba[:, :, NH:2 * NH]
            step(TTO(a4, a4, dt_b[:, :].unsqueeze(1).to_broadcast([P, TT, NH]), ADD))
            step(TS(g_t[0][:, :, :], a4, -1.0, None, MUL))
            TTO(g_t[0][:, :, :], g_t[0][:, :, :], a4, MAX).then_inc(g_abs, 1)
            lo(2, 0)
            lo(3, 1)
            dve.wait_ge(g_ln, 1)
            step(STT(g_t[1][:, :, :], a4, 0.0, g_t[0][:, :, :], MAX, ADD))
            STT(g_log[:, :, :], g_t[1][:, :, :], -1.0,
                neg_a[:, :].unsqueeze(1).to_broadcast([P, TT, NH]), MUL, MUL).then_inc(g_done, 1)
            dve.wait_ge(gc_sum, 1)
            step(dve.tensor_copy(gc[:, :, :], bank[7][:, 340:356].rearrange("p (c n) -> p c n", c=TT)))
            dve.tensor_copy(s_fac[:, :, :], bank[7][:, 356:372].rearrange("p (c n) -> p c n", c=TT))
            TTO(k_fac[:, :, :], bank[7][:, 356:372].rearrange("p (c n) -> p c n", c=TT), gc[:, :, :], SUB)\
                .then_inc(gc_diff, 1)
            for t in range(4):
                ada0_tile(2, t)
            for i in range(3):
                for r in range(4):
                    dve.wait_ge(conv_tap, 4 * i + r + 1)
                    for s in range(1, 4):
                        w_ = CONV + 12 * (3 - s) + 4 * i + r
                        d_ = conv[:, i, r, s:T]
                        last = STT(d_, bank[r][:, 0:T - s], vb[:, w_:w_ + 1], d_, MUL, ADD)
                        if s < 3:
                            step(last)
                    last.then_inc(block_free, 1)
                    if r == 1:
                        lo(4 + 2 * i, 0)
                    if r == 3:
                        lo(5 + 2 * i, 1)
                    if i == 0:
                        ada0_tile(2, 4 + r)
                    elif i == 1:
                        ada0_tile(3, 2 * r)
                        ada0_tile(3, 2 * r + 1)
            mod_parts(1, 2)
            for part in range(4, 6):
                for t in range(8):
                    ada0_tile(part, t)
            mod_parts(2, 4)
            dve.wait_ge(y_in, 64)
            dve.wait_ge(u2_in, 64)
            for r in range(4):
                last = STT(y_s5[:, r, :, :], u_again[:, r, :, :], vb[:, S5D + r:S5D + r + 1],
                           y_s5[:, r, :, :], MUL, ADD)
            last.then_inc(y_du, 1)
            lo(10, 0, 1024)
            lo(11, 1, 1024)

            def product(name, hd):
                q, b, _ = gp(name, hd)
                dve.wait_ge(gdn_done, q + 1)
                return bank[b].rearrange("p (c i) -> p c i", c=TT), drained[q % 4]

            for hd in range(NH):
                for w_ in range(2):
                    dve.wait_ge(qk_sq, 2 * hd + w_ + 1)
                    dve.tensor_reduce(qk_ss[:, w_, hd, :], tmp[w_][:, :].rearrange("p (c i) -> p c i", c=TT),
                                      AX.X, ADD).then_inc(qk_red, 1)
            dve.wait_ge(qk_root, 1)
            step(dve.reciprocal(qk_rn[:, :, :, :], qk_rn[:, :, :, :]))
            step(TS(qk_rn[:, 0, :, :], qk_rn[:, 0, :, :], float(P) ** -0.5, None, MUL))

            def col(t_, hd):
                return bc(t_[:, :, hd], P)

            dve.wait_ge(gates, 1)
            dve.wait_ge(beta_done, 1)
            for hd in range(NH):
                wait_drained(dve, "v", hd)
                TTO(k_tok[:, hd, :, :], k_tok[:, hd, :, :], bc(qk_rn[:, 1, hd, :], P), MUL).then_inc(kn_done, 1)
                TTO(q_tok[:, hd, :, :], q_tok[:, hd, :, :], bc(qk_rn[:, 0, hd, :], P), MUL).then_inc(qn_done, 1)
                dve.wait_ge(kn_done, hd + 1)
                TTO(kb_tok[:, hd, :, :], k_tok[:, hd, :, :], col(beta, hd), MUL).then_inc(kb_done, 1)
                TTO(v_tok[:, hd, :, :], v_tok[:, hd, :, :], col(beta, hd), MUL).then_inc(rv_done, 1)
            for hd in range(NH):
                src, free = product("gr", hd)
                dve.wait_ge(kd_done, hd + 1)
                wait_drained(dve, "kT", hd)
                for c_ in range(TT):
                    last = TS(dec[:, hd, c_, :], src[:, c_, :], gc[:, c_, hd:hd + 1], 0.0, SUB, MIN)
                last.then_inc(free, 1)
            for name, done, dst in (("at", dec_done, attnT), ("lt", dec_done, LT)):
                for hd in range(NH):
                    src, free = product(name, hd)
                    dve.wait_ge(done, hd + 1)
                    TTO(dst[:, hd, :, :], src, dec[:, hd, :, :], MUL).then_inc(free, 1)
            dve.wait_ge(ys_hi_done, 1)
            TTO(ys_lo[:, :, :], y_s5[:, :, :, :].rearrange("p k j c -> p k (j c)"),
                ys_hi[:, :, :].bitcast(F32), SUB).then_inc(ys_done, 1)
            for hd in range(NH):
                src, free = product("l", hd)
                TTO(Da[:, hd, :, :], src, bd16[:, :].unsqueeze(1).to_broadcast([P, TT, P]), MUL)\
                    .then_inc(free, 1)
                wait_drained(dve, "l", hd)
                TTO(X[:, hd, :, :], ident[:, :].unsqueeze(1).to_broadcast([P, TT, P]), Da[:, hd, :, :], SUB)\
                    .then_inc(x0_done, 1)

            def onto(name, dst, op):
                for hd in range(NH):
                    src, free = product(name, hd)
                    TTO(dst[:, hd, :, :], dst[:, hd, :, :], src, op).then_inc(free, 1)

            for r in range(4):
                dve.wait_ge(block_free, B_GLU + r + 1)
                TTO(y_s5[:, r, :, :], y_s5[:, r, :, :], tmp[r % 2][:, :].rearrange("p (j c) -> p j c", j=SC),
                    MUL).then_inc(glu_mul, 1)
            onto("x1", X, ADD)
            for hd in range(NH):
                src, free = product("d4t", hd)
                dve.tensor_copy(DaT[:, hd, :, :], src).then_inc(free, 1)
            onto("x2", X, ADD)
            onto("x3", X, ADD)
            for lv in range(3):
                for hd in range(NH):
                    src, free = product(f"z{lv}", hd)
                    TTO(Z[:, hd, :, :], src, level[lv][:, :].unsqueeze(1).to_broadcast([P, TT, P]), MUL)\
                        .then_inc(free, 1)
                if lv == 0:
                    for r in range(4):
                        dve.wait_ge(glu_hi, r + 1)
                        TTO(perm(ys_lo[:, r, :]), y_s5[:, r, :, :], perm(ys_hi[:, r, :].bitcast(F32)), SUB)\
                            .then_inc(mix_s5, 1)
                if lv < 2:
                    onto(f"xc{lv}", X, SUB)
                onto(f"xtc{lv}", XT, SUB)
                if lv < 2:
                    lo(12 + lv, lv)
            for c_ in range(TT):
                if c_ > 0:
                    for hd in range(NH):
                        q, b, _ = gp(f"ws{c_}", hd)
                        dve.wait_ge(gdn_done, q + 1)
                        TTO(vn[:, hd, c_, :], vn[:, hd, c_, :], bank[b][:, 0:P], SUB).then_inc(drained[q % 4], 1)
                if c_ < TT - 1:
                    for hd in range(NH):
                        q, b, _ = gp(f"s{c_}", hd)
                        dve.wait_ge(gdn_done, q + 1)
                        if c_ == 0:
                            dve.tensor_copy(S[:, hd, :], bank[b][:, 0:P]).then_inc(drained[q % 4], 1)
                        else:
                            STT(S[:, hd, :], S[:, hd, :], s_fac[:, c_, hd:hd + 1], bank[b][:, 0:P], MUL, ADD)\
                                .then_inc(drained[q % 4], 1)
            for hd in range(NH):
                dve.wait_ge(o_sq_done, hd + 1)
                dve.tensor_reduce(o_ss[:, hd, :], tmp_o[hd % 2][:, :].rearrange("p (c i) -> p c i", c=TT),
                                  AX.X, ADD).then_inc(o_red, 1)
            dve.wait_ge(o_root, 1)
            step(dve.reciprocal(o_rn[:, :, :], o_rn[:, :, :]))
            for hd in range(NH):
                TTO(o_n[:, hd, :, :], bank[hd].rearrange("p (c i) -> p c i", c=TT), bc(o_rn[:, hd, :], P), MUL)\
                    .then_inc(on_done, 1)
            for hd in range(NH):
                q, b, _ = gp("oT", hd)
                dve.wait_ge(gdn_done, q + 1)
                STT(o_z[:, hd, :], bank[b], vb[:, HNW:HNW + 1], z_act[:, hd, :], MUL, MUL).then_inc(oz_done, 1)
            for hd in range(NH):
                dve.wait_ge(mo_hi_done, hd + 1)
                TTO(mo_lo[:, hd, :], o_z[:, hd, :], mo_hi[:, hd, :].bitcast(F32), SUB).then_inc(mo_done, 1)

            def residual(value, b, gate, m, units=1):
                dve.wait_ge(block_done, value)
                STT(h[:, m, :], bank[b], mod[:, bass.ds(gate + m, 1)], h[:, m, :], MUL, ADD)\
                    .then_inc(block_free, units)

            def residual_blocks(unit, slot, n, gate, banks_of=(0, 1, 2, 3)):
                with dve.Fori(0, 2) as i:
                    for r in range(4):
                        m = 4 * i + r
                        residual(unit + 4 * i + r + 1, banks_of[r], gate, m)
                        if r % 2:
                            lo(slot + 2 + r // 2 + 2 * i, r // 2)
                        add_square(n, m)

            residual_blocks(B_OUT0, 12, 1, 16)
            norm(1, NFFN, 24)

            def ffn(layer, slot, unit, n, gate):
                hidden = FT * layer
                for half, n_f in enumerate(HALVES):
                    if layer == 0:
                        if half == 1:
                            dve.wait_ge(mod_sum, 4)
                        step(dve.memset(ada1_acc[:, :], 0.0))

                    def hidden_tiles(i, with_ada):
                        for s in range(2):
                            m = hidden + 2 * i + s
                            dve.wait_ge(block_done, unit + 4 * i + 2 * s + 2)
                            dve.wait_ge(gate_act, m + 1)
                            dve.wait_ge(block_free, unit + 4 * i + 2 * s)
                            TTO(tmp[1][:, :], tmp[0][:, :], bank[2 * s + 1], MUL).then_inc(up_mul, 1)
                            lo(slot + 2 + 2 * i + s, s)
                            dve.wait_ge(ff_hi_done, m + 1)
                            TTO(ff_lo[:, 2 * i + s, :], tmp[1][:, :], ff_hi[:, 2 * i + s, :].bitcast(F32), SUB)\
                                .then_inc(block_free, 2)
                            if with_ada:
                                dve.wait_ge(ada1_ld[s], 64 * half + 16 * i)
                                dve.wait_ge(ada_used, 46 + 8 * half + s + 2 * i)
                                STT(ada1_acc[:, :], ada1_in[s][:, :], c_act[:, bass.ds(i * 2 + (s - 2), 1)],
                                    ada1_acc[:, :], MUL, ADD).then_inc(ada_used, 1)

                    ada_steps(dve, layer, n_f, hidden_tiles)
                    slot, unit, hidden = slot + n_f, unit + 2 * n_f, hidden + n_f
                    if layer == 0 and half == 0:
                        mod_parts(3, 6, 3)

                    def body(i, last=False):
                        for s in range(4):
                            m = 4 * i + s
                            residual(unit + 8 * i + 2 * s + 2, s, gate, m, units=2)
                            if not (last and s >= 2):
                                lo(slot + 2 + s + 4 * i, s % 2, n_f * P if s < 2 else 2048)
                            if half == 1:
                                add_square(n + 1, m)
                    if layer == 1 and half == 1:
                        body(0)
                        body(1, True)
                    else:
                        with dve.Fori(0, 2) as i:
                            body(i)
                    slot, unit = slot + 8, unit + 16

            ffn(0, 16, B_FF0, 1, 40)
            norm_diag(2)
            mod_parts(4, 9, 3)
            norm_apply(2, NMIX + 8, 48)

            def scores(hd):
                dve.wait_ge(sbz_done, hd + 1)
                if hd > 0:
                    dve.wait_ge(sb_lo, hd)
                STT(e_b[:, :], zb[hd % 2][:, :], -1.0, zb[hd % 2][:, :], MUL, MIN).then_inc(sb_abs, 1)
                dve.wait_ge(sb_spe, hd + 1)
                STT(e_b[:, :], zb[hd % 2][:, :], 0.0, e_b[:, :], MAX, ADD).then_inc(sb_sp, 1)

            def softplus_lo(hd):
                dve.wait_ge(sb_hi, hd + 1)
                TTO(sp_lo[:, :], e_b[:, :], sp_hi[:, :].bitcast(F32), SUB).then_inc(sb_lo, 1)

            def exponents(hd):
                dve.wait_ge(sb_c, hd + 1)
                if hd > 0:
                    dve.wait_ge(sb_o, hd)
                TTO(w_b[:, :], zb[hd % 2][:, :], flat[:, 3 * T:3 * T + 1280], SUB).then_inc(sb_w, 1)

            def out_lo(hd):
                dve.wait_ge(sbo_hi, hd + 1)
                TTO(ff_lo[:, hd, :], bank[hd % 2], ff_hi[:, hd, :].bitcast(F32), SUB).then_inc(sbo_done, 1)

            def next_lo(p_, kind):
                if p_ < 4:
                    n = 56 + 3 * p_ + kind
                    lo(n, n % 2)

            for kind in range(3):
                next_lo(0, kind)
            for p_ in range(4):
                a, b = 2 * p_, 2 * p_ + 1
                scores(a)
                softplus_lo(a)
                scores(b)
                next_lo(p_ + 1, 0)
                exponents(a)
                softplus_lo(b)
                next_lo(p_ + 1, 1)
                exponents(b)
                out_lo(a)
                next_lo(p_ + 1, 2)
                out_lo(b)
            residual_blocks(B_OUT1, 66, 3, 64, (7, 6, 7, 6))
            norm(3, NFFN + 8, 72)
            ffn(1, 70, B_FF1, 3, 88)
            norm(4, NFIN, None)

        @block.gpsimd
        def _(pool):
            count = [0]

            def step(ins):
                count[0] += 1
                ins.then_inc(pool_step, 1)
                pool.wait_ge(pool_step, count[0])

            MUL, ADD, SUB = ALU.mult, ALU.add, ALU.subtract

            def select(ap, pattern, start, mult, op=ALU.is_ge, fill=0.0):
                return pool.affine_select(out=ap, in_=ap, compare_op=op, fill=fill, base=start,
                                          pattern=pattern, channel_multiplier=mult)

            pool.memset(EPS_C, EPS)
            pool.memset(ONE_C, 1.0)
            pool.memset(ones[:, :], 1.0)
            step(pool.memset(ident[:, :], 0.0))
            select(ident[:, :], [[-1, P]], 0, 1, ALU.not_equal, 1.0).then_inc(consts, 1)
            pool.memset(below[:, :], 0.0)
            for m_ in (triu, tril, bd16, level[0], level[1]):
                last = pool.memset(m_[:, :], 1.0)
            step(last)
            select(triu[:, :], [[1, P]], 0, -1)
            select(below[:, :], [[1, P]], -1, -1, fill=-1e30)
            select(tril[:, :], [[-1, P]], 0, 1)
            for m_, w_ in ((bd16, 16), (level[0], 32), (level[1], 64)):
                v = m_[:, :].rearrange("p (b x) -> p b x", x=w_)
                step(select(v, [[-w_, P // w_], [0, w_]], 0, 1))
                step(select(v, [[w_, P // w_], [0, w_]], w_ - 1, -1))
            step(pool.tensor_tensor(level[2][:, :], ones[:, :], level[1][:, :], SUB))
            step(pool.tensor_tensor(level[1][:, :], level[1][:, :], level[0][:, :], SUB))
            step(pool.tensor_tensor(level[0][:, :], level[0][:, :], bd16[:, :], SUB))
            pool.memset(pw_re[:, 0, :], 1.0)
            pool.memset(pw_im[:, 0, :], 0.0).then_inc(pw0_done, 1)
            pool.wait_ge(pw0_done, 1)
            for par in range(2):
                rows = slice(64 * par, 64 * par + 64)
                for dst, src in ((b_re, s5_b_re), (b_im, s5_b_im)):
                    pool.dma_start(dst[rows, :, :], src[0].rearrange("(i two) p h -> two p i h", two=2)[par])\
                        .then_inc(bc_in, 16)
            for part, src in enumerate((s5_c_re, s5_c_im)):
                rows = src[0].rearrange("(q g) h p -> (g h) q p", q=4)
                for two in range(2):
                    pool.dma_start(c_raw[:, part, :, 64 * two:64 * two + 64], rows).then_inc(bc_in, 16)
            pool.dma_start(w_ba[:, :, :], hy_w_in[0][:, 4 * W:4 * W + 8].rearrange("(k p) n -> p k n", p=P))\
                .then_inc(ba_in, 16)
            pool.dma_start(neg_a[:, :], hy_a_log.to_broadcast([P, NH]))\
                .then_inc(gdn_in, 16)
            pool.dma_start(dt_b[:, :], hy_dt_bias.to_broadcast([P, NH])).then_inc(gdn_in, 16)


            def L(i):
                return lam[:, i, :]

            pool.wait_ge(lam_trig, 1)
            pool.wait_ge(lam_recip, 1)
            step(pool.tensor_tensor(L(16), L(6), L(11), MUL))
            step(pool.tensor_tensor(L(24), L(6), L(10), MUL))
            step(pool.tensor_tensor(L(5), L(16), ones[0:16, :], SUB))
            step(pool.tensor_tensor(L(7), L(5), L(0), MUL))
            step(pool.tensor_tensor(L(8), L(24), L(1), MUL))
            step(pool.tensor_tensor(L(7), L(7), L(8), ADD))
            step(pool.tensor_tensor(L(12), L(7), L(9), MUL))
            step(pool.tensor_tensor(L(7), L(24), L(0), MUL))
            step(pool.tensor_tensor(L(8), L(5), L(1), MUL))
            step(pool.tensor_tensor(L(7), L(7), L(8), SUB))
            step(pool.tensor_tensor(L(13), L(7), L(9), MUL))

            for src, by, dst, n in ((0, 0, 1, 1), (0, 1, 2, 2), (0, 3, 4, 4)):
                ar, ai = lam[:, 16 + src:16 + src + n, :], lam[:, 24 + src:24 + src + n, :]
                br = lam[:, 16 + by:17 + by, :].to_broadcast([16, n, P])
                bi = lam[:, 24 + by:25 + by, :].to_broadcast([16, n, P])
                dr, di = lam[:, 16 + dst:16 + dst + n, :], lam[:, 24 + dst:24 + dst + n, :]
                t0 = lam[:, 0:n, :]
                step(pool.tensor_tensor(t0, ai, bi, MUL))
                step(pool.tensor_tensor(dr, ar, br, MUL))
                step(pool.tensor_tensor(dr, dr, t0, SUB))
                step(pool.tensor_tensor(t0, ai, br, MUL))
                step(pool.tensor_tensor(di, ar, bi, MUL))
                last = pool.tensor_tensor(di, di, t0, ADD)
                if n < 4:
                    step(last)
            last.then_inc(lam_done, 1)
            pool.wait_ge(c_done, 1)
            pool.wait_ge(ada_used, 12)
            pool.wait_ge(pw_done, 1)

            def c4(x_):
                return x_[:, :, :].unsqueeze(2).to_broadcast([P, PAIRS, SC + 1, GH])

            def p4(x_):
                return x_[:, :, :].rearrange("p k i -> p i k").unsqueeze(3).to_broadcast([P, PAIRS, SC + 1, GH])

            t_ = v_t[:, :, :, :]
            for dst, a_, b_ in ((v_re, c_re, nc_im), (v_im, nc_im, nc_re)):
                d_ = dst[:, :, :, :]
                pool.tensor_tensor(t_, c4(b_), p4(pw_im), MUL)
                step(pool.tensor_tensor(d_, c4(a_), p4(pw_re), MUL))
                last = pool.tensor_tensor(d_, d_, t_, ADD)
                if dst is v_re:
                    step(last)
            last.then_inc(v_done, 1)
            pool.wait_ge(v_done, 1)
            pool.memset(m_in[:, :, :], 0.0).then_inc(m_zero, 1)
            pool.tensor_copy(q_pw[:, 0, 0, :], pw_re[:, SC, :])
            step(pool.tensor_copy(q_pw[:, 1, 0, :], pw_im[:, SC, :]))
            q_t = g_tq[:, :, :]
            for src, by, dst, n in ((0, 0, 1, 1), (0, 1, 2, 2), (0, 3, 4, 4)):
                ar, ai = q_pw[:, 0, src:src + n, :], q_pw[:, 1, src:src + n, :]
                br = q_pw[:, 0, by:by + 1, :].to_broadcast([P, n, PAIRS])
                bi = q_pw[:, 1, by:by + 1, :].to_broadcast([P, n, PAIRS])
                dr, di = q_pw[:, 0, dst:dst + n, :], q_pw[:, 1, dst:dst + n, :]
                step(pool.tensor_tensor(q_t[:, 0:n, :], ai, bi, MUL))
                step(pool.tensor_tensor(dr, ar, br, MUL))
                step(pool.tensor_tensor(dr, dr, q_t[:, 0:n, :], SUB))
                step(pool.tensor_tensor(q_t[:, 0:n, :], ai, br, MUL))
                step(pool.tensor_tensor(di, ar, bi, MUL))
                step(pool.tensor_tensor(di, di, q_t[:, 0:n, :], ADD))

            pool.wait_ge(p_done, 4)
            pool.wait_ge(c_t, 1)
            xr = s_re[:, :, :].rearrange("p i (b s) -> p i b s", s=8)
            xi = s_im[:, :, :].rearrange("p i (b s) -> p i b s", s=8)

            def advance(dr, di, sr, si, cr, ci, shape):
                n = int(np.prod(shape))
                ta, tb = scan_a[:, 0:n], scan_b[:, 0:n]
                if len(shape) == 2:
                    ta, tb = (t0.rearrange("p (i b) -> p i b", i=shape[0]) for t0 in (ta, tb))
                elif len(shape) == 3:
                    ta, tb = (t0.rearrange("p (i b s) -> p i b s", i=shape[0], b=shape[1]) for t0 in (ta, tb))
                tt = pool.tensor_tensor
                tt(ta, sr, cr, MUL)
                step(tt(tb, si, ci, MUL))
                step(tt(ta, ta, tb, SUB))
                tt(dr, dr, ta, ADD)
                step(tt(tb, si, cr, MUL))
                step(tt(ta, sr, ci, MUL))
                step(tt(ta, ta, tb, ADD))
                last = tt(di, di, ta, ADD)
                if len(shape) == 3:
                    last.then_inc(scan_done, 1)
                else:
                    step(last)

            c1r = q_pw[:, 0, 0, :].unsqueeze(2).to_broadcast([P, PAIRS, 8])
            c1i = q_pw[:, 1, 0, :].unsqueeze(2).to_broadcast([P, PAIRS, 8])
            for s in range(1, 8):
                advance(xr[:, :, :, s], xi[:, :, :, s], xr[:, :, :, s - 1], xi[:, :, :, s - 1],
                        c1r, c1i, (PAIRS, 8))
            for b in range(1, 8):
                advance(xr[:, :, b, 7], xi[:, :, b, 7], xr[:, :, b - 1, 7], xi[:, :, b - 1, 7],
                        q_pw[:, 0, 7, :], q_pw[:, 1, 7, :], (PAIRS,))
            shape4 = [P, PAIRS, 7, 7]
            advance(xr[:, :, 1:8, 0:7], xi[:, :, 1:8, 0:7],
                    xr[:, :, 0:7, 7].unsqueeze(3).to_broadcast(shape4),
                    xi[:, :, 0:7, 7].unsqueeze(3).to_broadcast(shape4),
                    q_pw[:, 0, 0:7, :].rearrange("p s i -> p i s").unsqueeze(2).to_broadcast(shape4),
                    q_pw[:, 1, 0:7, :].rearrange("p s i -> p i s").unsqueeze(2).to_broadcast(shape4),
                    (PAIRS, 7, 7))

            pool.wait_ge(gates, 1)
            for hd in range(NH):
                pool.wait_ge(qn_done, hd + 1)
                pool.tensor_tensor(kd_tok[:, hd, :, :], k_tok[:, hd, :, :], bc(k_fac[:, :, hd], P), MUL)\
                    .then_inc(kd_done, 1)
                pool.tensor_tensor(qd_tok[:, hd, :, :], q_tok[:, hd, :, :], bc(gc_exp[:, :, hd], P), MUL)\
                    .then_inc(qd_done, 1)
                pool.wait_ge(kb_done, hd + 1)
                pool.tensor_tensor(rk_tok[:, hd, :, :], kb_tok[:, hd, :, :], bc(gc_exp[:, :, hd], P), MUL)\
                    .then_inc(rk_done, 1)
            for hd in range(NH):
                pool.wait_ge(dec_exp, hd + 1)
                select(dec[:, hd, :, :], [[0, TT], [1, P]], 0, -1).then_inc(dec_done, 1)
            for hd in range(NH):
                wait_drained(pool, "lt", hd)
                select(LT[:, hd, :, :], [[0, TT], [1, P]], -1, -1).then_inc(lt_done, 1)
                wait_drained(pool, "dT", hd)
                pool.wait_ge(lt_done, hd + 1)
                pool.tensor_tensor(DaT[:, hd, :, :], LT[:, hd, :, :],
                                   bd16[:, :].unsqueeze(1).to_broadcast([P, TT, P]), MUL).then_inc(dat_done, 1)
            for half in range(2):
                with pool.Fori(1, 5) as i:
                    for s in range(2):
                        pool.wait_ge(ada_used, 45 + 8 * half + s + 2 * i)
                        pool.wait_ge(block_done, B_FF0)
                        src = ada_w[1].rearrange("(p t) n -> p (t n)", t=8)[
                            :, bass.ds(i * (2 * 6 * D) + (s - 2) * 6 * D + half * 3 * D, 3 * D)]
                        pool.dma_start(ada1_in[s][:, :], src).then_inc(ada1_ld[s], 16)


_INS = ["x", "c", "ada_w", "ada_b", "norm_mix_w", "norm_ffn_w", "ffn_w_in", "ffn_w_out", "hy_w_in",
        "hy_conv_w", "hy_a_log", "hy_dt_bias", "hy_head_norm_w", "s5_lam_re", "s5_lam_im",
        "s5_log_dt", "s5_b_re", "s5_b_im", "s5_c_re", "s5_c_im", "s5_d", "s5_glu_w", "s5_glu_b",
        "hy_w_out", "sb_w_in", "sb_w_out", "final_norm_w"]


def kernel(**inputs):
    import concourse.bacc as bacc
    from concourse.bass_utils import run_bass_kernel_spmd

    nc = bacc.Bacc("TRN2", target_bir_lowering=False, num_devices=1)
    arrays, args = {}, []
    for name in _INS:
        v = np.ascontiguousarray(inputs[name])
        arrays[f"in_{name}_dram"] = v
        args.append(nc.dram_tensor(f"in_{name}_dram", v.shape, mybir.dt.from_np(v.dtype),
                                   kind="ExternalInput").ap())
    args.append(nc.dram_tensor("out_0_dram", (1, T, D), F32, kind="ExternalOutput").ap())
    trunk(nc, *args)
    r = run_bass_kernel_spmd(nc, [arrays], core_ids=[0])
    return r.results[0]["out_0_dram"]
```
